# Optimizing a Trainium2 kernel written in Bass

```python
import math
import jax
import jax.numpy as jnp
from jax import lax
import numpy as np

D_MODEL = 1024
BATCH = 1
SEQ = 1024
DEPTH = 2

GRID_W = 64
CTX_LEN = 256
NORM_EPS = 1e-6

S5_GROUP = 16
S5_GROUPS = 32
S5_WIDTH = S5_GROUP * S5_GROUPS
S5_STATE = 64
S5_DT_MIN = 1e-3
S5_DT_MAX = 1e-1
S5_LAMBDA_RE_MAX = -1e-4
NA_HEADS = 8
NA_HEAD_DIM = 64
NA_WIDTH = NA_HEADS * NA_HEAD_DIM
NA_KH_MAX = 8
NA_KW = 16
IN_WIDTH = S5_WIDTH + 3 * NA_WIDTH
MIX_WIDTH = S5_WIDTH + NA_WIDTH
FOURIER_GROUPS = 4
N_EXPERTS = 64
N_EXPERT_GROUPS = 8
TOPK_GROUPS = 4
TOP_K = 8
EXPERT_FF = 256
SHARED_FF = 256
ROUTED_SCALE = 2.5
EXPERT_BLOCK = 128

kernel_name = 'hybrid_s5_natten_fnet_moe_dit'

def rms_norm(x):
    xf = x.astype(jnp.float32)
    return (xf * lax.rsqrt(jnp.mean(xf * xf, axis=-1, keepdims=True) + NORM_EPS)).astype(x.dtype)

def modulate(h, shift, scale):
    return rms_norm(h) * (1 + scale) + shift

def adaln(cond, w, b):
    return jnp.split(jax.nn.silu(cond) @ w + b, 6, axis=-1)

def _linear_recurrence(left, right):
    a_l, b_l = left
    a_r, b_r = right
    return a_l * a_r, a_r * b_l + b_r

def s5_discretize(lam_re, lam_im, log_dt, b_re, b_im):
    f32 = jnp.float32
    lam = lax.complex(jnp.minimum(lam_re.astype(f32), S5_LAMBDA_RE_MAX), lam_im.astype(f32))
    dt = jnp.exp(log_dt.astype(f32))[:, None]
    lam_bar = jnp.exp(lam * dt)
    b_bar = ((lam_bar - 1.0) / lam)[..., None] * lax.complex(b_re.astype(f32), b_im.astype(f32))
    return lam_bar, b_bar

def s5_scan(u, lam_bar, b_bar, init, reverse):
    bu = jnp.einsum('btgc,gpc->btgp', u.astype(jnp.complex64), b_bar)
    entry = -1 if reverse else 0
    bu = bu.at[:, entry].add(lam_bar * init)
    a = jnp.broadcast_to(lam_bar, bu.shape)
    _, states = lax.associative_scan(_linear_recurrence, (a, bu), reverse=reverse, axis=1)
    return states

def s5_readout(st_f, st_b, c_f, c_b, d, u, w_glu, b_glu, out_dtype):
    y = (jnp.real(jnp.einsum('btgp,gcp->btgc', st_f, c_f))
         + jnp.real(jnp.einsum('btgp,gcp->btgc', st_b, c_b)) + d * u)
    g = jax.nn.gelu(y.reshape(u.shape[0], u.shape[1], S5_WIDTH).astype(out_dtype))
    return g * jax.nn.sigmoid(g @ w_glu + b_glu)

def neighbourhood_attention(q, k, v, k_ctx, v_ctx, rpb, rows):
    bsz = q.shape[0]
    kh = min(NA_KH_MAX, rows)
    n_local = kh * NA_KW
    scale = NA_HEAD_DIM ** -0.5
    q_col = np.arange(GRID_W)
    col_start = np.clip(q_col - NA_KW // 2, 0, GRID_W - NA_KW)
    key_cols = col_start[:, None] + np.arange(NA_KW)
    rpb_col = rpb[:, :, key_cols - q_col[:, None] + NA_KW - 1]

    def one_row(r):
        r0 = jnp.clip(r - kh // 2, 0, rows - kh)
        key_rows = r0 + jnp.arange(kh)
        idx = (key_rows[None, :, None] * GRID_W + key_cols[:, None, :]).reshape(GRID_W, n_local)
        q_r = lax.dynamic_slice_in_dim(q, r * GRID_W, GRID_W, axis=1)
        k_r = k[:, idx]
        v_r = v[:, idx]
        bias = rpb_col[:, key_rows - r + NA_KH_MAX - 1]
        bias = jnp.transpose(bias, (0, 2, 1, 3)).reshape(NA_HEADS, GRID_W, n_local)
        s_loc = jnp.einsum('bqhd,bqkhd->bhqk', q_r, k_r).astype(jnp.float32) * scale + bias
        s_ctx = jnp.einsum('bqhd,bkhd->bhqk', q_r, k_ctx).astype(jnp.float32) * scale
        p = jax.nn.softmax(jnp.concatenate([s_loc, s_ctx], axis=-1), axis=-1).astype(v.dtype)
        o = jnp.einsum('bhqk,bqkhd->bqhd', p[..., :n_local], v_r)
        return o + jnp.einsum('bhqk,bkhd->bqhd', p[..., n_local:], v_ctx)

    out = lax.map(one_row, jnp.arange(rows))
    return jnp.moveaxis(out, 0, 1).reshape(bsz, rows * GRID_W, NA_WIDTH)

def context_attention(q, k, v):
    s = jnp.einsum('bqhd,bkhd->bhqk', q, k).astype(jnp.float32) * NA_HEAD_DIM ** -0.5
    p = jax.nn.softmax(s, axis=-1).astype(v.dtype)
    o = jnp.einsum('bhqk,bkhd->bqhd', p, v)
    return o.reshape(q.shape[0], q.shape[1], NA_WIDTH)

def even_mixer(a_c, a_l, rows, w_in, lam_re, lam_im, log_dt, b_re, b_im, c_re, c_im, s5_d,
               w_glu, b_glu, q_gain, k_gain, rpb, w_out, need_ctx):
    def project(a):
        bsz, t = a.shape[:2]
        z = a @ w_in
        u = z[..., :S5_WIDTH].astype(jnp.float32).reshape(bsz, t, S5_GROUPS, S5_GROUP)
        qkv = z[..., S5_WIDTH:].reshape(bsz, t, 3, NA_HEADS, NA_HEAD_DIM)
        return u, qkv[:, :, 0], rms_norm(qkv[:, :, 1]) * k_gain, qkv[:, :, 2]

    u_c, qr_c, k_c, v_c = project(a_c)
    u_l, qr_l, k_l, v_l = project(a_l)

    f32 = jnp.float32
    lam_f, bb_f = s5_discretize(lam_re[0], lam_im[0], log_dt[0], b_re[0], b_im[0])
    lam_b, bb_b = s5_discretize(lam_re[1], lam_im[1], log_dt[1], b_re[1], b_im[1])
    cc_f = lax.complex(c_re[0].astype(f32), c_im[0].astype(f32))
    cc_b = lax.complex(c_re[1].astype(f32), c_im[1].astype(f32))
    d32 = s5_d.astype(f32)
    zero = jnp.zeros((u_c.shape[0], S5_GROUPS, S5_STATE), jnp.complex64)
    st_cf = s5_scan(u_c, lam_f, bb_f, zero, False)
    st_cb = s5_scan(u_c, lam_b, bb_b, zero, True)
    st_lf = s5_scan(u_l, lam_f, bb_f, st_cf[:, -1], False)
    st_lb = s5_scan(u_l, lam_b, bb_b, st_cb[:, 0], True)
    s5_l = s5_readout(st_lf, st_lb, cc_f, cc_b, d32, u_l, w_glu, b_glu, a_l.dtype)
    na_l = neighbourhood_attention(rms_norm(qr_l) * q_gain, k_l, v_l, k_c, v_c, rpb, rows)
    y_l = jnp.concatenate([s5_l, na_l], axis=-1) @ w_out
    if not need_ctx:
        return None, y_l
    s5_c = s5_readout(st_cf, st_cb, cc_f, cc_b, d32, u_c, w_glu, b_glu, a_c.dtype)
    na_c = context_attention(rms_norm(qr_c) * q_gain, k_c, v_c)
    y_c = jnp.concatenate([s5_c, na_c], axis=-1) @ w_out
    return y_c, y_l

def fourier_mixer(a, w, b):
    bsz, t, d = a.shape
    hg = a.astype(jnp.float32).reshape(bsz, t, FOURIER_GROUPS, d // FOURIER_GROUPS)
    f = jnp.real(jnp.fft.fft2(hg, axes=(1, 3), norm='ortho'))
    return f.reshape(bsz, t, d).astype(a.dtype) @ w + b

def routed_experts(h, e_idx, e_w, w_gate, w_up, w_down):
    n, d = h.shape
    n_exp = w_gate.shape[0]
    nk = n * TOP_K
    flat_e = e_idx.reshape(-1)
    flat_tok = jnp.repeat(jnp.arange(n, dtype=jnp.int32), TOP_K)
    flat_w = e_w.reshape(-1)
    order = jnp.argsort(flat_e)
    se, st, sw = flat_e[order], flat_tok[order], flat_w[order]
    counts = jnp.bincount(flat_e, length=n_exp)
    padded = (counts + EXPERT_BLOCK - 1) // EXPERT_BLOCK * EXPERT_BLOCK
    pad_end = jnp.cumsum(padded)
    pad_start = pad_end - padded
    start = jnp.cumsum(counts) - counts
    dest = pad_start[se] + (jnp.arange(nk) - start[se])
    n_blocks = (nk + n_exp * (EXPERT_BLOCK - 1) + EXPERT_BLOCK - 1) // EXPERT_BLOCK
    cap = n_blocks * EXPERT_BLOCK
    buf_tok = jnp.full((cap,), n, jnp.int32).at[dest].set(st)
    buf_w = jnp.zeros((cap,), h.dtype).at[dest].set(sw)
    blk_e = jnp.minimum(jnp.searchsorted(pad_end, jnp.arange(n_blocks) * EXPERT_BLOCK, side='right'),
                        n_exp - 1)
    h_pad = jnp.concatenate([h, jnp.zeros((1, d), h.dtype)], axis=0)

    def one_block(args):
        tok, wgt, e = args
        xb = h_pad[tok]
        hid = jax.nn.silu(xb @ w_gate[e]) * (xb @ w_up[e])
        return (hid @ w_down[e]) * wgt[:, None]

    y = lax.map(one_block, (buf_tok.reshape(n_blocks, EXPERT_BLOCK),
                            buf_w.reshape(n_blocks, EXPERT_BLOCK), blk_e))
    out = jnp.zeros((n + 1, d), h.dtype).at[buf_tok].add(y.reshape(cap, d))
    return out[:n]

def moe_ffn(h, w_router, router_bias, w_eg, w_eu, w_ed, w_sg, w_su, w_sd):
    n = h.shape[0]
    scores = jax.nn.sigmoid((h @ w_router).astype(jnp.float32))
    sel = scores + router_bias.astype(jnp.float32)
    grp = sel.reshape(n, N_EXPERT_GROUPS, N_EXPERTS // N_EXPERT_GROUPS)
    grp_score = jnp.sum(lax.top_k(grp, 2)[0], axis=-1)
    _, top_grp = lax.top_k(grp_score, TOPK_GROUPS)
    grp_keep = jnp.any(top_grp[:, :, None] == jnp.arange(N_EXPERT_GROUPS), axis=1)
    keep = jnp.repeat(grp_keep, N_EXPERTS // N_EXPERT_GROUPS, axis=1)
    _, idx = lax.top_k(jnp.where(keep, sel, -jnp.inf), TOP_K)
    gate = jnp.take_along_axis(scores, idx, axis=1)
    gate = ROUTED_SCALE * gate / jnp.sum(gate, axis=-1, keepdims=True)
    routed = routed_experts(h, idx, gate.astype(h.dtype), w_eg, w_eu, w_ed)
    shared = (jax.nn.silu(h @ w_sg) * (h @ w_su)) @ w_sd
    return routed + shared

def setup_inputs(seed: int = 0) -> dict:
    key = jax.random.key(seed)
    keys = iter(jax.random.split(key, 40))
    f32 = jnp.float32
    d = D_MODEL
    n_even = (DEPTH + 1) // 2
    n_odd = DEPTH // 2

    def nrm(shape, scale):
        return jax.random.normal(next(keys), shape, f32) * scale

    s5_shape = (n_even, 2, S5_GROUPS, S5_STATE)
    c_scale = S5_STATE ** -0.25
    return {
        'x': nrm((BATCH, SEQ, d), 1.0),
        'c': nrm((BATCH, d), 1.0),
        'ctx': nrm((BATCH, CTX_LEN, d), 1.0),
        'c_ctx': nrm((d,), 1.0),
        'w_ada': nrm((DEPTH, d, 6 * d), 0.5 * d ** -0.5),
        'b_ada': nrm((DEPTH, 6 * d), 0.02),
        'w_in': nrm((n_even, d, IN_WIDTH), d ** -0.5),
        's5_lam_re': -0.5 + nrm(s5_shape, 0.01),
        's5_lam_im': jnp.pi * jnp.arange(S5_STATE, dtype=f32) + nrm(s5_shape, 0.01),
        's5_log_dt': jax.random.uniform(next(keys), (n_even, 2, S5_GROUPS), f32,
                                        math.log(S5_DT_MIN), math.log(S5_DT_MAX)),
        's5_b_re': nrm((n_even, 2, S5_GROUPS, S5_STATE, S5_GROUP), (2 * S5_GROUP) ** -0.5),
        's5_b_im': nrm((n_even, 2, S5_GROUPS, S5_STATE, S5_GROUP), (2 * S5_GROUP) ** -0.5),
        's5_c_re': nrm((n_even, 2, S5_GROUPS, S5_GROUP, S5_STATE), c_scale),
        's5_c_im': nrm((n_even, 2, S5_GROUPS, S5_GROUP, S5_STATE), c_scale),
        's5_d': nrm((n_even, S5_GROUPS, S5_GROUP), 1.0),
        's5_w_glu': nrm((n_even, S5_WIDTH, S5_WIDTH), S5_WIDTH ** -0.5),
        's5_b_glu': nrm((n_even, S5_WIDTH), 0.01),
        'na_q_gain': 1.0 + nrm((n_even, NA_HEAD_DIM), 0.01),
        'na_k_gain': 1.0 + nrm((n_even, NA_HEAD_DIM), 0.01),
        'na_rpb': nrm((n_even, NA_HEADS, 2 * NA_KH_MAX - 1, 2 * NA_KW - 1), 0.1),
        'w_mix_out': nrm((n_even, MIX_WIDTH, d), MIX_WIDTH ** -0.5),
        'w_fourier_out': nrm((n_odd, d, d), d ** -0.5),
        'b_fourier_out': nrm((n_odd, d), 0.01),
        'w_router': nrm((DEPTH, d, N_EXPERTS), d ** -0.5),
        'router_bias': nrm((DEPTH, N_EXPERTS), 0.01),
        'w_exp_gate': nrm((DEPTH, N_EXPERTS, d, EXPERT_FF), d ** -0.5),
        'w_exp_up': nrm((DEPTH, N_EXPERTS, d, EXPERT_FF), d ** -0.5),
        'w_exp_down': nrm((DEPTH, N_EXPERTS, EXPERT_FF, d), EXPERT_FF ** -0.5),
        'w_sh_gate': nrm((DEPTH, d, SHARED_FF), d ** -0.5),
        'w_sh_up': nrm((DEPTH, d, SHARED_FF), d ** -0.5),
        'w_sh_down': nrm((DEPTH, SHARED_FF, d), SHARED_FF ** -0.5),
    }

def reference(x, c, ctx, c_ctx, w_ada, b_ada, w_in, s5_lam_re, s5_lam_im, s5_log_dt,
              s5_b_re, s5_b_im, s5_c_re, s5_c_im, s5_d, s5_w_glu, s5_b_glu, na_q_gain,
              na_k_gain, na_rpb, w_mix_out, w_fourier_out, b_fourier_out, w_router,
              router_bias, w_exp_gate, w_exp_up, w_exp_down, w_sh_gate, w_sh_up, w_sh_down):
    d = x.shape[-1]
    rows = x.shape[1] // GRID_W
    h_l, h_c = x, ctx
    for i in range(DEPTH):
        need_ctx = any(j % 2 == 0 for j in range(i + 1, DEPTH))
        ml = [m[:, None, :] for m in adaln(c, w_ada[i], b_ada[i])]
        a_l = modulate(h_l, ml[0], ml[1])
        if i % 2 == 0 or need_ctx:
            mc = adaln(c_ctx, w_ada[i], b_ada[i])
        if i % 2 == 0:
            e = i // 2
            y_c, y_l = even_mixer(modulate(h_c, mc[0], mc[1]), a_l, rows, w_in[e],
                                  s5_lam_re[e], s5_lam_im[e], s5_log_dt[e], s5_b_re[e],
                                  s5_b_im[e], s5_c_re[e], s5_c_im[e], s5_d[e], s5_w_glu[e],
                                  s5_b_glu[e], na_q_gain[e], na_k_gain[e], na_rpb[e],
                                  w_mix_out[e], need_ctx)
        else:
            o = i // 2
            y_l = fourier_mixer(a_l, w_fourier_out[o], b_fourier_out[o])
            y_c = (fourier_mixer(modulate(h_c, mc[0], mc[1]), w_fourier_out[o], b_fourier_out[o])
                   if need_ctx else None)
        h_l = h_l + ml[2] * y_l
        f_l = modulate(h_l, ml[3], ml[4]).reshape(-1, d)
        moe_w = (w_router[i], router_bias[i], w_exp_gate[i], w_exp_up[i], w_exp_down[i],
                 w_sh_gate[i], w_sh_up[i], w_sh_down[i])
        if need_ctx:
            h_c = h_c + mc[2] * y_c
            f_c = modulate(h_c, mc[3], mc[4]).reshape(-1, d)
            n_c = f_c.shape[0]
            ffn = moe_ffn(jnp.concatenate([f_c, f_l], axis=0), *moe_w)
            h_c = h_c + mc[5] * ffn[:n_c].reshape(h_c.shape)
            h_l = h_l + ml[5] * ffn[n_c:].reshape(h_l.shape)
        else:
            h_l = h_l + ml[5] * moe_ffn(f_l, *moe_w).reshape(h_l.shape)
    return h_l


_drawn_inputs = setup_inputs


def setup_inputs(seed=0):
    import zlib

    import numpy as np

    out = dict(_drawn_inputs(seed))
    spreads = {}
    factors = {'s5_lam_re': 8.0,
     's5_b_glu': 8.0,
     'na_q_gain': 8.0,
     'na_k_gain': 8.0,
     'na_rpb': 5.266,
     'b_fourier_out': 4.606}
    for name, (base, spread) in spreads.items():
        noise = np.random.default_rng([zlib.crc32(name.encode()), seed]).standard_normal(out[name].shape)
        drawn = base * np.exp(spread * noise) if base else spread * noise
        out[name] = jnp.asarray(drawn.astype(out[name].dtype))
    for name, factor in factors.items():
        out[name] = (out[name] * factor).astype(out[name].dtype)
    return out
```

```python
import math
from contextlib import ExitStack

import concourse.bass as bass
from concourse import mybir

F32 = mybir.dt.float32
I32 = mybir.dt.int32
U32 = mybir.dt.uint32
ALU = mybir.AluOpType
ACT = mybir.ActivationFunctionType
AX = mybir.AxisListType

P = 128
D = 1024
KD = D // P
SEQ = 1024
CTX = 256
TOK = CTX + SEQ
TT = SEQ // P
CT = CTX // P
EPS = 1e-6
GRID_W = 64
ROWS = SEQ // GRID_W
NCH = 512
ADA = 6 * D
G5, C5, S5 = 32, 16, 64
W5 = G5 * C5
LCH = 8
NCK = TOK // LCH
NCC = CTX // LCH
NCL = SEQ // LCH
HEADS, HD = 8, 64
HP = HEADS // 2
KH, KW = 8, 16
RPB_R, RPB_C = 2 * KH - 1, 2 * KW - 1
NE, NG, EG = 64, 8, 8
TOPG, TOPK = 4, 8
FF = 256
NEG = -1e30


class Phase:

    def __init__(self, nc, name):
        self.nc, self.name, self.stack, self.sems = nc, name, ExitStack(), []

    def __enter__(self):
        self.stack.__enter__()
        return self

    def __exit__(self, *a):
        self.stack.__exit__(*a)
        if self.sems:
            self.nc.clear_and_free_semaphores(self.sems)
            self.nc.all_engine_barrier()

    def sb(self, name, shape, dt=F32):
        return self.stack.enter_context(self.nc.sbuf_tensor(f"{self.name}_{name}", shape, dt))

    def ps(self, name, shape, dt=F32):
        return self.stack.enter_context(self.nc.psum_tensor(f"{self.name}_{name}", shape, dt))

    def sem(self, name):
        self.sems.append(self.nc.alloc_semaphore(name=f"{self.name}_{name}"))
        return self.sems[-1]

    def block(self):
        return self.stack.enter_context(self.nc.Block())


class Chain:

    def __init__(self, eng, sem):
        self.eng, self.sem, self.n = eng, sem, 0

    def __call__(self, ins):
        self.n += 1
        ins.then_inc(self.sem, 1)
        self.eng.wait_ge(self.sem, self.n)


def make_identity(nc, ident):
    with Phase(nc, "ident") as ph:
        zero = ph.sem("zero")
        done = ph.sem("done")
        block = ph.block()

        @block.gpsimd
        def _(pool):
            pool.memset(ident[:, :], 0.0).then_inc(zero, 1)
            pool.wait_ge(zero, 1)
            pool.affine_select(out=ident[:, :], in_=ident[:, :], compare_op=ALU.not_equal, fill=1.0,
                               base=0, pattern=[[-1, P]], channel_multiplier=1).then_inc(done, 1)
            pool.wait_ge(done, 1)


def conditioning(nc, tag, c_col, w, b, mod, ctx_col=None, mod_ctx=None):
    NB = ADA // NCH
    with Phase(nc, tag) as ph:
        col = ph.sb("col", [P, 2, KD])
        act = ph.sb("act", [P, 2, KD])
        ones = ph.sb("ones", [P, P])
        rep = ph.sb("rep", [P, 2, KD, P])
        wbuf = ph.sb("w", [P, 2, KD, NCH])
        pmod = [ph.ps(f"pmod{i}", [P, NCH]) for i in range(2)]
        pctx = [ph.ps(f"pctx{i}", [P, NCH]) for i in range(2)]
        col_in, bias_in = ph.sem("col_in"), ph.sem("bias_in")
        w_in = [ph.sem(f"w_in{i}") for i in range(2)]
        silu_done, ones_done, rep_done = ph.sem("silu_done"), ph.sem("ones_done"), ph.sem("rep_done")
        mod_mm, mod_out = ph.sem("mod_mm"), ph.sem("mod_out")
        ctx_mm, ctx_out = ph.sem("ctx_mm"), ph.sem("ctx_out")
        scaled = ph.sem("scaled")
        both = ctx_col is not None
        w_v = w.rearrange("(p k) n -> p k n", k=KD)
        SPLIT = 2 if both else 0
        block = ph.block()

        @block.sync
        def _(sp):
            sp.dma_start(col[:, 0, :], c_col).then_inc(col_in, 16)
            if both:
                sp.dma_start(col[:, 1, :], ctx_col).then_inc(col_in, 16)
            for u in range(2):
                sp.dma_start(wbuf[:, u, :, :], w_v[:, :, u * NCH:(u + 1) * NCH]).then_inc(w_in[u], 16)
            sp.dma_start(mod[:, :], b[None, :].to_broadcast([P, ADA])).then_inc(bias_in, 16)
            if both:
                sp.dma_start(mod_ctx[:, :], b[None, 0:2 * D].to_broadcast([P, 2 * D])).then_inc(bias_in, 16)
            with sp.Fori(1, NB // 2) as i:
                for u in range(2):
                    sp.wait_ge(mod_mm, i * 2 + (u - 1))
                    sp.dma_start(wbuf[:, u, :, :], w_v[:, :, bass.ds(i * (2 * NCH) + u * NCH, NCH)]).then_inc(w_in[u], 16)

        @block.scalar
        def _(act_e):
            act_e.wait_ge(col_in, 32 if both else 16)
            n = 2 if both else 1
            act_e.activation(act[:, 0:n, :], col[:, 0:n, :], ACT.Silu).then_inc(silu_done, 1)

        @block.tensor
        def _(pe):
            pe.wait_ge(rep_done, 2 * KD if both else KD)

            def step(i, with_ctx):
                for u in range(2):
                    pe.wait_ge(w_in[u], i * 16 + 16)
                    if with_ctx:
                        pe.wait_ge(mod_out, i * 2 + u - 1) if not isinstance(i, int) or i * 2 + u - 1 > 0 else None
                        pe.wait_ge(ctx_out, i * 2 + u - 1) if not isinstance(i, int) or i * 2 + u - 1 > 0 else None
                        for k in range(KD):
                            mm = pe.matmul(pctx[u][:, :], rep[:, 1, k, :], wbuf[:, u, k, :], start=k == 0, stop=k == KD - 1)
                        mm.then_inc(ctx_mm, 1)
                    elif not isinstance(i, int) or i > 0:
                        pe.wait_ge(mod_out, i * 2 + (u - 1))
                    for k in range(KD):
                        mm = pe.matmul(pmod[u][:, :], rep[:, 0, k, :], wbuf[:, u, k, :], start=k == 0, stop=k == KD - 1)
                    mm.then_inc(mod_mm, 1)

            step(0, both)
            if both:
                step(1, True)
            with pe.Fori(SPLIT if both else 1, NB // 2) as i:
                step(i, False)

        @block.vector
        def _(dve):
            dve.memset(ones[:, :], 1.0).then_inc(ones_done, 1)
            dve.wait_ge(ones_done, 1)
            dve.wait_ge(silu_done, 1)
            for s in range(2 if both else 1):
                for k in range(KD):
                    dve.tensor_scalar(rep[:, s, k, :], ones[:, :], act[:, s, k:k + 1], None, ALU.mult).then_inc(rep_done, 1)
            dve.wait_ge(bias_in, 32 if both else 16)

            def step(i, with_ctx):
                for u in range(2):
                    if with_ctx:
                        dve.wait_ge(ctx_mm, i * 2 + u + 1)
                        m = mod_ctx[:, (2 * i + u) * NCH:(2 * i + u + 1) * NCH]
                        dve.tensor_tensor(m, pctx[u][:, :], m, ALU.add).then_inc(ctx_out, 1)
                    dve.wait_ge(mod_mm, i * 2 + u + 1)
                    m = mod[:, bass.ds(i * (2 * NCH) + u * NCH, NCH)]
                    dve.tensor_tensor(m, pmod[u][:, :], m, ALU.add).then_inc(mod_out, 1)

            for i in range(SPLIT):
                step(i, True)
            with dve.Fori(SPLIT, NB // 2) as i:
                step(i, False)
            dve.wait_ge(mod_out, NB)
            for s in (1, 4):
                m = mod[:, s * D:(s + 1) * D]
                dve.tensor_scalar(m, m, 1.0, None, ALU.add).then_inc(scaled, 1)
            if both:
                dve.wait_ge(ctx_out, 2 * SPLIT)
                dve.tensor_scalar(mod_ctx[:, D:2 * D], mod_ctx[:, D:2 * D], 1.0, None, ALU.add).then_inc(scaled, 1)
            dve.wait_ge(scaled, 3 if both else 2)


def norm_modulate_transpose(nc, tag, ident, tiles, aT, permuted, store=None, keep_rows=None):
    n = len(tiles)
    with Phase(nc, tag) as ph:
        from_dram = [t[2] for t in tiles]
        nload = sum(from_dram)
        xin = ph.sb("xin", [P, max(nload, 1), D]) if nload else None
        junk = ph.sb("junk", [P, 2, D])
        ss = ph.sb("ss", [P, n])
        var = ph.sb("var", [P, n])
        std = ph.sb("std", [P, n])
        rstd = ph.sb("rstd", [P, n])
        a = ph.sb("a", [P, 3, D])
        pT = [ph.ps(f"pT{i}", [P, KD, P]) for i in range(3)]
        x_in = [ph.sem(f"x_in{i}") for i in range(max(nload, 1))]
        sq_done, var_done, std_done, rstd_done = (ph.sem(s) for s in ("sq_done", "var_done", "std_done", "rstd_done"))
        scale_done, a_done, tr_done, copied = (ph.sem(s) for s in ("scale_done", "a_done", "tr_done", "copied"))
        stored = [ph.sem(f"stored{i}") for i in range(3)]
        src = []
        m = 0
        for t in tiles:
            if t[2]:
                src.append((xin[:, m, :], m))
                m += 1
            else:
                src.append((t[0], None))
        block = ph.block()

        @block.sync
        def _(sp):
            for i, t in enumerate(tiles):
                if t[2]:
                    sp.dma_start(src[i][0], t[0]).then_inc(x_in[src[i][1]], 16)
            if store is not None:
                for i in range(n):
                    sp.wait_ge(a_done, i + 1)
                    sp.dma_start(store[i], a[:, i % 3, :]).then_inc(stored[i % 3], 16)
                for j in range(min(3, n)):
                    sp.wait_ge(stored[j], 16 * len(range(j, n, 3)))

        @block.scalar
        def _(act):
            for i in range(n):
                if src[i][1] is not None:
                    act.wait_ge(x_in[src[i][1]], 16)
                if i >= 2:
                    act.wait_ge(sq_done, i - 1)
                act.activation(junk[:, i % 2, :], src[i][0], ACT.Square, accum_out=ss[:, i:i + 1]).then_inc(sq_done, 1)
            act.wait_ge(var_done, 1)
            act.activation(std[:, :], var[:, :], ACT.Sqrt).then_inc(std_done, 1)
            for i in range(n):
                act.wait_ge(tr_done, i + 1)
                act.activation(aT[:, :, i * P:(i + 1) * P], pT[i % 3][:, :, :], ACT.Copy).then_inc(copied, 1)
            act.wait_ge(copied, n)

        @block.vector
        def _(dve):
            dve.wait_ge(sq_done, n)
            dve.tensor_scalar(var[:, :], ss[:, :], 1.0 / D, EPS, ALU.mult, ALU.add).then_inc(var_done, 1)
            dve.wait_ge(std_done, 1)
            dve.reciprocal(rstd[:, :], std[:, :]).then_inc(rstd_done, 1)
            dve.wait_ge(rstd_done, 1)
            for i in range(n):
                if i >= 3:
                    dve.wait_ge(tr_done, i - 2)
                    if store is not None:
                        dve.wait_ge(stored[i % 3], 16 * (i // 3))
                shift, scale1 = tiles[i][1]
                av = a[:, i % 3, :]
                if permuted:
                    av = av.rearrange("q (k p) -> q p k", k=KD)
                    sv = src[i][0].rearrange("q (p k) -> q p k", k=KD)
                    hv, cv = shift.rearrange("q (p k) -> q p k", k=KD), scale1.rearrange("q (p k) -> q p k", k=KD)
                else:
                    sv, hv, cv = src[i][0], shift, scale1
                dve.scalar_tensor_tensor(av, sv, rstd[:, i:i + 1], cv, ALU.mult, ALU.mult).then_inc(scale_done, 1)
                dve.wait_ge(scale_done, i + 1)
                dve.tensor_tensor(av, av, hv, ALU.add).then_inc(a_done, 1)

        @block.tensor
        def _(pe):
            for i in range(n):
                pe.wait_ge(a_done, i + 1)
                if i >= 3:
                    pe.wait_ge(copied, i - 2)
                for k in range(KD):
                    tr = pe.transpose(pT[i % 3][:, k, :], a[:, i % 3, k * P:(k + 1) * P], ident[:, :])
                tr.then_inc(tr_done, 1)


def project(nc, ident, aT, w_in, q_gain, k_gain, u_dram, qT, kT, v_even, v_odd, v_ctx):
    TG = [(0, NCH), (NCH, NCH), (2 * NCH, TOK - 2 * NCH)]
    NU = (W5 // P) * len(TG)
    w_v = w_in.rearrange("(p k) n -> p k n", k=KD)
    jobs = [(1, t) for t in range(CT, CT + TT)] + [(2, t) for t in range(CT + TT)] + [(3, t) for t in range(CT + TT)]
    NQK = TT + TT + CT
    last_of = {0: NU, 1: NU + TT, 2: NU + NQK, 3: NU + NQK + TT + CT}
    with Phase(nc, "proj") as ph:
        w = ph.sb("w", [P, 2, KD, NCH])
        uT = ph.sb("uT", [P, 2, LCH, NCK])
        sq = ph.sb("sq", [P, 2, NCH])
        ss = ph.sb("ss", [P, 2, HEADS])
        var = ph.sb("var", [P, 2, HEADS])
        std = ph.sb("std", [P, 2, HEADS])
        rstd = ph.sb("rstd", [P, 2, HEADS])
        qn = ph.sb("qn", [P, 2, NCH])
        gain = ph.sb("gain", [P, 2, HD])
        pz = [ph.ps(f"pz{i}", [P, NCH]) for i in range(4)]
        pt = [ph.ps(f"pt{i}", [P, HP, P]) for i in range(2)]
        w_got = [ph.sem(f"w_got{g}") for g in range(4)]
        gain_got, gain_scaled = ph.sem("gain_got"), ph.sem("gain_scaled")
        mm_done, z_used = ph.sem("mm_done"), ph.sem("z_used")
        u_out = [ph.sem(f"u_out{i}") for i in range(2)]
        sq_done, dve_step, std_done, n_done = ph.sem("sq_done"), ph.sem("dve_step"), ph.sem("std_done"), ph.sem("n_done")
        t_done, t_copied = ph.sem("t_done"), ph.sem("t_copied")
        v_done = ph.sem("v_done")
        odd_lo, odd_hi = ph.sem("odd_lo"), ph.sem("odd_hi")
        block = ph.block()

        @block.sync
        def _(sp):
            for g in range(4):
                if g >= 2:
                    sp.wait_ge(mm_done, last_of[g - 2])
                sp.dma_start(w[:, g % 2, :, :], w_v[:, :, g * NCH:(g + 1) * NCH]).then_inc(w_got[g], 16)
                if g == 0:
                    sp.dma_start(gain[:, 0, :], q_gain[None, :].to_broadcast([P, HD])).then_inc(gain_got, 16)
                    sp.dma_start(gain[:, 1, :], k_gain[None, :].to_broadcast([P, HD])).then_inc(gain_got, 16)
                if g == 1:
                    for c in range(W5 // P):
                        sp.wait_ge(z_used, (c + 1) * len(TG))
                        sp.dma_start(u_dram[c * P:(c + 1) * P, :], uT[:, c % 2, :, :]).then_inc(u_out[c % 2], 16)
            sp.wait_ge(v_done, CT + TT)
            sp.dma_start(v_odd[0:64, :, :], v_even[64:128, 0:TT - 1, :]).then_inc(odd_lo, 16)
            sp.dma_start(v_odd[64:128, :, :], v_even[0:64, 1:TT, :]).then_inc(odd_hi, 16)
            sp.wait_ge(odd_lo, 16)
            sp.wait_ge(odd_hi, 16)
            for j in range(2):
                sp.wait_ge(u_out[j], 16 * (W5 // P // 2))

        @block.tensor
        def _(pe):
            n = 0
            pe.wait_ge(w_got[0], 16)
            for c in range(W5 // P):
                for t0, tn in TG:
                    if n >= 4:
                        pe.wait_ge(z_used, n - 3)
                    for k in range(KD):
                        mm = pe.matmul(pz[n % 4][:, 0:tn], w[:, 0, k, c * P:(c + 1) * P], aT[:, k, t0:t0 + tn],
                                       start=k == 0, stop=k == KD - 1)
                    mm.then_inc(mm_done, 1)
                    n += 1

            def turn(j):
                pe.wait_ge(n_done, j + 1)
                if j >= 2:
                    pe.wait_ge(t_copied, j - 1)
                for h in range(HP):
                    tr = pe.transpose(pt[j % 2][:, h, :], qn[:, j % 2, h * P:(h + 1) * P], ident[:, :])
                tr.then_inc(t_done, 1)

            for j, (g, t) in enumerate(jobs):
                pe.wait_ge(w_got[g], 16)
                pe.wait_ge(z_used, n - 3)
                for k in range(KD):
                    mm = pe.matmul(pz[n % 4][:, :], aT[:, k, t * P:(t + 1) * P], w[:, g % 2, k, :],
                                   start=k == 0, stop=k == KD - 1)
                mm.then_inc(mm_done, 1)
                n += 1
                if 2 <= j < NQK + 2:
                    turn(j - 2)

        @block.scalar
        def _(act):
            for j, (g, t) in enumerate(jobs):
                n = NU + j
                if g < 3:
                    act.wait_ge(mm_done, n + 1)
                    if j >= 2:
                        act.wait_ge(dve_step, 5 * (j - 2) + 1)
                    act.activation(sq[:, j % 2, :], pz[n % 4][:, :], ACT.Square).then_inc(sq_done, 1)
                    act.wait_ge(dve_step, 5 * j + 2)
                    act.activation(std[:, j % 2, :], var[:, j % 2, :], ACT.Sqrt).then_inc(std_done, 1)
                if g == 3 or j >= 2:
                    i = j - 2
                    if i < NQK:
                        gi, ti = jobs[i]
                        act.wait_ge(t_done, i + 1)
                        dst = qT[:, :, (ti - CT) * P:(ti - CT + 1) * P] if gi == 1 else kT[:, :, ti * P:(ti + 1) * P]
                        act.activation(dst, pt[i % 2][:, :, :], ACT.Copy).then_inc(t_copied, 1)
            act.wait_ge(t_copied, NQK)

        @block.vector
        def _(dve):
            dve.wait_ge(gain_got, 32)
            dve.tensor_scalar(gain[:, 0, :], gain[:, 0, :], HD ** -0.5, None, ALU.mult).then_inc(gain_scaled, 1)
            n = 0
            for c in range(W5 // P):
                for t0, tn in TG:
                    dve.wait_ge(mm_done, n + 1)
                    if c >= 2 and t0 == 0:
                        dve.wait_ge(u_out[c % 2], 16 * (c // 2))
                    m0, mn = t0 // LCH, tn // LCH
                    dve.tensor_copy(uT[:, c % 2, :, m0:m0 + mn],
                                    pz[n % 4][:, 0:tn].rearrange("p (m j) -> p j m", j=LCH)).then_inc(z_used, 1)
                    n += 1
            dve.wait_ge(gain_scaled, 1)
            for j, (g, t) in enumerate(jobs):
                n = NU + j
                z = pz[n % 4]
                if g == 3:
                    dve.wait_ge(mm_done, n + 1)
                    dst = v_ctx[:, t, :] if t < CT else v_even[:, t - CT, :]
                    cp = dve.tensor_copy(dst, z[:, :])
                    cp.then_inc(v_done, 1)
                    dve.wait_ge(v_done, j - NQK + 1)
                    dve.sem_inc(z_used, 1)
                    continue
                b = j % 2
                dve.wait_ge(sq_done, j + 1)
                dve.tensor_reduce(ss[:, b, :], sq[:, b, :].rearrange("p (h d) -> p h d", d=HD), AX.X, ALU.add).then_inc(dve_step, 1)
                dve.wait_ge(dve_step, 5 * j + 1)
                dve.tensor_scalar(var[:, b, :], ss[:, b, :], 1.0 / HD, EPS, ALU.mult, ALU.add).then_inc(dve_step, 1)
                dve.wait_ge(std_done, j + 1)
                dve.reciprocal(rstd[:, b, :], std[:, b, :]).then_inc(dve_step, 1)
                dve.wait_ge(dve_step, 5 * j + 3)
                if j >= 2:
                    dve.wait_ge(t_done, j - 1)
                q3 = qn[:, b, :].rearrange("p (h d) -> p h d", d=HD)
                dve.tensor_tensor(q3, z[:, :].rearrange("p (h d) -> p h d", d=HD),
                                  rstd[:, b, :, None].to_broadcast([P, HEADS, HD]), ALU.mult).then_inc(dve_step, 1)
                dve.wait_ge(dve_step, 5 * j + 4)
                dve.sem_inc(z_used, 1)
                dve.tensor_tensor(q3, q3, gain[:, g - 1, None, :].to_broadcast([P, HEADS, HD]), ALU.mult).then_inc(dve_step, 1)
                dve.wait_ge(dve_step, 5 * j + 5)
                dve.sem_inc(n_done, 1)


def bias_table(nc, rpb, pad_dram, bt):
    W = 2 * GRID_W - 1
    with Phase(nc, "bias") as ph:
        table = ph.sb("table", [HEADS * RPB_R, RPB_C])
        pad = ph.sb("pad", [HEADS * RPB_R, W])
        back = ph.sb("back", [P, HP, RPB_R, GRID_W])
        cleared, rpb_got, pad_ready, pad_out, table_in = (ph.sem(s) for s in ("cleared", "rpb_got", "pad_ready", "pad_out", "table_in"))
        forward, low, high = ph.sem("forward"), ph.sem("low"), ph.sem("high")
        block = ph.block()

        @block.sync
        def _(sp):
            sp.dma_start(table[:, :], rpb.rearrange("h r c -> (h r) c")).then_inc(rpb_got, 16)
            sp.wait_ge(pad_ready, 1)
            sp.dma_start(pad_dram, pad[:, :]).then_inc(pad_out, 16)
            sp.wait_ge(pad_out, 16)
            for a in range(2):
                for h in range(HP):
                    src = bass.AP(tensor=pad_dram.tensor, offset=(2 * h + a) * RPB_R * W,
                                  ap=[[1, GRID_W], [W, RPB_R], [1, GRID_W]])
                    sp.dma_start(back[a * 64:(a + 1) * 64, h, :, :], src).then_inc(table_in, 16)

        @block.vector
        def _(dve):
            dve.wait_ge(rpb_got, 16)
            dve.wait_ge(cleared, 1)
            first = GRID_W - 1 - (KW - 1)
            dve.tensor_copy(pad[:, first:first + RPB_C], table[:, RPB_C - 1::-1]).then_inc(pad_ready, 1)
            dve.wait_ge(table_in, 16 * 2 * HP)
            dve.tensor_copy(bt[:, :, :, :].rearrange("p h r c -> p (h r) c"),
                            back[:, :, :, :].rearrange("p h r c -> p (h r) c")[:, :, GRID_W - 1::-1]).then_inc(forward, 1)

        @block.gpsimd
        def _(pool):
            pool.memset(pad[:, :], NEG).then_inc(cleared, 1)
            pool.wait_ge(forward, 1)
            last = GRID_W - KW
            for a in range(2):
                t = bt[a * 64:(a + 1) * 64, :, :, 0:last].rearrange("p h r c -> p (h r) c")
                pool.affine_select(out=t, in_=t, compare_op=ALU.is_ge, fill=NEG, base=KW // 2,
                                   pattern=[[0, HP * RPB_R], [1, last]], channel_multiplier=-1).then_inc(low, 1)
            pool.wait_ge(low, 2)
            for a in range(2):
                t = bt[a * 64:(a + 1) * 64, :, :, KW:GRID_W].rearrange("p h r c -> p (h r) c")
                pool.affine_select(out=t, in_=t, compare_op=ALU.is_ge, fill=NEG, base=KW // 2 - 1 - KW,
                                   pattern=[[0, HP * RPB_R], [-1, GRID_W - KW]], channel_multiplier=1).then_inc(high, 1)
            pool.wait_ge(high, 2)


def attention(nc, ident, qT, kT, v_even, v_odd, v_ctx, bt, out_dram):
    units = [(h, r) for h in range(HP) for r in range(ROWS)]
    N = len(units)
    NL = KH * GRID_W
    NK = NL + CTX
    NKT = NK // P
    first_row = [min(max(r - KH // 2, 0), ROWS - KH) for r in range(ROWS)]
    with Phase(nc, "att") as ph:
        qbd = ph.sb("qbd", [P, 2, P])
        sl = ph.sb("sl", [P, 2, NL])
        m = ph.sb("m", [P, 2, 4])
        nm = ph.sb("nm", [P, 2])
        sums = ph.sb("sums", [P, 2, 2])
        den = ph.sb("den", [P, 2])
        rden = ph.sb("rden", [P, 2])
        pr = ph.sb("pr", [P, 2, NK])
        prT = ph.sb("prT", [P, 2, NKT, P])
        obd = ph.sb("obd", [P, 2, P])
        oT = ph.sb("oT", [P, HP, SEQ])
        stored = ph.sem("stored")
        p_loc = [ph.ps(f"p_loc{i}", [P, NL]) for i in range(2)]
        p_ctx = [ph.ps(f"p_ctx{i}", [P, NCH]) for i in range(2)]
        p_t = [ph.ps(f"p_t{i}", [P, 4, P]) for i in range(2)]
        p_o = ph.ps("p_o", [P, NCH])
        p_ot = ph.ps("p_ot", [P, NCH])
        zeroed = ph.sem("zeroed")
        q_ready, s_done, max_done, nm_done, exp_done = (ph.sem(s) for s in ("q_ready", "s_done", "max_done", "nm_done", "exp_done"))
        pt_done, ptc_act, ptc_dve = ph.sem("pt_done"), ph.sem("ptc_act"), ph.sem("ptc_dve")
        den_done, rden_done, pv_done, o_ready, ot_done, o_out = (ph.sem(s) for s in ("den_done", "rden_done", "pv_done", "o_ready", "ot_done", "o_out"))
        block = ph.block()

        @block.sync
        def _(sp):
            for h in range(HP):
                sp.wait_ge(o_out, 2 * ROWS * (h + 1))
                sp.dma_start(out_dram[h * P:(h + 1) * P, :], oT[:, h, :]).then_inc(stored, 16)
            sp.wait_ge(stored, 16 * HP)

        @block.gpsimd
        def _(pool):
            pool.memset(qbd[:, :, :], 0.0).then_inc(zeroed, 1)
            pool.memset(obd[:, :, :], 0.0).then_inc(zeroed, 1)
            pool.wait_ge(zeroed, 2)
            for n, (h, r) in enumerate(units):
                if n >= 2:
                    pool.wait_ge(s_done, n - 1)
                for a in range(2):
                    pool.tensor_copy(qbd[a * 64:(a + 1) * 64, n % 2, a * 64:(a + 1) * 64],
                                     qT[a * 64:(a + 1) * 64, h, r * 64:(r + 1) * 64]).then_inc(q_ready, 1)

        @block.tensor
        def _(pe):
            def scores(n):
                h, r = units[n]
                b = n % 2
                pe.wait_ge(q_ready, 2 * n + 2)
                if n >= 2:
                    pe.wait_ge(max_done, 2 * (n - 1))
                    pe.wait_ge(exp_done, 2 * (n - 1))
                k0 = CTX + first_row[r] * GRID_W
                pe.matmul(p_loc[b][:, :], qbd[:, b, :], kT[:, h, k0:k0 + NL], start=True, stop=True)
                pe.matmul(p_ctx[b][:, 0:CTX], qbd[:, b, :], kT[:, h, 0:CTX], start=True, stop=True).then_inc(s_done, 1)

            def turn(n):
                b = n % 2
                pe.wait_ge(exp_done, 2 * n + 2)
                if n >= 1:
                    pe.wait_ge(ptc_act, n)
                    pe.wait_ge(ptc_dve, n)
                for t in range(NKT):
                    tr = pe.transpose(p_t[t // 3][:, t % 3, :], pr[:, b, t * P:(t + 1) * P], ident[:, :])
                tr.then_inc(pt_done, 1)

            def values(n):
                h, r = units[n]
                b = n % 2
                pe.wait_ge(ptc_act, n + 1)
                pe.wait_ge(ptc_dve, n + 1)
                if n >= 1:
                    pe.wait_ge(o_ready, 2 * n)
                r0 = first_row[r]
                v_loc = v_odd if r0 % 2 else v_even
                for t in range(NKT):
                    v = v_loc[:, r0 // 2 + t, h * P:(h + 1) * P] if t < NL // P else v_ctx[:, t - NL // P, h * P:(h + 1) * P]
                    mm = pe.matmul(p_o[:, 0:P], prT[:, b, t, :], v, start=t == 0, stop=t == NKT - 1)
                mm.then_inc(pv_done, 1)

            def turn_out(n):
                b = n % 2
                pe.wait_ge(o_ready, 2 * n + 2)
                if n >= 1:
                    pe.wait_ge(o_out, 2 * n)
                pe.transpose(p_ot[:, 0:P], obd[:, b, :], ident[:, :]).then_inc(ot_done, 1)

            pe.wait_ge(zeroed, 2)
            for i in range(N + 3):
                if i < N:
                    scores(i)
                if 1 <= i <= N:
                    turn(i - 1)
                if 2 <= i <= N + 1:
                    values(i - 2)
                if 3 <= i:
                    turn_out(i - 3)

        @block.vector
        def _(dve):
            def maxima(n):
                h, r = units[n]
                b = n % 2
                rel = first_row[r] - r + KH - 1
                dve.wait_ge(s_done, n + 1)
                if n >= 2:
                    dve.wait_ge(exp_done, 2 * (n - 1))
                dve.tensor_tensor_reduce(sl[:, b, :], p_loc[b][:, :],
                                         bt[:, h, rel:rel + KH, :].rearrange("p r c -> p (r c)"),
                                         1.0, -3e38, ALU.add, ALU.max, m[:, b, 0:1]).then_inc(max_done, 1)
                dve.tensor_reduce(m[:, b, 1:2], p_ctx[b][:, 0:CTX], AX.X, ALU.max).then_inc(max_done, 1)
                dve.wait_ge(max_done, 2 * n + 2)
                dve.tensor_scalar(nm[:, b:b + 1], m[:, b, 0:1], m[:, b, 1:2], -1.0, ALU.max, ALU.mult).then_inc(nm_done, 1)

            def copy_half(n):
                b = n % 2
                dve.wait_ge(pt_done, n + 1)
                if n >= 2:
                    dve.wait_ge(pv_done, n - 1)
                dve.tensor_copy(prT[:, b, 3:NKT, :], p_t[1][:, 0:3, :]).then_inc(ptc_dve, 1)
                dve.wait_ge(exp_done, 2 * n + 2)
                dve.tensor_tensor(den[:, b:b + 1], sums[:, b, 0:1], sums[:, b, 1:2], ALU.add).then_inc(den_done, 1)
                dve.wait_ge(den_done, n + 1)
                dve.reciprocal(rden[:, b:b + 1], den[:, b:b + 1]).then_inc(rden_done, 1)

            def scale(n):
                b = n % 2
                dve.wait_ge(pv_done, n + 1)
                dve.wait_ge(rden_done, n + 1)
                if n >= 2:
                    dve.wait_ge(ot_done, n - 1)
                for a in range(2):
                    s = slice(a * 64, (a + 1) * 64)
                    dve.tensor_scalar(obd[s, b, s], p_o[s, s], rden[s, b:b + 1], None, ALU.mult).then_inc(o_ready, 1)

            dve.wait_ge(zeroed, 2)
            for i in range(N + 2):
                if i < N:
                    maxima(i)
                if 1 <= i <= N:
                    copy_half(i - 1)
                if 2 <= i:
                    scale(i - 2)

        @block.scalar
        def _(act):
            def exps(n):
                b = n % 2
                act.wait_ge(nm_done, n + 1)
                if n >= 2:
                    act.wait_ge(pt_done, n - 1)
                    act.wait_ge(den_done, n - 1)
                act.activation(pr[:, b, 0:NL], sl[:, b, :], ACT.Exp, bias=nm[:, b:b + 1], accum_out=sums[:, b, 0:1]).then_inc(exp_done, 1)
                act.activation(pr[:, b, NL:NK], p_ctx[b][:, 0:CTX], ACT.Exp, bias=nm[:, b:b + 1], accum_out=sums[:, b, 1:2]).then_inc(exp_done, 1)

            def copy_half(n):
                b = n % 2
                act.wait_ge(pt_done, n + 1)
                if n >= 2:
                    act.wait_ge(pv_done, n - 1)
                act.activation(prT[:, b, 0:3, :], p_t[0][:, 0:3, :], ACT.Copy).then_inc(ptc_act, 1)

            def out(n):
                h, r = units[n]
                b = n % 2
                act.wait_ge(ot_done, n + 1)
                for a in range(2):
                    s = slice(a * 64, (a + 1) * 64)
                    act.activation(oT[s, h, r * 64:(r + 1) * 64], p_ot[s, s], ACT.Copy).then_inc(o_out, 1)

            for i in range(N + 3):
                if i < N:
                    exps(i)
                if 1 <= i <= N:
                    copy_half(i - 1)
                if 3 <= i:
                    out(i - 3)
            act.wait_ge(o_out, 2 * N)


GS = G5 // 8
NP9 = LCH + 1
TAUS = 2 * LCH - 1
TWO_PI = 2 * math.pi
PI_A = 6.28125
PI_B = 0.0019350051879882812
PI_C = TWO_PI - PI_A - PI_B
ROUND = 1.5 * 2.0 ** 23


def s5_matrices(nc, ident, lam_re, lam_im, log_dt, b_re, b_im, c_re, c_im, d, mats, k_dram, rot_dram, decay):
    with Phase(nc, "mats") as ph:
        nat = ph.sb("nat", [G5, 2, 2, S5])
        ldt = ph.sb("ldt", [G5, 2])
        edt = ph.sb("edt", [G5, 2])
        dtn = ph.sb("dtn", [G5, 2, S5])
        ones = ph.sb("ones", [P, S5])
        base = ph.sb("base", [P, 3, G5])
        sm = ph.sb("sm", [P, 24, G5])
        pw = ph.sb("pw", [P, 2, NP9, G5])
        tp = ph.sb("tp", [P, 4, 4, G5])
        pg = ph.sb("pg", [P, 2, LCH, G5])
        pw9 = ph.sb("pw9", [P, 2, NP9, G5])
        bn = ph.sb("bn", [P, 2, G5, C5])
        bb = ph.sb("bb", [P, 2, G5, C5])
        cn = ph.sb("cn", [P, 2, GS, 2, S5])
        cc = ph.sb("cc", [P, 2, W5])
        g = ph.sb("g", [P, 8, LCH, C5])
        g2 = ph.sb("g2", [P, 8, LCH, C5])
        w9 = ph.sb("w9", [P, 2, G5, NP9, C5])
        big = ph.sb("big", [P, 2, 8, NP9, C5])
        winT = ph.sb("winT", [P, 2, 8, P])
        bpad = ph.sb("bpad", [P, 2, G5, P])
        dcol = ph.sb("dcol", [P, GS])
        eye16 = ph.sb("eye16", [P, C5])
        kall = ph.sb("kall", [P, GS, TAUS, C5])
        toep = ph.sb("toep", [P, G5, P])
        rot = ph.sb("rot", [P, 2, G5, NCK])
        rt = toep[:, :, :].rearrange("p (i a) c -> p i (a c)", i=4)
        p_in = ph.ps("p_in", [P, NCH])
        p_c = ph.ps("p_c", [P, 4, P])
        p_g = [ph.ps(f"p_g{i}", [P, 4, P]) for i in range(2)]
        p_k = [ph.ps(f"p_k{i}", [P, NCH]) for i in range(2)]
        got_lam, got_b, got_c, got_d = (ph.sem(s) for s in ("got_lam", "got_b", "got_c", "got_d"))
        exp_done, dtn_done, base_tr, act_done = (ph.sem(s) for s in ("exp_done", "dtn_done", "base_tr", "act_done"))
        step = ph.sem("step")
        angles, c_tr, c_copied = ph.sem("angles"), ph.sem("c_tr"), ph.sem("c_copied")
        g_ready, g_tr, g_copied, g_out = ph.sem("g_ready"), ph.sem("g_tr"), ph.sem("g_copied"), ph.sem("g_out")
        w9_ready, w9_out, bpad_ready, k_done, k_read = (ph.sem(s) for s in ("w9_ready", "w9_out", "bpad_ready", "k_done", "k_read"))
        zeroed, kall_ready, k_out, toep_in, toep_out = (ph.sem(s) for s in ("zeroed", "kall_ready", "k_out", "toep_in", "toep_out"))
        rot_ready, rot_out = ph.sem("rot_ready"), ph.sem("rot_out")
        block = ph.block()

        @block.sync
        def _(sp):
            sp.dma_start(nat[:, 0, :, :], lam_re.rearrange("s g p -> g s p")).then_inc(got_lam, 16)
            sp.dma_start(nat[:, 1, :, :], lam_im.rearrange("s g p -> g s p")).then_inc(got_lam, 16)
            sp.dma_start(ldt[:, :], log_dt.rearrange("s g -> g s"), allow_slow_non_contiguous=True).then_inc(got_lam, 16)
            for i, src in enumerate((c_re, c_im)):
                for s in range(2):
                    sp.dma_start(cn[:, i, :, s, :], src[s].rearrange("(q e) c p -> (e c) q p", e=8)).then_inc(got_c, 16)
            for i, src in enumerate((b_re, b_im)):
                for s in range(2):
                    sp.dma_start(bn[s * 64:(s + 1) * 64, i, :, :], src[s].rearrange("g p c -> p g c")).then_inc(got_b, 16)
            sp.dma_start(dcol[:, :], d.rearrange("(q e) c -> (e c) q", e=8), allow_slow_non_contiguous=True).then_inc(got_d, 16)
            for q in range(GS):
                sp.wait_ge(g_copied, 4 * (q + 1))
                for i in range(2):
                    sp.dma_start(mats[:, i, 8 * q:8 * q + 8, :], winT[:, i, :, :]).then_inc(g_out, 16)
            sp.wait_ge(w9_ready, GS)
            for i in range(2):
                sp.dma_start(mats[:, 2 + i, :, :], w9[:, i, :, 0:LCH, :].rearrange("p g j c -> p g (j c)")).then_inc(w9_out, 16)
            sp.wait_ge(rot_ready, 1)
            sp.dma_start(rot_dram, rot[:, :, :, :]).then_inc(rot_out, 16)
            sp.wait_ge(kall_ready, GS)
            sp.dma_start(k_dram.rearrange("(q e c) t -> (e c) q t", e=8, c=C5), kall[:, :, :, :].rearrange("p q t c -> p q (t c)")).then_inc(k_out, 16)
            sp.wait_ge(k_out, 16)
            for i in range(LCH):
                src = k_dram.rearrange("(g c) t -> c g t", c=C5)[:, :, (LCH - 1 - i) * C5:(2 * LCH - 1 - i) * C5]
                sp.dma_start(toep[i * C5:(i + 1) * C5, :, :], src).then_inc(toep_in, 16)
            sp.wait_ge(toep_in, 16 * LCH)
            sp.dma_start(mats[:, 4, :, :], toep[:, :, :]).then_inc(toep_out, 16)
            sp.wait_ge(g_out, 16 * 2 * GS)
            sp.wait_ge(w9_out, 32)
            sp.wait_ge(toep_out, 16)
            sp.wait_ge(rot_out, 16)

        @block.scalar
        def _(act):
            act.wait_ge(got_lam, 48)
            act.activation(edt[:, :], ldt[:, :], ACT.Exp).then_inc(exp_done, 1)
            act.wait_ge(angles, 1)
            act.activation(sm[:, 4, :], sm[:, 2, :], ACT.Exp).then_inc(act_done, 1)
            act.activation(decay[:, :], sm[:, 2, :], ACT.Exp, scale=float(LCH)).then_inc(act_done, 1)
            act.wait_ge(angles, 2)
            act.activation(sm[:, 8, :], sm[:, 5, :], ACT.Sin).then_inc(act_done, 1)
            act.activation(sm[:, 9, :], sm[:, 7, :], ACT.Sin).then_inc(act_done, 1)
            for q in range(GS):
                for i in range(2):
                    for h in range(2):
                        n = 4 * q + 2 * i + h
                        act.wait_ge(g_tr, n + 1)
                        if q >= 1:
                            act.wait_ge(g_out, 16 * 2 * q)
                        act.activation(winT[:, i, 4 * h:4 * h + 4, :], p_g[n % 2][:, :, :], ACT.Copy).then_inc(g_copied, 1)
            act.wait_ge(g_copied, 4 * GS)

        @block.gpsimd
        def _(pool):
            pool.memset(bpad[:, :, :, :], 0.0).then_inc(zeroed, 1)

        @block.tensor
        def _(pe):
            pe.wait_ge(dtn_done, 2)
            for i, src in enumerate((nat[:, 0, :, :], nat[:, 1, :, :], dtn[:, :, :])):
                tr = pe.transpose(p_in[:, i * G5:(i + 1) * G5], src.rearrange("g s p -> g (s p)"), ident[0:G5, 0:G5])
            tr.then_inc(base_tr, 1)
            pe.wait_ge(got_c, 64)
            for i in range(2):
                if i == 1:
                    pe.wait_ge(c_copied, 1)
                for q in range(GS):
                    tr = pe.transpose(p_c[:, q, :], cn[:, i, q, :, :].rearrange("p s c -> p (s c)"), ident[:, :])
                tr.then_inc(c_tr, 1)
            for q in range(GS):
                for i in range(2):
                    pe.wait_ge(g_ready, 2 * q + i + 1)
                    for h in range(2):
                        n = 4 * q + 2 * i + h
                        if n >= 2:
                            pe.wait_ge(g_copied, n - 1)
                        for e in range(4):
                            tr = pe.transpose(p_g[n % 2][:, e, :], (g, g2)[i][:, 4 * h + e, :, :].rearrange("p j c -> p (j c)"), ident[:, :])
                        tr.then_inc(g_tr, 1)
            pe.wait_ge(bpad_ready, 1)
            pe.wait_ge(w9_ready, GS)
            for q in range(GS):
                for s in range(2):
                    if q >= 1:
                        pe.wait_ge(k_read, q)
                    r = slice(s * 64, (s + 1) * 64)
                    for e in range(8):
                        for i in range(2):
                            mm = pe.matmul(p_k[s][:, 0:NP9 * C5], bpad[r, i, 8 * q + e, :],
                                           w9[r, i, 8 * q + e, :, :].rearrange("p j c -> p (j c)"),
                                           start=e == 0 and i == 0, stop=e == 7 and i == 1)
                    mm.then_inc(k_done, 1)

        @block.vector
        def _(dve):
            link = Chain(dve, step)

            def cmul(o_re, o_im, a_re, a_im, b_re_, b_im_, t):
                dve.tensor_tensor(t[0], a_re, b_re_, ALU.mult).then_inc(step, 1)
                dve.tensor_tensor(t[1], a_im, b_im_, ALU.mult).then_inc(step, 1)
                dve.tensor_tensor(t[2], a_re, b_im_, ALU.mult).then_inc(step, 1)
                dve.tensor_tensor(t[3], a_im, b_re_, ALU.mult).then_inc(step, 1)
                link.n += 4
                dve.wait_ge(step, link.n)
                dve.tensor_tensor(o_re, t[0], t[1], ALU.subtract).then_inc(step, 1)
                dve.tensor_tensor(o_im, t[2], t[3], ALU.add).then_inc(step, 1)
                link.n += 2
                dve.wait_ge(step, link.n)

            dve.wait_ge(exp_done, 1)
            link(dve.memset(ones[:, :], 1.0))
            for s in range(2):
                dve.tensor_scalar(dtn[:, s, :], ones[0:G5, :], edt[:, s:s + 1], None, ALU.mult).then_inc(dtn_done, 1)
            dve.wait_ge(base_tr, 1)
            link(dve.tensor_copy(base[:, :, :], p_in[:, 0:3 * G5].rearrange("p (i g) -> p i g", i=3)))
            re, im, dt = base[:, 0, :], base[:, 1, :], base[:, 2, :]
            T = lambda i: sm[:, i, :]
            link(dve.tensor_scalar(T(0), re, -1e-4, None, ALU.min))
            link(dve.tensor_tensor(T(1), im, dt, ALU.mult))
            dve.tensor_tensor(T(2), T(0), dt, ALU.mult).then_inc(angles, 1)
            link(dve.tensor_scalar(T(3), T(1), 1.0 / TWO_PI, None, ALU.mult))
            link(dve.tensor_scalar(T(3), T(3), ROUND, None, ALU.add))
            link(dve.tensor_scalar(T(3), T(3), ROUND, None, ALU.subtract))
            link(dve.scalar_tensor_tensor(T(5), T(3), -PI_A, T(1), ALU.mult, ALU.add))
            link(dve.scalar_tensor_tensor(T(5), T(3), -PI_B, T(5), ALU.mult, ALU.add))
            link(dve.scalar_tensor_tensor(T(5), T(3), -PI_C, T(5), ALU.mult, ALU.add))
            link(dve.tensor_scalar(T(6), T(5), math.pi / 2, None, ALU.add))
            link(dve.tensor_scalar(T(7), T(6), math.pi, -TWO_PI, ALU.is_gt, ALU.mult))
            link(dve.tensor_tensor(T(7), T(6), T(7), ALU.add))
            link(dve.tensor_scalar(T(5), T(5), 3.1415925, -3.1415925, ALU.min, ALU.max))
            link(dve.tensor_scalar(T(7), T(7), 3.1415925, -3.1415925, ALU.min, ALU.max))
            dve.sem_inc(angles, 1)
            dve.wait_ge(act_done, 4)
            link(dve.memset(pw[:, 0, 0, :], 1.0))
            link(dve.memset(pw[:, 1, 0, :], 0.0))
            link(dve.tensor_tensor(pw[:, 1, 1, :], T(8), T(4), ALU.mult))
            link(dve.tensor_tensor(pw[:, 0, 1, :], T(9), T(4), ALU.mult))
            for m in (1, 2, 4):
                x = [tp[:, i, 0:m, :] for i in range(4)]
                top = [pw[:, i, m, None, :].to_broadcast([P, m, G5]) for i in range(2)]
                cmul(pw[:, 0, m + 1:2 * m + 1, :], pw[:, 1, m + 1:2 * m + 1, :],
                     pw[:, 0, 1:m + 1, :], pw[:, 1, 1:m + 1, :], top[0], top[1], x)
            f, b = slice(0, 64), slice(64, P)
            for i in range(2):
                link(dve.tensor_copy(pg[f, i, :, :], pw[f, i, LCH - 1::-1, :]))
                link(dve.tensor_copy(pg[b, i, :, :], pw[b, i, 0:LCH, :]))
                link(dve.tensor_copy(pw9[f, i, 0:LCH, :], pw[f, i, 1:NP9, :]))
                link(dve.tensor_copy(pw9[b, i, 0:LCH, :], pw[b, i, LCH:0:-1, :]))
                link(dve.tensor_copy(pw9[:, i, LCH, :], pw[:, i, 0, :]))
            link(dve.tensor_scalar(T(10), pw[:, 0, 1, :], -1.0, None, ALU.add))
            link(dve.tensor_tensor(T(11), T(0), T(0), ALU.mult))
            link(dve.tensor_tensor(T(12), im, im, ALU.mult))
            link(dve.tensor_tensor(T(11), T(11), T(12), ALU.add))
            link(dve.reciprocal(T(12), T(11)))
            link(dve.tensor_tensor(T(13), T(0), T(12), ALU.mult))
            link(dve.tensor_tensor(T(14), im, T(12), ALU.mult))
            link(dve.tensor_scalar(T(14), T(14), -1.0, None, ALU.mult))
            cmul(T(15), T(16), T(10), pw[:, 1, 1, :], T(13), T(14), [T(17), T(18), T(19), T(20)])
            dve.wait_ge(got_b, 64)
            fr, fi = (T(i)[:, :, None].to_broadcast([P, G5, C5]) for i in (15, 16))
            tb = [big[:, i, :, :, :].rearrange("p e j c -> p (e j c)")[:, 0:G5 * C5].rearrange("p (g c) -> p g c", g=G5) for i in range(2)]
            tc = [big[:, i, :, :, :].rearrange("p e j c -> p (e j c)")[:, G5 * C5:2 * G5 * C5].rearrange("p (g c) -> p g c", g=G5) for i in range(2)]
            cmul(bb[:, 0, :, :], bb[:, 1, :, :], bn[:, 0, :, :], bn[:, 1, :, :], fr, fi, [tb[0], tb[1], tc[0], tc[1]])
            for i in range(2):
                dve.wait_ge(c_tr, i + 1)
                dve.tensor_copy(cc[:, i, :], p_c[:, :, :].rearrange("p q c -> p (q c)")).then_inc(c_copied, 1)
            dve.wait_ge(c_copied, 2)
            dve.wait_ge(zeroed, 1)
            for i in range(2):
                for e in range(8):
                    link(dve.tensor_copy(bpad[:, i, e::8, e * C5:(e + 1) * C5], bb[:, i, e::8, :]))
            dve.sem_inc(bpad_ready, 1)
            for q in range(GS):
                e8 = slice(8 * q, 8 * q + 8)
                sh = [P, 8, LCH, C5]
                pr = [pg[:, i, :, e8].rearrange("p j g -> p g j")[:, :, :, None].to_broadcast(sh) for i in range(2)]
                br = [bb[:, i, e8, None, :].to_broadcast(sh) for i in range(2)]
                t0, t1 = big[:, 0, :, 0:LCH, :], big[:, 1, :, 0:LCH, :]
                if q >= 1:
                    dve.wait_ge(g_tr, 4 * q)
                link(dve.tensor_tensor(t0, pr[0], br[0], ALU.mult))
                link(dve.tensor_tensor(t1, pr[1], br[1], ALU.mult))
                link(dve.tensor_tensor(g[:, :, :, :], t0, t1, ALU.subtract))
                dve.sem_inc(g_ready, 1)
                link(dve.tensor_tensor(t0, pr[0], br[1], ALU.mult))
                link(dve.tensor_tensor(t1, pr[1], br[0], ALU.mult))
                link(dve.tensor_tensor(g2[:, :, :, :], t0, t1, ALU.add))
                dve.sem_inc(g_ready, 1)
                sh = [P, 8, NP9, C5]
                pr = [pw9[:, i, :, e8].rearrange("p j g -> p g j")[:, :, :, None].to_broadcast(sh) for i in range(2)]
                cr = [cc[:, i, 8 * q * C5:8 * (q + 1) * C5].rearrange("p (g c) -> p g c", g=8)[:, :, None, :].to_broadcast(sh) for i in range(2)]
                t0, t1 = big[:, 0, :, :, :], big[:, 1, :, :, :]
                link(dve.tensor_tensor(t0, pr[0], cr[0], ALU.mult))
                link(dve.tensor_tensor(t1, pr[1], cr[1], ALU.mult))
                link(dve.tensor_tensor(w9[:, 0, e8, :, :], t0, t1, ALU.subtract))
                link(dve.tensor_tensor(t0, pr[0], cr[1], ALU.mult))
                link(dve.tensor_tensor(t1, pr[1], cr[0], ALU.mult))
                link(dve.tensor_tensor(t0, t0, t1, ALU.add))
                link(dve.tensor_scalar(w9[:, 1, e8, :, :], t0, -1.0, None, ALU.mult))
                dve.sem_inc(w9_ready, 1)
            u = [(T(9), T(8))]
            spare = iter([(T(21), T(22)), (T(4), T(23)), (T(21), T(22))])
            for _ in range(3):
                nre, nim = next(spare)
                cmul(nre, nim, u[-1][0], u[-1][1], u[-1][0], u[-1][1], [T(17), T(18), T(19), T(20)])
                u.append((nre, nim))
            link(dve.memset(rot[:, 0, :, 0], 1.0))
            link(dve.memset(rot[:, 1, :, 0], 0.0))
            link(dve.tensor_copy(rot[:, 0, :, 1], u[-1][0]))
            link(dve.tensor_copy(rot[:, 1, :, 1], u[-1][1]))
            m = 1
            while m < NCK - 1:
                n = min(m, NCK - 1 - m, 32)
                w = n * G5
                x = [rt[:, i, 0:w].rearrange("p (g n) -> p g n", g=G5) for i in range(4)]
                top = [rot[:, i, :, m:m + 1].to_broadcast([P, G5, n]) for i in range(2)]
                cmul(rot[:, 0, :, m + 1:m + 1 + n], rot[:, 1, :, m + 1:m + 1 + n],
                     rot[:, 0, :, 1:1 + n], rot[:, 1, :, 1:1 + n], top[0], top[1], x)
                m += n
            dve.sem_inc(rot_ready, 1)
            link(dve.tensor_reduce(eye16[:, :], ident[:, :].rearrange("p (q c) -> p c q", c=C5), AX.X, ALU.add))
            dve.wait_ge(got_d, 16)
            for q in range(GS):
                dve.wait_ge(k_done, 2 * q + 2)
                kf = p_k[0][:, 0:NP9 * C5].rearrange("p (t c) -> p t c", c=C5)
                kb = p_k[1][:, 0:NP9 * C5].rearrange("p (t c) -> p t c", c=C5)
                link(dve.tensor_copy(kall[:, q, 0:LCH - 1, :], kb[:, 1:LCH, :]))
                link(dve.tensor_copy(kall[:, q, LCH:TAUS, :], kf[:, 0:LCH - 1, :]))
                link(dve.scalar_tensor_tensor(kall[:, q, LCH - 1, :], eye16[:, :], dcol[:, q:q + 1], kf[:, LCH, :], ALU.mult, ALU.add))
                link(dve.tensor_tensor(kall[:, q, LCH - 1, :], kall[:, q, LCH - 1, :], kb[:, LCH, :], ALU.add))
                dve.sem_inc(k_read, 1)
                dve.sem_inc(kall_ready, 1)


def s5_scan_readout(nc, ident, u_dram, mats, rot_dram, decay, y_dram, w_glu, b_glu, out_dram):
    NX = NCK + NCC
    SC = 8
    L0 = NCC - 1
    with Phase(nc, "scan") as ph:
        u = ph.sb("u", [P, G5, NX])
        mt = ph.sb("mt", [P, 3, 5, 2, P])
        bs = ph.sb("bs", [P, 2, SC, NCK])
        xs = ph.sb("xs", [P, 2, SC, NCK])
        tmp = ph.sb("tmp", [P, 4, SC, NCK])
        dk = ph.sb("dk", [P, SC, NCK])
        ones = ph.sb("ones", [P, NCK])
        rot = ph.sb("rot", [P, 2, 2, SC, NCK])
        rot_in = [ph.sem(f"rot_in{i}") for i in range(2)]
        st = ph.sb("st", [P, 2, SC, NCL])
        y = ph.sb("y", [P, 2, SC, NCL])
        p_b = [[ph.ps(f"p_b{i}{n}", [P, 2, NCK]) for n in range(2)] for i in range(2)]
        p_y = [ph.ps(f"p_y{n}", [P, 2, NCL]) for n in range(2)]
        u_in, m_in = ph.sem("u_in"), [ph.sem(f"m_in{i}") for i in range(3)]
        b_mm, b_out, step, st_ready, y_mm, y_out = (ph.sem(s) for s in ("b_mm", "b_out", "step", "st_ready", "y_mm", "y_out"))
        y_st = [ph.sem(f"y_st{i}") for i in range(2)]
        step_a = ph.sem("step_a")
        dk_ready = ph.sem("dk_ready")
        block = ph.block()
        NPAIR = SC // 2
        TOTAL = GS * NPAIR

        order = []
        for q in range(GS + 1):
            if q < GS:
                order += [(0, q, e) for e in range(NPAIR)]
            if q >= 1:
                order += [(1, q - 1, e) for e in range(NPAIR)]

        @block.sync
        def _(sp):
            for j in range(LCH):
                src = u_dram.rearrange("(g c) (j m) -> j c g m", c=C5, j=LCH)[j]
                sp.dma_start(u[j * C5:(j + 1) * C5, :, 0:NCK], src).then_inc(u_in, 16)
                sp.dma_start(u[j * C5:(j + 1) * C5, :, NCK:NX], src[:, :, 0:NCC]).then_inc(u_in, 16)
            for q in range(2):
                sp.dma_start(rot[:, q, :, :, :], rot_dram[:, :, SC * q:SC * (q + 1), :]).then_inc(rot_in[q], 16)
            nb, ny, users = 0, 0, []
            for n, (s, q, e) in enumerate(order):
                if n >= 3:
                    k, v = users[n - 3]
                    sp.wait_ge((b_mm, y_mm)[k], v)
                if s == 0:
                    nb += 1
                    users.append((0, nb))
                else:
                    ny += 1
                    users.append((1, ny))
                g0 = SC * q + 2 * e
                sel = slice(0, 2) if s == 0 else slice(2, 5)
                if s == 1 and e == 0 and q < GS - 2:
                    sp.wait_ge(st_ready, q + 1)
                    sp.dma_start(rot[:, q % 2, :, :, :], rot_dram[:, :, SC * (q + 2):SC * (q + 3), :]).then_inc(rot_in[q % 2], 16)
                sp.dma_start(mt[:, n % 3, sel, :, :], mats[:, sel, g0:g0 + 2, :]).then_inc(m_in[n % 3], 16)

        @block.gpsimd
        def _(pool):
            for q in range(GS):
                pool.wait_ge(y_out, NPAIR * (q + 1))
                for j in range(LCH):
                    dst = y_dram.rearrange("(g c) (j m) -> j c g m", c=C5, j=LCH)[j][:, SC * q:SC * (q + 1), :]
                    pool.dma_start(dst, y[j * C5:(j + 1) * C5, q % 2, :, :]).then_inc(y_st[q % 2], 16)
            for i in range(2):
                pool.wait_ge(y_st[i], 16 * LCH * GS // 2)

        @block.tensor
        def _(pe):
            pe.wait_ge(u_in, 16 * 2 * LCH)
            nb = ny = 0
            f, b = slice(0, 64), slice(64, P)
            for n, (s, q, e) in enumerate(order):
                pe.wait_ge(m_in[n % 3], 16 * (n // 3 + 1))
                m = mt[:, n % 3]
                if s == 0:
                    if nb >= 2:
                        pe.wait_ge(b_out, 2 * (nb - 1))
                    for i in range(2):
                        for k in range(2):
                            g = SC * q + 2 * e + k
                            pe.matmul(p_b[i][nb % 2][f, k, :], m[:, i, k, f], u[:, g, 0:NCK], start=True, stop=True)
                            mm = pe.matmul(p_b[i][nb % 2][b, k, :], m[:, i, k, b], u[:, g, NX - 1:NCC - 1:-1], start=True, stop=True)
                    nb += 1
                    mm.then_inc(b_mm, 1)
                else:
                    if ny >= 2:
                        pe.wait_ge(y_out, ny - 1)
                    pe.wait_ge(st_ready, q + 1)
                    for k in range(2):
                        g, l = SC * q + 2 * e + k, 2 * e + k
                        o = p_y[ny % 2][:, k, :]
                        pe.matmul(o, m[:, 4, k, :], u[:, g, NCC:NCK], start=True, stop=False)
                        pe.matmul(o, m[:, 2, k, :], st[:, 0, l, :], start=False, stop=False)
                        mm = pe.matmul(o, m[:, 3, k, :], st[:, 1, l, :], start=False, stop=True)
                    mm.then_inc(y_mm, 1)
                    ny += 1

        @block.scalar
        def _(act):
            nb = ny = 0
            for n, (s, q, e) in enumerate(order):
                if s == 0:
                    act.wait_ge(b_mm, nb + 1)
                    if e == 0 and q >= 1:
                        act.wait_ge(step_a, 4 * q)
                    for i in range(2):
                        act.activation(bs[:, i, 2 * e:2 * e + 2, :], p_b[i][nb % 2][:, :, :], ACT.Copy).then_inc(b_out, 1)
                    nb += 1
                else:
                    act.wait_ge(y_mm, ny + 1)
                    if e == 0 and q >= 2:
                        act.wait_ge(y_st[q % 2], 16 * LCH * (q // 2))
                    act.activation(y[:, q % 2, 2 * e:2 * e + 2, :], p_y[ny % 2][:, :, :], ACT.Copy).then_inc(y_out, 1)
                    ny += 1

        @block.vector
        def _(dve):
            link = Chain(dve, step)
            link(dve.memset(ones[:, :], 1.0))
            for q in range(GS):
                c, s = rot[:, q % 2, 0, :, :], rot[:, q % 2, 1, :, :]
                dve.wait_ge(rot_in[q % 2], 16 * (q // 2 + 1))
                for e in range(SC):
                    dve.tensor_scalar(dk[:, e, :], ones[:, :], decay[:, SC * q + e:SC * q + e + 1], None, ALU.mult).then_inc(step, 1)
                link.n += SC
                dve.wait_ge(step, link.n)
                link(dve.memset(dk[:, :, 0:1], 0.0))
                dve.wait_ge(b_out, 2 * NPAIR * (q + 1))
                dve.tensor_tensor(tmp[:, 0, :, :], bs[:, 0, :, :], c, ALU.mult).then_inc(step_a, 1)
                dve.tensor_tensor(tmp[:, 1, :, :], bs[:, 1, :, :], s, ALU.mult).then_inc(step_a, 1)
                dve.tensor_tensor(tmp[:, 2, :, :], bs[:, 1, :, :], c, ALU.mult).then_inc(step_a, 1)
                dve.tensor_tensor(tmp[:, 3, :, :], bs[:, 0, :, :], s, ALU.mult).then_inc(step_a, 1)
                dve.wait_ge(step_a, 4 * (q + 1))
                dve.tensor_tensor(tmp[:, 0, :, :], tmp[:, 0, :, :], tmp[:, 1, :, :], ALU.add).then_inc(step, 1)
                dve.tensor_tensor(tmp[:, 2, :, :], tmp[:, 2, :, :], tmp[:, 3, :, :], ALU.subtract).then_inc(step, 1)
                link.n += 2
                dve.wait_ge(step, link.n)
                flat = lambda t: t.rearrange("p g m -> p (g m)")
                for i in range(2):
                    dve.tensor_tensor_scan(flat(xs[:, i, :, :]), flat(dk[:, :, :]), flat(tmp[:, 2 * i, :, :]),
                                           0.0, ALU.mult, ALU.add).then_inc(step, 1)
                link.n += 2
                dve.wait_ge(step, link.n)
                w = slice(L0, L0 + NCL)
                x0, x1, cw, sw = xs[:, 0, :, w], xs[:, 1, :, w], c[:, :, w], s[:, :, w]
                t = [tmp[:, i, :, 0:NCL] for i in range(4)]
                for o, a, r in ((0, x0, cw), (1, x1, sw), (2, x1, cw), (3, x0, sw)):
                    dve.tensor_tensor(t[o], a, r, ALU.mult).then_inc(step, 1)
                link.n += 4
                dve.wait_ge(step, link.n)
                if q >= 1:
                    dve.wait_ge(y_mm, NPAIR * q)
                for r, back in ((slice(0, 64), 1), (slice(64, P), -1)):
                    dve.tensor_tensor(st[r, 0, :, ::back], t[0][r], t[1][r], ALU.subtract).then_inc(step, 1)
                    dve.tensor_tensor(st[r, 1, :, ::back], t[2][r], t[3][r], ALU.add).then_inc(step, 1)
                link.n += 4
                dve.wait_ge(step, link.n)
                dve.sem_inc(st_ready, 1)

    NT = W5 // P
    with Phase(nc, "glu") as ph:
        yT = ph.sb("yT", [P, NT, LCH, NCL])
        gT = ph.sb("gT", [P, NT, SEQ])
        w = ph.sb("w", [P, NT, W5])
        bias = ph.sb("bias", [P, NT])
        sg = ph.sb("sg", [P, 2, NCH])
        oT = ph.sb("oT", [P, NT, SEQ])
        stored = ph.sem("stored")
        pz = [ph.ps(f"pz{i}", [P, NCH]) for i in range(2)]
        y_in, w_in = [ph.sem(f"y_in{i}") for i in range(NT)], ph.sem("w_in")
        gelu_done, mm_done, sg_done, out_done = (ph.sem(s) for s in ("gelu_done", "mm_done", "sg_done", "out_done"))
        block = ph.block()

        @block.sync
        def _(sp):
            for i in range(NT):
                sp.dma_start(yT[:, i, :, :].rearrange("p j m -> p (j m)"), y_dram[i * P:(i + 1) * P, :]).then_inc(y_in[i], 16)
            sp.dma_start(w[:, :, :], w_glu.rearrange("(k p) n -> p k n", p=P)).then_inc(w_in, 16)
            sp.dma_start(bias[:, :], b_glu.rearrange("(k p) -> p k", p=P), allow_slow_non_contiguous=True).then_inc(w_in, 16)
            for i in range(NT):
                sp.wait_ge(out_done, 2 * i + 2)
                sp.dma_start(out_dram[i * P:(i + 1) * P, :], oT[:, i, :]).then_inc(stored, 16)
            sp.wait_ge(stored, 16 * NT)

        @block.scalar
        def _(act):
            for i in range(NT):
                act.wait_ge(y_in[i], 16)
                act.activation(gT[:, i, :].rearrange("p (m j) -> p j m", j=LCH), yT[:, i, :, :], ACT.Gelu_apprx_tanh).then_inc(gelu_done, 1)
            act.wait_ge(w_in, 32)
            for n in range(2 * NT):
                act.wait_ge(mm_done, n + 1)
                if n >= 2:
                    act.wait_ge(out_done, n - 1)
                act.activation(sg[:, n % 2, :], pz[n % 2][:, :], ACT.Sigmoid, bias=bias[:, n // 2:n // 2 + 1]).then_inc(sg_done, 1)

        @block.tensor
        def _(pe):
            pe.wait_ge(w_in, 32)
            pe.wait_ge(gelu_done, NT)
            for n in range(2 * NT):
                if n >= 2:
                    pe.wait_ge(sg_done, n - 1)
                for k in range(NT):
                    mm = pe.matmul(pz[n % 2][:, :], w[:, k, (n // 2) * P:(n // 2 + 1) * P], gT[:, k, (n % 2) * NCH:(n % 2 + 1) * NCH],
                                   start=k == 0, stop=k == NT - 1)
                mm.then_inc(mm_done, 1)

        @block.vector
        def _(dve):
            for n in range(2 * NT):
                dve.wait_ge(sg_done, n + 1)
                s = slice((n % 2) * NCH, (n % 2 + 1) * NCH)
                dve.tensor_tensor(oT[:, n // 2, s], sg[:, n % 2, :], gT[:, n // 2, s], ALU.mult).then_inc(out_done, 1)
            dve.wait_ge(out_done, 2 * NT)

MAXB = SEQ * TOPK // P + NE - 1
NIDX = P + 2
PAD_ROWS = P
SCALE = 2.5


def residual(nc, tag, srcT, w, bias, gate, h, x=None, src_dram=None):
    with Phase(nc, tag) as ph:
        wb = ph.sb("w", [P, KD, D])
        row = ph.sb("row", [1, D]) if bias is not None else None
        ones = ph.sb("ones", [1, P])
        tmp = ph.sb("tmp", [P, 2, NCH])
        pz = [ph.ps(f"pz{i}", [P, NCH]) for i in range(4)]
        w_in, b_in, ones_done = [ph.sem(f"w_in{i}") for i in range(2)], ph.sem("b_in"), ph.sem("ones_done")
        x_in = ph.sem("x_in")
        s_in = ph.sem("s_in")
        mm_done, gated, added = ph.sem("mm_done"), ph.sem("gated"), ph.sem("added")
        jobs = [(t, n) for n in range(2) for t in range(TT)]
        w_v = w.rearrange("(k p) n -> p k n", p=P)
        block = ph.block()

        @block.sync
        def _(sp):
            if src_dram is not None:
                sp.dma_start(srcT[:, :, :], src_dram.rearrange("(k p) n -> p k n", p=P)).then_inc(s_in, 16)
            for n in range(2):
                sp.dma_start(wb[:, :, n * NCH:(n + 1) * NCH], w_v[:, :, n * NCH:(n + 1) * NCH]).then_inc(w_in[n], 16)
                if n == 0 and x is not None:
                    sp.dma_start(h[:, :, :], x.rearrange("(t p) d -> p t d", p=P)).then_inc(x_in, 16)
            if bias is not None:
                sp.dma_start(row[:, :], bias[None, :]).then_inc(b_in, 16)

        @block.tensor
        def _(pe):
            if src_dram is not None:
                pe.wait_ge(s_in, 16)
            if bias is not None:
                pe.wait_ge(b_in, 16)
                pe.wait_ge(ones_done, 1)
            for j, (t, n) in enumerate(jobs):
                pe.wait_ge(w_in[n], 16)
                if j >= 4:
                    pe.wait_ge(gated, j - 3)
                s = slice(n * NCH, (n + 1) * NCH)
                for k in range(KD):
                    mm = pe.matmul(pz[j % 4][:, :], srcT[:, k, t * P:(t + 1) * P], wb[:, k, s],
                                   start=k == 0, stop=k == KD - 1 and bias is None)
                if bias is not None:
                    mm = pe.matmul(pz[j % 4][:, :], ones[:, :], row[:, s], start=False, stop=True)
                mm.then_inc(mm_done, 1)

        @block.vector
        def _(dve):
            dve.memset(ones[:, :], 1.0).then_inc(ones_done, 1)
            if x is not None:
                dve.wait_ge(x_in, 16)
            for j, (t, n) in enumerate(jobs):
                dve.wait_ge(mm_done, j + 1)
                if j >= 2:
                    dve.wait_ge(added, j - 1)
                s = slice(n * NCH, (n + 1) * NCH)
                dve.tensor_tensor(tmp[:, j % 2, :], pz[j % 4][:, :], gate[:, s], ALU.mult).then_inc(gated, 1)
                dve.wait_ge(gated, j + 1)
                dve.tensor_tensor(h[:, t, s], h[:, t, s], tmp[:, j % 2, :], ALU.add).then_inc(added, 1)
            dve.wait_ge(added, len(jobs))


def route_and_share(nc, tag, ident, fT, w_router, r_bias, w_sg, w_su, w_sd, f_dram, acc_dram, idx, wslot, meta, eb):
    with Phase(nc, tag) as ph:
        wr = ph.sb("wr", [P, KD, NE])
        rb = ph.sb("rb", [P, NE])
        wg = ph.sb("wg", [P, KD, FF])
        wu = ph.sb("wu", [P, KD, FF])
        wd = ph.sb("wd", [P, 2, D])
        zero = ph.sb("zero", [P, D])
        sil, up = ph.sb("sil", [P, 2, FF]), ph.sb("up", [P, 2, FF])
        hid, hidT = ph.sb("hid", [P, 2, FF]), ph.sb("hidT", [P, 2, 2, P])
        yo = ph.sb("yo", [P, 2, D])
        sc, sel, ms, mr, M = (ph.sb(s, [P, TT, NE]) for s in ("sc", "sel", "ms", "mr", "M"))
        t1, t2, gate, slot = (ph.sb(s, [P, TT, NE]) for s in ("t1", "t2", "gate", "slot"))
        gm = ph.sb("gm", [P, 8, TT, NG])
        low = ph.sb("low", [P, NG, NG])
        tri, ones, iota_f = ph.sb("tri", [P, P]), ph.sb("ones", [P, P]), ph.sb("iota_f", [P, P])
        iota_i = ph.sb("iota_i", [P, P], I32)
        col_i, col = ph.sb("col_i", [P, 1], I32), ph.sb("col", [P, 1])
        tok = ph.sb("tok", [P, TT])
        top = ph.sb("top", [P, TT, 8])
        s8, q8, r8, w8 = (ph.sb(s, [P, TT, TOPK]) for s in ("s8", "q8", "r8", "w8"))
        s8i, q8i, r8i = (ph.sb(s, [P, TT, TOPK], I32) for s in ("s8i", "q8i", "r8i"))
        den, rden = ph.sb("den", [P, TT]), ph.sb("rden", [P, TT])
        nbk = ph.sb("nbk", [P, 4, NE])
        thr = ph.sb("thr", [P, NE, KD])
        ebc = ph.sb("ebc", [P, 2])
        hot_r = ph.sb("hot_r", [P, 4, P])
        hot_q = ph.sb("hot_q", [P, 4, 2, P])
        tabf = ph.sb("tabf", [P, 2, P])
        p_l, p_pos = ph.ps("p_l", [P, TT, NE]), ph.ps("p_pos", [P, TT, NE])
        p_misc = ph.ps("p_misc", [P, NCH])
        p_g, p_u, p_h = ph.ps("p_g", [P, NCH]), ph.ps("p_u", [P, NCH]), ph.ps("p_h", [P, NCH])
        p_d = [ph.ps(f"p_d{i}", [P, NCH]) for i in range(2)]
        got_r, got_w, got_b = ph.sem("got_r"), ph.sem("got_w"), ph.sem("got_b")
        zeroed, zero_out, consts, made, step = (ph.sem(s) for s in ("zeroed", "zero_out", "consts", "made", "step"))
        logits, scored, masked, counted, placed = (ph.sem(s) for s in ("logits", "scored", "masked", "counted", "placed"))
        hot_ready, hot_mm, eb_ready, eb_mm, tri_ready, ones_ready = (ph.sem(s) for s in ("hot_ready", "hot_mm", "eb_ready", "eb_mm", "tri_ready", "ones_ready"))
        gu_done, sil_done, hid_ready, h_tr, h_out, d_done, y_ready = (ph.sem(s) for s in ("gu_done", "sil_done", "hid_ready", "h_tr", "h_out", "d_done", "y_ready"))
        y_st = [ph.sem(f"y_st{i}") for i in range(2)]
        block = ph.block()

        @block.sync
        def _(sp):
            sp.dma_start(wr[:, :, :], w_router.rearrange("(p k) e -> p k e", k=KD)).then_inc(got_r, 16)
            sp.dma_start(rb[:, :], r_bias[None, :].to_broadcast([P, NE])).then_inc(got_b, 16)
            sp.dma_start(wg[:, :, :], w_sg.rearrange("(p k) f -> p k f", k=KD)).then_inc(got_w, 16)
            sp.dma_start(wu[:, :, :], w_su.rearrange("(p k) f -> p k f", k=KD)).then_inc(got_w, 16)
            sp.dma_start(wd[:, :, :], w_sd.rearrange("(j p) n -> p j n", p=P)).then_inc(got_w, 16)
            sp.wait_ge(zeroed, 1)
            sp.dma_start(f_dram[SEQ:SEQ + PAD_ROWS, :], zero[:, :]).then_inc(zero_out, 16)
            sp.dma_start(acc_dram[SEQ:SEQ + PAD_ROWS, :], zero[:, :]).then_inc(zero_out, 16)
            for t in range(TT):
                sp.wait_ge(y_ready, 2 * t + 2)
                sp.dma_start(acc_dram[t * P:(t + 1) * P, :], yo[:, t % 2, :]).then_inc(y_st[t % 2], 16)
            sp.wait_ge(zero_out, 32)
            for i in range(2):
                sp.wait_ge(y_st[i], 16 * TT // 2)

        @block.gpsimd
        def _(pool):
            pool.memset(zero[:, :], 0.0).then_inc(zeroed, 1)
            pool.memset(ones[:, :], 1.0).then_inc(ones_ready, 1)
            pool.memset(tri[:, :], 1.0).then_inc(made, 1)
            pool.memset(low[:, :, :], 1.0).then_inc(made, 1)
            pool.iota(iota_i[:, :], [[1, P]], base=0, channel_multiplier=0).then_inc(consts, 1)
            pool.iota(col_i[:, :], [[0, 1]], base=0, channel_multiplier=1).then_inc(consts, 1)
            pool.wait_ge(made, 2)
            pool.affine_select(out=tri[:, :], in_=tri[:, :], compare_op=ALU.is_gt, fill=0.0, base=0,
                               pattern=[[1, P]], channel_multiplier=-1).then_inc(tri_ready, 1)
            pool.affine_select(out=low[:, :, :], in_=low[:, :, :], compare_op=ALU.is_gt, fill=0.0, base=0,
                               pattern=[[1, NG], [-1, NG]], channel_multiplier=0).then_inc(consts, 1)
            for t in range(TT):
                pool.wait_ge(sil_done, 2 * t + 2)
                if t >= 2:
                    pool.wait_ge(h_tr, t - 1)
                pool.tensor_tensor(hid[:, t % 2, :], sil[:, t % 2, :], up[:, t % 2, :], ALU.mult).then_inc(hid_ready, 1)

        @block.tensor
        def _(pe):
            pe.wait_ge(got_r, 16)
            for t in range(TT):
                for k in range(KD):
                    mm = pe.matmul(p_l[:, t, :], fT[:, k, t * P:(t + 1) * P], wr[:, k, :], start=k == 0, stop=k == KD - 1)
            mm.then_inc(logits, 1)
            pe.wait_ge(got_w, 48)

            def gate_up(t):
                if t >= 1:
                    pe.wait_ge(sil_done, 2 * t)
                for k in range(KD):
                    pe.matmul(p_g[:, 0:FF], fT[:, k, t * P:(t + 1) * P], wg[:, k, :], start=k == 0, stop=k == KD - 1)
                for k in range(KD):
                    mm = pe.matmul(p_u[:, 0:FF], fT[:, k, t * P:(t + 1) * P], wu[:, k, :], start=k == 0, stop=k == KD - 1)
                mm.then_inc(gu_done, 1)

            def turn(t):
                pe.wait_ge(hid_ready, t + 1)
                if t >= 1:
                    pe.wait_ge(h_out, t)
                for j in range(2):
                    tr = pe.transpose(p_h[:, j * P:(j + 1) * P], hid[:, t % 2, j * P:(j + 1) * P], ident[:, :])
                tr.then_inc(h_tr, 1)

            def down(t):
                pe.wait_ge(h_out, t + 1)
                for n in range(2):
                    if t >= 1:
                        pe.wait_ge(y_ready, 2 * (t - 1) + n + 1)
                    for j in range(2):
                        mm = pe.matmul(p_d[n][:, :], hidT[:, t % 2, j, :], wd[:, j, n * NCH:(n + 1) * NCH], start=j == 0, stop=j == 1)
                    mm.then_inc(d_done, 1)

            def positions():
                pe.wait_ge(ones_ready, 1)
                pe.wait_ge(tri_ready, 1)
                pe.wait_ge(masked, 1)
                for t in range(TT):
                    mm = pe.matmul(p_misc[:, 0:NE], ones[:, :], M[:, t, :], start=t == 0, stop=t == TT - 1)
                mm.then_inc(counted, 1)
                for t in range(TT):
                    for s in range(t):
                        pe.matmul(p_pos[:, t, :], ones[:, :], M[:, s, :], start=s == 0, stop=False)
                    mm = pe.matmul(p_pos[:, t, :], tri[:, :], M[:, t, :], start=t == 0, stop=True)
                mm.then_inc(placed, 1)

            for t in range(TT):
                gate_up(t)
                if t >= 1:
                    down(t - 1)
                turn(t)
                if t == 3:
                    positions()
            down(TT - 1)
            for j in range(TT * TOPK):
                pe.wait_ge(hot_ready, 3 * (j + 1))
                mm = pe.matmul(p_l[:, 0:4, :].rearrange("p a e -> p (a e)"), hot_r[:, j % 4, :], hot_q[:, j % 4, :, :].rearrange("p a b -> p (a b)"),
                               start=j == 0, stop=j == TT * TOPK - 1)
                mm.then_inc(hot_mm, 1)
            pe.wait_ge(eb_ready, 1)
            pe.matmul(p_pos[0:1, 0:2, :].rearrange("p a e -> p (a e)"), ebc[:, 0:1], ident[:, :], start=True, stop=True).then_inc(eb_mm, 1)

        @block.scalar
        def _(act):
            act.wait_ge(logits, 1)
            act.activation(sc[:, :, :], p_l[:, :, :], ACT.Sigmoid).then_inc(scored, 1)
            for t in range(TT + 1):
                if t < TT:
                    act.wait_ge(gu_done, t + 1)
                    if t >= 2:
                        act.wait_ge(hid_ready, t - 1)
                    act.activation(sil[:, t % 2, :], p_g[:, 0:FF], ACT.Silu).then_inc(sil_done, 1)
                    act.activation(up[:, t % 2, :], p_u[:, 0:FF], ACT.Copy).then_inc(sil_done, 1)
                if t >= 1:
                    for n in range(2):
                        act.wait_ge(d_done, 2 * (t - 1) + n + 1)
                        if t >= 3 and n == 0:
                            act.wait_ge(y_st[(t - 1) % 2], 16 * ((t - 1) // 2))
                        act.activation(yo[:, (t - 1) % 2, n * NCH:(n + 1) * NCH], p_d[n][:, :], ACT.Copy).then_inc(y_ready, 1)
                if t < TT:
                    act.wait_ge(h_tr, t + 1)
                    act.activation(hidT[:, t % 2, :, :], p_h[:, 0:2 * P].rearrange("p (j c) -> p j c", j=2), ACT.Copy).then_inc(h_out, 1)

        @block.vector
        def _(dve):
            link = Chain(dve, step)
            dve.wait_ge(consts, 3)
            link(dve.tensor_copy(iota_f[:, :], iota_i[:, :]))
            link(dve.tensor_copy(col[:, :], col_i[:, :]))
            for t in range(TT):
                link(dve.tensor_scalar(tok[:, t:t + 1], col[:, :], float(t * P + 1), None, ALU.add))
                link(dve.memset(thr[:, :, t], float(t * P)))
            dve.wait_ge(got_b, 16)
            dve.wait_ge(scored, 1)
            link(dve.tensor_tensor(sel[:, :, :], sc[:, :, :], rb[:, None, :].to_broadcast([P, TT, NE]), ALU.add))
            g64 = lambda t: t[:, :, :].rearrange("p t (g e) -> p (t g) e", e=EG)
            col64 = lambda i: gm[:, i, :, :].rearrange("p t g -> p (t g)")
            bc64 = lambda i: col64(i)[:, :, None].to_broadcast([P, TT * NG, EG])
            link(dve.tensor_reduce(col64(0), g64(sel), AX.X, ALU.max))
            link(dve.tensor_tensor(g64(t1), g64(sel), bc64(0), ALU.is_equal))
            link(dve.tensor_reduce(col64(1), g64(t1), AX.X, ALU.add))
            link(dve.scalar_tensor_tensor(t2[:, :, :], t1[:, :, :], NEG, sel[:, :, :], ALU.mult, ALU.add))
            link(dve.tensor_reduce(col64(2), g64(t2), AX.X, ALU.max))
            link(dve.tensor_scalar(col64(3), col64(1), 1.5, -2 * NEG, ALU.is_gt, ALU.mult))
            link(dve.tensor_scalar(col64(3), col64(3), NEG, None, ALU.add))
            link(dve.tensor_tensor(col64(2), col64(2), col64(3), ALU.max))
            link(dve.tensor_tensor(col64(2), col64(2), col64(0), ALU.min))
            link(dve.tensor_tensor(col64(4), col64(0), col64(2), ALU.add))
            other = gm[:, 4, :, None, :].to_broadcast([P, TT, NG, NG])
            own = gm[:, 4, :, :, None].to_broadcast([P, TT, NG, NG])
            sq = lambda t: t[:, :, :].rearrange("p t (g e) -> p t g e", e=NG)
            link(dve.tensor_tensor(sq(t1), other, own, ALU.is_gt))
            link(dve.tensor_tensor(sq(t2), other, own, ALU.is_equal))
            link(dve.tensor_tensor(sq(t2), sq(t2), low[:, None, :, :].to_broadcast([P, TT, NG, NG]), ALU.mult))
            link(dve.tensor_tensor(t1[:, :, :], t1[:, :, :], t2[:, :, :], ALU.add))
            link(dve.tensor_reduce(col64(5), g64(t1), AX.X, ALU.add))
            link(dve.tensor_scalar(col64(6), col64(5), TOPG - 0.5, None, ALU.is_lt))
            link(dve.tensor_scalar(col64(7), col64(6), 1.0, -NEG, ALU.subtract, ALU.mult))
            link(dve.tensor_tensor(g64(ms), g64(sel), bc64(6), ALU.mult))
            link(dve.tensor_tensor(g64(ms), g64(ms), bc64(7), ALU.add))
            for t in range(TT):
                dve.max(top[:, t, :], ms[:, t, :]).then_inc(step, 1)
            link.n += TT
            dve.wait_ge(step, link.n)
            for t in range(TT):
                dve.match_replace(mr[:, t, :], top[:, t, :], ms[:, t, :], -3e38).then_inc(step, 1)
            link.n += TT
            dve.wait_ge(step, link.n)
            link(dve.tensor_tensor(M[:, :, :], mr[:, :, :], ms[:, :, :], ALU.not_equal))
            dve.sem_inc(masked, 1)
            link(dve.tensor_tensor(t1[:, :, :], M[:, :, :], sc[:, :, :], ALU.mult))
            link(dve.tensor_reduce(den[:, :], t1[:, :, :], AX.X, ALU.add))
            link(dve.reciprocal(rden[:, :], den[:, :]))
            link(dve.scalar_tensor_tensor(gate[:, :, :], t1[:, :, :], SCALE, rden[:, :, None].to_broadcast([P, TT, NE]), ALU.mult, ALU.mult))
            dve.wait_ge(counted, 1)
            link(dve.tensor_copy(nbk[:, 0, :], p_misc[:, 0:NE]))
            th = t2[:, :, :].rearrange("p t e -> p (t e)").rearrange("p (e j) -> p e j", j=KD)
            link(dve.tensor_tensor(th, nbk[:, 0, :, None].to_broadcast([P, NE, KD]), thr[:, :, :], ALU.is_gt))
            link(dve.tensor_reduce(nbk[:, 1, :], th, AX.X, ALU.add))
            link(dve.tensor_tensor_scan(nbk[:, 2, :], ones[:, 0:NE], nbk[:, 1, :], 0.0, ALU.mult, ALU.add))
            link(dve.tensor_tensor(nbk[:, 3, :], nbk[:, 2, :], nbk[:, 1, :], ALU.subtract))
            link(dve.tensor_scalar(nbk[:, 3, :], nbk[:, 3, :], float(P), None, ALU.mult))
            link(dve.tensor_scalar(t1[:, 0, :], nbk[:, 2, :], col[:, 0:1], None, ALU.is_le))
            link(dve.tensor_reduce(ebc[:, 1:2], t1[:, 0, :], AX.X, ALU.add))
            link(dve.tensor_scalar(ebc[:, 0:1], ebc[:, 1:2], float(NE - 1), None, ALU.min))
            dve.sem_inc(eb_ready, 1)
            link(dve.tensor_copy(meta[0:1, 1:2], nbk[0:1, 2, NE - 1:NE]))
            link(dve.tensor_scalar(meta[0:1, 0:1], meta[0:1, 1:2], 1, None, ALU.logical_shift_right))
            dve.wait_ge(placed, 1)
            link(dve.tensor_tensor(slot[:, :, :], p_pos[:, :, :], nbk[:, 3, None, :].to_broadcast([P, TT, NE]), ALU.add))
            link(dve.scalar_tensor_tensor(slot[:, :, :], slot[:, :, :], 1.0, M[:, :, :], ALU.add, ALU.mult))
            for t in range(TT):
                dve.max(s8[:, t, :], slot[:, t, :]).then_inc(step, 1)
            link.n += TT
            dve.wait_ge(step, link.n)
            for t in range(TT):
                sh = [P, TOPK, NE]
                link(dve.tensor_tensor(t1[:, :, :], slot[:, t, None, :].to_broadcast(sh), s8[:, t, :, None].to_broadcast(sh), ALU.is_equal))
                link(dve.tensor_tensor(t1[:, :, :], t1[:, :, :], gate[:, t, None, :].to_broadcast(sh), ALU.mult))
                link(dve.tensor_reduce(w8[:, t, :], t1[:, :, :], AX.X, ALU.add))
            link(dve.tensor_scalar(s8[:, :, :], s8[:, :, :], 1.0, None, ALU.subtract))
            link(dve.tensor_copy(s8i[:, :, :], s8[:, :, :]))
            link(dve.tensor_scalar(q8i[:, :, :], s8i[:, :, :], 7, None, ALU.logical_shift_right))
            link(dve.tensor_scalar(r8i[:, :, :], s8i[:, :, :], P - 1, None, ALU.bitwise_and))
            link(dve.tensor_copy(q8[:, :, :], q8i[:, :, :]))
            link(dve.tensor_copy(r8[:, :, :], r8i[:, :, :]))
            for j in range(TT * TOPK):
                t, k = j // TOPK, j % TOPK
                if j >= 4:
                    dve.wait_ge(hot_mm, j - 3)
                dve.tensor_scalar(hot_r[:, j % 4, :], iota_f[:, :], r8[:, t, k:k + 1], None, ALU.is_equal).then_inc(hot_ready, 1)
                dve.tensor_scalar(hot_q[:, j % 4, 0, :], iota_f[:, :], q8[:, t, k:k + 1], tok[:, t:t + 1], ALU.is_equal, ALU.mult).then_inc(hot_ready, 1)
                dve.tensor_scalar(hot_q[:, j % 4, 1, :], iota_f[:, :], q8[:, t, k:k + 1], w8[:, t, k:k + 1], ALU.is_equal, ALU.mult).then_inc(hot_ready, 1)
            dve.wait_ge(hot_mm, TT * TOPK)
            tab = p_l[:, 0:4, :].rearrange("p a e -> p (a e)")
            link(dve.tensor_copy(wslot[:, 0:P], tab[:, P:2 * P]))
            link(dve.tensor_copy(tabf[:, 0, :], tab[:, 0:P]))
            link(dve.memset(wslot[:, P:NIDX], 0.0))
            link(dve.tensor_scalar(col[:, :], col[:, :], float(SEQ + 1), None, ALU.add))
            link(dve.tensor_scalar(tabf[:, 1, :], tabf[:, 0, :], 0.5, col[:, 0:1], ALU.is_lt, ALU.mult))
            link(dve.scalar_tensor_tensor(tabf[:, 0, :], tabf[:, 0, :], 1.0, tabf[:, 1, :], ALU.subtract, ALU.add))
            link(dve.tensor_copy(idx[:, 0:P], tabf[:, 0, :]))
            link(dve.tensor_scalar(tabf[:, 1, 0:1], col[:, :], 1.0, None, ALU.subtract))
            for j in range(P, NIDX):
                link(dve.tensor_copy(idx[:, j:j + 1], tabf[:, 1, 0:1]))
            dve.wait_ge(eb_mm, 1)
            link(dve.tensor_copy(eb[0:1, :], p_pos[0:1, 0:2, :].rearrange("p a e -> p (a e)")))


def experts(nc, tag, ident, w_gate, w_up, w_down, f_dram, acc_dram, idx, wslot, meta, eb):
    with Phase(nc, tag) as ph:
        wg, wu, wd = (ph.sb(s, [P, 2, KD, FF]) for s in ("wg", "wu", "wd"))
        wdv = wd[:, :, :, :].rearrange("p u (j a) f -> p u j (a f)", j=2)
        xg = ph.sb("xg", [P, 2, D])
        xT = ph.sb("xT", [P, 2, KD, P])
        sil, hid, hidT = ph.sb("sil", [P, 2, FF]), ph.sb("hid", [P, 2, FF]), ph.sb("hidT", [P, 2, 2, P])
        yo = ph.sb("yo", [P, 2, D])
        ig = [ph.sb(f"ig{u}", [P, 1], U32) for u in range(2)]
        iss = [ph.sb(f"is{u}", [P, 1], U32) for u in range(2)]
        p_x = [ph.ps(f"p_x{i}", [P, 4, P]) for i in range(2)]
        p_g, p_u, p_h = ph.ps("p_g", [P, NCH]), ph.ps("p_u", [P, NCH]), ph.ps("p_h", [P, NCH])
        p_d = [ph.ps(f"p_d{i}", [P, NCH]) for i in range(2)]
        g_in, u_in, d_in = ([ph.sem(f"{s}_in{u}") for u in range(2)] for s in "gud")
        x_in = [ph.sem(f"x_in{u}") for u in range(2)]
        x_tr, xc_act, xc_dve = ph.sem("x_tr"), ph.sem("xc_act"), ph.sem("xc_dve")
        g_mm, u_mm, sil_done, hid_done, h_tr, h_out = (ph.sem(s) for s in ("g_mm", "u_mm", "sil_done", "hid_done", "h_tr", "h_out"))
        d_mm, y_act, y_dve = ph.sem("d_mm"), ph.sem("y_act"), ph.sem("y_dve")
        scat = [ph.sem(f"scat{u}") for u in range(2)]
        tick, copied = ph.sem("tick"), ph.sem("copied")
        block = ph.block()

        @block.sync
        def _(sp):
            def load(n, m, u, first=False):
                e = sp.value_load(eb[0:1, n:n + 1] if isinstance(n, int) else eb[0:1, bass.ds(n, 1)], min_val=0, max_val=NE - 1)
                for buf, w, k, got, used in ((wg, w_gate, KD, g_in, g_mm), (wu, w_up, KD, u_in, u_mm)):
                    if not first:
                        sp.wait_ge(used, n - 1)
                    sp.dma_start(buf[:, u, :, :], w[bass.ds(e, 1), :, :].rearrange("a (p k) f -> p (a k) f", k=k)).then_inc(got[u], 16)
                if not first:
                    sp.wait_ge(d_mm, n - 1)
                sp.dma_start(wdv[:, u, :, :], w_down[bass.ds(e, 1), :, :].rearrange("a (j p) n -> p (a j) n", p=P)).then_inc(d_in[u], 16)

            pairs = sp.value_load(meta[0:1, 0:1], min_val=2, max_val=P // 2 - 1)
            load(0, 0, 0, True)
            load(1, 0, 1, True)
            load(2, 1, 0)
            with sp.Fori(1, pairs) as i:
                load(i * 2 + 1, i, 1)
                load(i * 2 + 2, i + 1, 0)

        @block.gpsimd
        def _(pool):
            pairs = pool.value_load(meta[0:1, 0:1], min_val=2, max_val=P // 2 - 1)

            def gather(n, u, tr):
                if tr is not None:
                    pool.wait_ge(x_tr, tr)
                pool.sem_inc(tick, 1)
                c = idx[:, n:n + 1] if isinstance(n, int) else idx[:, bass.ds(n, 1)]
                pool.tensor_copy(ig[u][:, :], c).then_inc(copied, 1)

            def gather_go(u, count):
                pool.wait_ge(copied, count)
                pool.sem_inc(tick, 1)
                pool.indirect_dma_start(xg[:, u, :], None, f_dram, bass.IndirectOffsetOnAxis(ap=ig[u][:, :], axis=0)).then_inc(x_in[u], 16)

            def scatter(n, u, count, before):
                c = idx[:, n:n + 1] if isinstance(n, int) else idx[:, bass.ds(n, 1)]
                if before is not None:
                    pool.wait_ge(scat[before[0]], before[1])
                    pool.sem_inc(tick, 1)
                pool.tensor_copy(iss[u][:, :], c).then_inc(copied, 1)
                pool.wait_ge(copied, count)
                pool.wait_ge(y_act, n + 1)
                pool.sem_inc(tick, 1)
                pool.wait_ge(y_dve, n + 1)
                pool.sem_inc(tick, 1)
                pool.indirect_dma_start(acc_dram, bass.IndirectOffsetOnAxis(ap=iss[u][:, :], axis=0), yo[:, u, :], None,
                                        compute_op=ALU.add).then_inc(scat[u], 16)

            gather(0, 0, None)
            gather_go(0, 1)
            gather(1, 1, None)
            gather_go(1, 2)
            gather(2, 0, 1)
            gather_go(0, 3)
            gather(3, 1, 2)
            gather_go(1, 4)
            scatter(0, 0, 5, None)
            gather(4, 0, 3)
            gather_go(0, 6)
            scatter(1, 1, 7, (0, 16))
            with pool.Fori(1, pairs) as i:
                n = i * 2 + 1
                gather(n + 2, 1, n + 1)
                gather_go(1, i * 4 + 4)
                scatter(n - 1, 0, i * 4 + 5, (1, i * 16))
                gather(n + 3, 0, n + 2)
                gather_go(0, i * 4 + 6)
                scatter(n, 1, i * 4 + 7, (0, i * 16 + 16))
            last = pool.snap(pairs * 2)
            scatter(last, 0, pairs * 4 + 4, (1, pairs * 16))
            pool.wait_ge(scat[0], pairs * 16 + 16)
            pool.wait_ge(x_in[0], pairs * 16 + 32)
            pool.sem_inc(tick, 1)

        @block.tensor
        def _(pe):
            pairs = pe.value_load(meta[0:1, 0:1], min_val=2, max_val=P // 2 - 1)

            def turn_x(n, u, m):
                pe.wait_ge(x_in[u], m * 16 + 16)
                if not isinstance(n, int) or n > 0:
                    pe.wait_ge(xc_act, n)
                    pe.wait_ge(xc_dve, n)
                for k in range(KD):
                    tr = pe.transpose(p_x[k // 4][:, k % 4, :], xg[:, u, k * P:(k + 1) * P], ident[:, :])
                tr.then_inc(x_tr, 1)

            def gate_up(n, u, m):
                pe.wait_ge(xc_act, n + 1)
                pe.wait_ge(xc_dve, n + 1)
                pe.wait_ge(g_in[u], m * 16 + 16)
                if not isinstance(n, int) or n > 0:
                    pe.wait_ge(sil_done, n)
                for k in range(KD):
                    mm = pe.matmul(p_g[:, 0:FF], xT[:, u, k, :], wg[:, u, k, :], start=k == 0, stop=k == KD - 1)
                mm.then_inc(g_mm, 1)
                pe.wait_ge(u_in[u], m * 16 + 16)
                if not isinstance(n, int) or n > 0:
                    pe.wait_ge(hid_done, n)
                for k in range(KD):
                    mm = pe.matmul(p_u[:, 0:FF], xT[:, u, k, :], wu[:, u, k, :], start=k == 0, stop=k == KD - 1)
                mm.then_inc(u_mm, 1)

            def turn_h(n, u):
                pe.wait_ge(hid_done, n + 1)
                for j in range(2):
                    tr = pe.transpose(p_h[:, j * P:(j + 1) * P], hid[:, u, j * P:(j + 1) * P], ident[:, :])
                tr.then_inc(h_tr, 1)

            def down(n, u, m):
                pe.wait_ge(h_out, n + 1)
                pe.wait_ge(d_in[u], m * 16 + 16)
                for c in range(2):
                    if not isinstance(n, int) or n > 0:
                        pe.wait_ge((y_act, y_dve)[c], n)
                    for j in range(2):
                        mm = pe.matmul(p_d[c][:, :], hidT[:, u, j, :], wdv[:, u, j, c * NCH:(c + 1) * NCH], start=j == 0, stop=j == 1)
                mm.then_inc(d_mm, 1)

            turn_x(0, 0, 0)
            gate_up(0, 0, 0)
            turn_x(1, 1, 0)
            turn_h(0, 0)

            def pair(i):
                n = i * 2 + 1
                gate_up(n, 1, i)
                turn_x(n + 1, 0, i + 1)
                down(n - 1, 0, i)
                turn_h(n, 1)
                gate_up(n + 1, 0, i + 1)
                turn_x(n + 2, 1, i + 1)
                down(n, 1, i)
                turn_h(n + 1, 0)

            pair(0)
            with pe.Fori(1, pairs) as i:
                pair(i)
            last = pe.snap(pairs * 2)
            down(last, 0, pairs)

        @block.scalar
        def _(act):
            pairs = act.value_load(meta[0:1, 0:1], min_val=2, max_val=P // 2 - 1)

            def copy_x(n, u):
                act.wait_ge(x_tr, n + 1)
                if not isinstance(n, int) or n > 1:
                    act.wait_ge(u_mm, n - 1)
                act.activation(xT[:, u, 0:4, :], p_x[0][:, :, :], ACT.Copy).then_inc(xc_act, 1)

            def silu(n, u):
                act.wait_ge(g_mm, n + 1)
                if not isinstance(n, int) or n > 1:
                    act.wait_ge(hid_done, n - 1)
                act.activation(sil[:, u, :], p_g[:, 0:FF], ACT.Silu).then_inc(sil_done, 1)

            def copy_h(n, u):
                act.wait_ge(h_tr, n + 1)
                if not isinstance(n, int) or n > 1:
                    act.wait_ge(d_mm, n - 1)
                act.activation(hidT[:, u, :, :], p_h[:, 0:2 * P].rearrange("p (j c) -> p j c", j=2), ACT.Copy).then_inc(h_out, 1)

            def out(n, u, m):
                act.wait_ge(d_mm, n + 1)
                if not isinstance(n, int) or n > 1:
                    act.wait_ge(scat[u], m * 16)
                act.activation(yo[:, u, 0:NCH], p_d[0][:, :], ACT.Copy).then_inc(y_act, 1)

            copy_x(0, 0)
            silu(0, 0)
            copy_x(1, 1)
            copy_h(0, 0)

            def pair(i):
                n = i * 2 + 1
                silu(n, 1)
                copy_x(n + 1, 0)
                out(n - 1, 0, i)
                copy_h(n, 1)
                silu(n + 1, 0)
                copy_x(n + 2, 1)
                out(n, 1, i)
                copy_h(n + 1, 0)

            pair(0)
            with act.Fori(1, pairs) as i:
                pair(i)
            last = act.snap(pairs * 2)
            out(last, 0, pairs)

        @block.vector
        def _(dve):
            pairs = dve.value_load(meta[0:1, 0:1], min_val=2, max_val=P // 2 - 1)

            def copy_x(n, u):
                dve.wait_ge(x_tr, n + 1)
                if not isinstance(n, int) or n > 1:
                    dve.wait_ge(u_mm, n - 1)
                dve.tensor_copy(xT[:, u, 4:KD, :], p_x[1][:, :, :]).then_inc(xc_dve, 1)

            def hidden(n, u):
                dve.wait_ge(sil_done, n + 1)
                dve.wait_ge(u_mm, n + 1)
                if not isinstance(n, int) or n > 1:
                    dve.wait_ge(h_tr, n - 1)
                ws = wslot[:, n:n + 1] if isinstance(n, int) else wslot[:, bass.ds(n, 1)]
                dve.scalar_tensor_tensor(hid[:, u, :], sil[:, u, :], ws, p_u[:, 0:FF], ALU.mult, ALU.mult).then_inc(hid_done, 1)

            def out(n, u, m):
                dve.wait_ge(d_mm, n + 1)
                if not isinstance(n, int) or n > 1:
                    dve.wait_ge(scat[u], m * 16)
                dve.tensor_copy(yo[:, u, NCH:D], p_d[1][:, :]).then_inc(y_dve, 1)

            copy_x(0, 0)
            hidden(0, 0)
            copy_x(1, 1)

            def pair(i):
                n = i * 2 + 1
                hidden(n, 1)
                copy_x(n + 1, 0)
                out(n - 1, 0, i)
                hidden(n + 1, 0)
                copy_x(n + 2, 1)
                out(n, 1, i)

            pair(0)
            with dve.Fori(1, pairs) as i:
                pair(i)
            last = dve.snap(pairs * 2)
            out(last, 0, pairs)

FG = 4
FW = D // FG


def add_gated(nc, tag, acc_dram, gate, h, out=None):
    with Phase(nc, tag) as ph:
        a = ph.sb("a", [P, TT, D])
        a_in = [ph.sem(f"a_in{t}") for t in range(TT)]
        gated, added, stored = ph.sem("gated"), ph.sem("added"), ph.sem("stored")
        block = ph.block()

        @block.sync
        def _(sp):
            for t in range(TT):
                sp.dma_start(a[:, t, :], acc_dram[t * P:(t + 1) * P, :]).then_inc(a_in[t], 16)
            if out is not None:
                for t in range(TT):
                    sp.wait_ge(added, t + 1)
                    sp.dma_start(out[t * P:(t + 1) * P, :], h[:, t, :]).then_inc(stored, 16)
                sp.wait_ge(stored, 16 * TT)

        @block.vector
        def _(dve):
            for t in range(TT):
                dve.wait_ge(a_in[t], 16)
                dve.tensor_tensor(a[:, t, :], a[:, t, :], gate, ALU.mult).then_inc(gated, 1)
                dve.wait_ge(gated, t + 1)
                dve.tensor_tensor(h[:, t, :], h[:, t, :], a[:, t, :], ALU.add).then_inc(added, 1)
            dve.wait_ge(added, TT)


def fourier(nc, tag, aT, cs_feat, cos_tok, sin_tok, fT):
    with Phase(nc, tag) as ph:
        cf = ph.sb("cf", [P, 2, 2 * FW])
        y = ph.sb("y", [P, TT, 2, D])
        ct = ph.sb("ct", [P, TT, NCH])
        st = ph.sb("st", [P, TT, NCH])
        pz = [ph.ps(f"pz{i}", [P, NCH]) for i in range(4)]
        c_in, t_in = ph.sem("c_in"), ph.sem("t_in")
        mm_done = ph.sem("mm_done")
        copied = [ph.sem(f"copied{i}") for i in range(2)]
        jobs1 = [(t, g) for t in range(TT) for g in range(FG)]
        jobs2 = [(n, f) for n in range(2) for f in range(KD)]
        NJ = len(jobs1)
        block = ph.block()

        @block.sync
        def _(sp):
            sp.dma_start(cf[:, :, :], cs_feat).then_inc(c_in, 16)
            for n in range(2):
                if n == 1:
                    sp.wait_ge(mm_done, NJ + KD)
                for buf, src in ((ct, cos_tok), (st, sin_tok)):
                    sp.dma_start(buf[:, :, :], src.rearrange("(k p) n -> p k n", p=P)[:, :, n * NCH:(n + 1) * NCH]).then_inc(t_in, 16)

        @block.tensor
        def _(pe):
            pe.wait_ge(c_in, 16)
            for j, (t, g) in enumerate(jobs1):
                if j >= 4:
                    pe.wait_ge(copied[j % 2], (j - 4) // 2 + 1)
                for k in range(2):
                    mm = pe.matmul(pz[j % 4][:, :], aT[:, 2 * g + k, t * P:(t + 1) * P], cf[:, k, :], start=k == 0, stop=k == 1)
                mm.then_inc(mm_done, 1)
            for i in range(2):
                pe.wait_ge(copied[i], NJ // 2)
            for m, (n, f) in enumerate(jobs2):
                j = NJ + m
                pe.wait_ge(copied[j % 2], (j - 4) // 2 + 1)
                pe.wait_ge(t_in, 32 * (n + 1))
                for k in range(TT):
                    pe.matmul(pz[j % 4][:, :], y[:, k, 0, f * P:(f + 1) * P], ct[:, k, :], start=k == 0, stop=False)
                    mm = pe.matmul(pz[j % 4][:, :], y[:, k, 1, f * P:(f + 1) * P], st[:, k, :], start=False, stop=k == TT - 1)
                mm.then_inc(mm_done, 1)

        def evacuate(eng, copy, i):
            for j in range(i, NJ + len(jobs2), 2):
                eng.wait_ge(mm_done, j + 1)
                if j < NJ:
                    t, g = jobs1[j]
                    dst = y[:, t, :, g * FW:(g + 1) * FW]
                    copy(dst, pz[j % 4][:, :].rearrange("p (s f) -> p s f", s=2)).then_inc(copied[i], 1)
                else:
                    n, f = jobs2[j - NJ]
                    copy(fT[:, f, n * NCH:(n + 1) * NCH], pz[j % 4][:, :]).then_inc(copied[i], 1)
            eng.wait_ge(copied[i], (NJ + len(jobs2)) // 2)

        @block.scalar
        def _(act):
            evacuate(act, lambda o, i: act.activation(o, i, ACT.Copy), 0)

        @block.vector
        def _(dve):
            evacuate(dve, lambda o, i: dve.tensor_copy(o, i), 1)
def program(nc, x, c, ctx, c_ctx, w_ada, b_ada, w_in, s5_lam_re, s5_lam_im, s5_log_dt, s5_b_re, s5_b_im,
            s5_c_re, s5_c_im, s5_d, s5_w_glu, s5_b_glu, na_q_gain, na_k_gain, na_rpb, w_mix_out,
            w_fourier_out, b_fourier_out, w_router, router_bias, w_exp_gate, w_exp_up, w_exp_down,
            w_sh_gate, w_sh_up, w_sh_down, cs_feat, cos_tok, sin_tok, out):
    def scratch(name, shape):
        return nc.dram_tensor(f"scratch_{name}", shape, F32, kind="Internal").ap()

    mats, rot, k_lags = scratch("mats", (P, 5, G5, P)), scratch("rot", (P, 2, G5, NCK)), scratch("lags", (W5, TAUS * C5))
    mix_dram = scratch("mix", (D, SEQ))
    u_dram, y_dram = scratch("u", (W5, TOK)), scratch("y", (W5, SEQ))
    pad = scratch("pad", (HEADS * RPB_R, 2 * GRID_W - 1))
    f_dram, acc_dram = scratch("f", (SEQ + PAD_ROWS, D)), scratch("acc", (SEQ + PAD_ROWS, D))
    xr = x[0]
    rows = lambda t, n: [t[i * P:(i + 1) * P, :] for i in range(n)]

    def moe(layer, mod, h, ident, last):
        tag = f"moe{layer}"
        with Phase(nc, tag) as ph:
            idx, wslot = ph.sb("idx", [P, NIDX], U32), ph.sb("wslot", [P, NIDX])
            meta, eb = ph.sb("meta", [1, 2], I32), ph.sb("eb", [1, P], I32)
            with Phase(nc, tag + "in") as ph2:
                fT = ph2.sb("fT", [P, KD, SEQ])
                tiles = [(h[:, t, :], (mod[:, 3 * D:4 * D], mod[:, 4 * D:5 * D]), False) for t in range(TT)]
                norm_modulate_transpose(nc, tag + "norm", ident, tiles, fT, True, store=rows(f_dram, TT))
                route_and_share(nc, tag + "route", ident, fT, w_router[layer], router_bias[layer], w_sh_gate[layer],
                                w_sh_up[layer], w_sh_down[layer], f_dram, acc_dram, idx, wslot, meta, eb)
            experts(nc, tag + "exp", ident, w_exp_gate[layer], w_exp_up[layer], w_exp_down[layer], f_dram, acc_dram,
                    idx, wslot, meta, eb)
        add_gated(nc, tag + "add", acc_dram, mod[:, 5 * D:6 * D], h, out[0] if last else None)

    with Phase(nc, "main") as main:
        ident = main.sb("ident", [P, P])
        decay = main.sb("decay", [P, G5])
        make_identity(nc, ident)
        s5_matrices(nc, ident, s5_lam_re[0], s5_lam_im[0], s5_log_dt[0], s5_b_re[0], s5_b_im[0], s5_c_re[0],
                    s5_c_im[0], s5_d[0], mats, k_lags, rot, decay)
        mod = main.sb("mod", [P, ADA])
        with Phase(nc, "attn") as at:
            qT, kT = at.sb("qT", [P, HP, SEQ]), at.sb("kT", [P, HP, TOK])
            v_even, v_odd, v_ctx = at.sb("v_even", [P, TT, NCH]), at.sb("v_odd", [P, TT - 1, NCH]), at.sb("v_ctx", [P, CT, NCH])
            with Phase(nc, "pre") as pre:
                aT = pre.sb("aT", [P, KD, TOK])
                with Phase(nc, "cond") as cond:
                    mod_ctx = cond.sb("mod_ctx", [P, 2 * D])
                    conditioning(nc, "ada0", c.rearrange("a (p k) -> p (a k)", k=KD), w_ada[0], b_ada[0], mod,
                                 c_ctx.rearrange("(p k) -> p k", k=KD), mod_ctx)
                    norm_modulate_transpose(nc, "norm_ctx", ident,
                                            [(r, (mod_ctx[:, 0:D], mod_ctx[:, D:2 * D]), True) for r in rows(ctx[0], CT)],
                                            aT[:, :, 0:CTX], True)
                for part in range(2):
                    n = TT // 2
                    norm_modulate_transpose(nc, f"norm_x{part}", ident,
                                            [(r, (mod[:, 0:D], mod[:, D:2 * D]), True) for r in rows(xr, TT)[n * part:n * part + n]],
                                            aT[:, :, CTX + part * n * P:CTX + (part + 1) * n * P], True)
                project(nc, ident, aT, w_in[0], na_q_gain[0], na_k_gain[0], u_dram, qT, kT, v_even, v_odd, v_ctx)
            bt = at.sb("bt", [P, HP, RPB_R, GRID_W])
            bias_table(nc, na_rpb[0], pad, bt)
            attention(nc, ident, qT, kT, v_even, v_odd, v_ctx, bt, mix_dram[W5:, :])
        s5_scan_readout(nc, ident, u_dram, mats, rot, decay, y_dram, s5_w_glu[0], s5_b_glu[0], mix_dram[0:W5, :])
        h = main.sb("h", [P, TT, D])
        with Phase(nc, "mixed") as mx:
            residual(nc, "mix", mx.sb("mixT", [P, KD, SEQ]), w_mix_out[0], None, mod[:, 2 * D:3 * D], h, x=xr, src_dram=mix_dram)
        moe(0, mod, h, ident, False)

        conditioning(nc, "ada1", c.rearrange("a (p k) -> p (a k)", k=KD), w_ada[1], b_ada[1], mod)
        with Phase(nc, "four") as fo:
            aT = fo.sb("aT", [P, KD, SEQ])
            norm_modulate_transpose(nc, "norm_f", ident, [(h[:, t, :], (mod[:, 0:D], mod[:, D:2 * D]), False) for t in range(TT)], aT, False)
            fourier(nc, "fft", aT, cs_feat, cos_tok, sin_tok, aT)
            residual(nc, "fout", aT, w_fourier_out[0], b_fourier_out[0], mod[:, 2 * D:3 * D], h)
        moe(1, mod, h, ident, True)


INPUTS = ["x", "c", "ctx", "c_ctx", "w_ada", "b_ada", "w_in", "s5_lam_re", "s5_lam_im", "s5_log_dt", "s5_b_re", "s5_b_im",
          "s5_c_re", "s5_c_im", "s5_d", "s5_w_glu", "s5_b_glu", "na_q_gain", "na_k_gain", "na_rpb", "w_mix_out",
          "w_fourier_out", "b_fourier_out", "w_router", "router_bias", "w_exp_gate", "w_exp_up", "w_exp_down",
          "w_sh_gate", "w_sh_up", "w_sh_down"]


def transform_constants():
    import numpy as np

    i = np.arange(FW)
    a = 2 * np.pi * ((i[:, None] * i[None, :]) % FW) / FW
    feat = np.concatenate([np.cos(a), np.sin(a)], axis=1) / np.sqrt(SEQ * FW)
    t = np.arange(SEQ)
    b = 2 * np.pi * ((t[:, None] * t[None, :]) % SEQ) / SEQ
    return {
        "cs_feat": np.ascontiguousarray(feat.reshape(2, P, 2 * FW).transpose(1, 0, 2), dtype=np.float32),
        "cos_tok": np.cos(b).astype(np.float32),
        "sin_tok": (-np.sin(b)).astype(np.float32),
    }


def kernel(**inputs):
    import numpy as np
    import concourse.bacc as bacc
    from concourse.bass_utils import run_bass_kernel_spmd

    nc = bacc.Bacc("TRN2", target_bir_lowering=False, num_devices=1)
    arrays, args = {}, []
    for name, a in [(n, inputs[n]) for n in INPUTS] + list(transform_constants().items()):
        a = np.ascontiguousarray(a)
        arrays[f"in_{name}"] = a
        args.append(nc.dram_tensor(f"in_{name}", a.shape, mybir.dt.from_np(a.dtype), kind="ExternalInput").ap())
    out = nc.dram_tensor("out_h", (1, SEQ, D), F32, kind="ExternalOutput").ap()
    program(nc, *args, out)
    r = run_bass_kernel_spmd(nc, [arrays], core_ids=[0])
    return r.results[0]["out_h"]
```

```python
import math
from contextlib import ExitStack

import concourse.bass as bass
from concourse import mybir

F32 = mybir.dt.float32
I32 = mybir.dt.int32
U32 = mybir.dt.uint32
F32R = mybir.dt.float32r
ALU = mybir.AluOpType
ACT = mybir.ActivationFunctionType
AX = mybir.AxisListType

P = 128
D = 1024
KD = D // P
SEQ = 1024
CTX = 256
TOK = CTX + SEQ
TT = SEQ // P
CT = CTX // P
EPS = 1e-6
GRID_W = 64
ROWS = SEQ // GRID_W
NCH = 512
ADA = 6 * D
G5, C5, S5 = 32, 16, 64
W5 = G5 * C5
LCH = 8
NCK = TOK // LCH
NCC = CTX // LCH
NCL = SEQ // LCH
HEADS, HD = 8, 64
HP = HEADS // 2
KH, KW = 8, 16
RPB_R, RPB_C = 2 * KH - 1, 2 * KW - 1
NE, NG, EG = 64, 8, 8
TOPG, TOPK = 4, 8
FF = 256
NEG = -1e30


class Phase:

    def __init__(self, nc, name):
        self.nc, self.name, self.stack, self.sems = nc, name, ExitStack(), []

    def __enter__(self):
        self.stack.__enter__()
        return self

    def __exit__(self, *a):
        self.stack.__exit__(*a)
        if self.sems:
            self.nc.clear_and_free_semaphores(self.sems)
            self.nc.all_engine_barrier()

    def sb(self, name, shape, dt=F32):
        return self.stack.enter_context(self.nc.sbuf_tensor(f"{self.name}_{name}", shape, dt))

    def ps(self, name, shape, dt=F32):
        return self.stack.enter_context(self.nc.psum_tensor(f"{self.name}_{name}", shape, dt))

    def sem(self, name):
        self.sems.append(self.nc.alloc_semaphore(name=f"{self.name}_{name}"))
        return self.sems[-1]

    def block(self):
        return self.stack.enter_context(self.nc.Block())


class Chain:

    def __init__(self, eng, sem):
        self.eng, self.sem, self.n = eng, sem, 0

    def __call__(self, ins):
        self.n += 1
        ins.then_inc(self.sem, 1)
        self.eng.wait_ge(self.sem, self.n)


def make_identity(nc, ident):
    with Phase(nc, "ident") as ph:
        zero = ph.sem("zero")
        done = ph.sem("done")
        block = ph.block()

        @block.gpsimd
        def _(pool):
            pool.memset(ident[:, :], 0.0).then_inc(zero, 1)
            pool.wait_ge(zero, 1)
            pool.affine_select(out=ident[:, :], in_=ident[:, :], compare_op=ALU.not_equal, fill=1.0,
                               base=0, pattern=[[-1, P]], channel_multiplier=1).then_inc(done, 1)
            pool.wait_ge(done, 1)


def conditioning(nc, tag, c_col, w, b, mod, ctx_col=None, mod_ctx=None):
    HALF = KD // 2
    NB = ADA // NCH
    with Phase(nc, tag) as ph:
        col = ph.sb("col", [P, 2, KD])
        act = ph.sb("act", [P, 2, KD])
        ones = ph.sb("ones", [P, P])
        rep = ph.sb("rep", [P, 2, HALF, P])
        part = ph.sb("part", [P, 2, 2, NCH])
        wbuf = ph.sb("w", [P, 2, KD, NCH])
        pmod = [ph.ps(f"pmod{i}", [P, NCH]) for i in range(2)]
        pctx = [ph.ps(f"pctx{i}", [P, NCH]) for i in range(2)]
        col_in, bias_in = ph.sem("col_in"), ph.sem("bias_in")
        w_in = [ph.sem(f"w_in{i}") for i in range(2)]
        silu_done, ones_done, rep_done = ph.sem("silu_done"), ph.sem("ones_done"), ph.sem("rep_done")
        mod_mm, mod_out = ph.sem("mod_mm"), ph.sem("mod_out")
        ctx_mm, ctx_out = ph.sem("ctx_mm"), ph.sem("ctx_out")
        scaled = ph.sem("scaled")
        summed = [ph.sem("summed"), ph.sem("summed_ctx")]
        both = ctx_col is not None
        w_v = w.rearrange("(p k) n -> p k n", k=KD)
        SPLIT = 2 if both else 0
        block = ph.block()

        @block.sync
        def _(sp):
            sp.dma_start(col[:, 0, :], c_col).then_inc(col_in, 16)
            if both:
                sp.dma_start(col[:, 1, :], ctx_col).then_inc(col_in, 16)
            for u in range(2):
                sp.dma_start(wbuf[:, u, :, :], w_v[:, :, u * NCH:(u + 1) * NCH]).then_inc(w_in[u], 16)
            sp.dma_start(mod[:, :], b[None, :].to_broadcast([P, ADA])).then_inc(bias_in, 16)
            if both:
                sp.dma_start(mod_ctx[:, :], b[None, 0:2 * D].to_broadcast([P, 2 * D])).then_inc(bias_in, 16)
            with sp.Fori(1, NB // 2) as i:
                for u in range(2):
                    sp.wait_ge(mod_mm, i * 2 + (u - 1))
                    sp.dma_start(wbuf[:, u, :, :], w_v[:, :, bass.ds(i * (2 * NCH) + u * NCH, NCH)]).then_inc(w_in[u], 16)

        @block.scalar
        def _(act_e):
            act_e.wait_ge(col_in, 32 if both else 16)
            n = 2 if both else 1
            act_e.activation(act[:, 0:n, :], col[:, 0:n, :], ACT.Silu).then_inc(silu_done, 1)

        @block.tensor
        def _(pe):
            pe.wait_ge(rep_done, 2 * HALF if both else HALF)

            def products(bank, i, u, s, done):
                for k in range(HALF):
                    pe.matmul(bank, rep[:, s, k, :], wbuf[:, u, k, :], start=k == 0, stop=False)
                pe.wait_ge(summed[s], (i * 2 + u + 1) * HALF)
                pe.matmul(bank, ones[:, :], part[:, u, s, :], start=False, stop=True).then_inc(done, 1)

            def step(i, with_ctx):
                for u in range(2):
                    pe.wait_ge(w_in[u], i * 16 + 16)
                    if with_ctx:
                        pe.wait_ge(mod_out, i * 2 + u - 1) if not isinstance(i, int) or i * 2 + u - 1 > 0 else None
                        pe.wait_ge(ctx_out, i * 2 + u - 1) if not isinstance(i, int) or i * 2 + u - 1 > 0 else None
                        products(pctx[u][:, :], i, u, 1, ctx_mm)
                    elif not isinstance(i, int) or i > 0:
                        pe.wait_ge(mod_out, i * 2 + (u - 1))
                    products(pmod[u][:, :], i, u, 0, mod_mm)

            step(0, both)
            if both:
                step(1, True)
            with pe.Fori(SPLIT if both else 1, NB // 2) as i:
                step(i, False)

        @block.vector
        def _(dve):
            dve.memset(ones[:, :], 1.0).then_inc(ones_done, 1)
            dve.wait_ge(ones_done, 1)
            dve.wait_ge(silu_done, 1)
            for s in range(2 if both else 1):
                for k in range(HALF):
                    dve.tensor_scalar(rep[:, s, k, :], ones[:, :], act[:, s, k:k + 1], None, ALU.mult).then_inc(rep_done, 1)
            dve.wait_ge(bias_in, 32 if both else 16)

            def row_sums(i, u, s):
                for j in range(HALF):
                    k = HALF + j
                    if j == 0:
                        dve.tensor_scalar(part[:, u, s, :], wbuf[:, u, k, :], act[:, s, k:k + 1], None, ALU.mult).then_inc(summed[s], 1)
                    else:
                        dve.wait_ge(summed[s], (i * 2 + u) * HALF + j)
                        dve.scalar_tensor_tensor(part[:, u, s, :], wbuf[:, u, k, :], act[:, s, k:k + 1], part[:, u, s, :],
                                                 ALU.mult, ALU.add).then_inc(summed[s], 1)

            def step(i, with_ctx):
                for u in range(2):
                    dve.wait_ge(w_in[u], i * 16 + 16)
                    for s in ((1, 0) if with_ctx else (0,)):
                        row_sums(i, u, s)
                    if with_ctx:
                        dve.wait_ge(ctx_mm, i * 2 + u + 1)
                        m = mod_ctx[:, (2 * i + u) * NCH:(2 * i + u + 1) * NCH]
                        dve.tensor_tensor(m, pctx[u][:, :], m, ALU.add).then_inc(ctx_out, 1)
                    dve.wait_ge(mod_mm, i * 2 + u + 1)
                    m = mod[:, bass.ds(i * (2 * NCH) + u * NCH, NCH)]
                    dve.tensor_tensor(m, pmod[u][:, :], m, ALU.add).then_inc(mod_out, 1)

            for i in range(SPLIT):
                step(i, True)
            with dve.Fori(SPLIT, NB // 2) as i:
                step(i, False)
            dve.wait_ge(mod_out, NB)
            for s in (1, 4):
                m = mod[:, s * D:(s + 1) * D]
                dve.tensor_scalar(m, m, 1.0, None, ALU.add).then_inc(scaled, 1)
            if both:
                dve.wait_ge(ctx_out, 2 * SPLIT)
                dve.tensor_scalar(mod_ctx[:, D:2 * D], mod_ctx[:, D:2 * D], 1.0, None, ALU.add).then_inc(scaled, 1)
            dve.wait_ge(scaled, 3 if both else 2)


def norm_modulate_transpose(nc, tag, ident, tiles, aT, permuted, store=None, keep_rows=None):
    n = len(tiles)
    with Phase(nc, tag) as ph:
        from_dram = [t[2] for t in tiles]
        nload = sum(from_dram)
        xin = ph.sb("xin", [P, max(nload, 1), D]) if nload else None
        junk = ph.sb("junk", [P, 2, D])
        ss = ph.sb("ss", [P, n])
        var = ph.sb("var", [P, n])
        std = ph.sb("std", [P, n])
        rstd = ph.sb("rstd", [P, n])
        a = ph.sb("a", [P, 3, D])
        pT = [ph.ps(f"pT{i}", [P, KD, P]) for i in range(3)]
        x_in = [ph.sem(f"x_in{i}") for i in range(max(nload, 1))]
        sq_done, var_done, std_done, rstd_done = (ph.sem(s) for s in ("sq_done", "var_done", "std_done", "rstd_done"))
        scale_done, a_done, tr_done, copied = (ph.sem(s) for s in ("scale_done", "a_done", "tr_done", "copied"))
        stored = [ph.sem(f"stored{i}") for i in range(3)]
        src = []
        m = 0
        for t in tiles:
            if t[2]:
                src.append((xin[:, m, :], m))
                m += 1
            else:
                src.append((t[0], None))
        block = ph.block()

        @block.sync
        def _(sp):
            for i, t in enumerate(tiles):
                if t[2]:
                    sp.dma_start(src[i][0], t[0]).then_inc(x_in[src[i][1]], 16)
            if store is not None:
                for i in range(n):
                    sp.wait_ge(a_done, i + 1)
                    sp.dma_start(store[i], a[:, i % 3, :]).then_inc(stored[i % 3], 16)
                for j in range(min(3, n)):
                    sp.wait_ge(stored[j], 16 * len(range(j, n, 3)))

        @block.scalar
        def _(act):
            for i in range(n):
                if src[i][1] is not None:
                    act.wait_ge(x_in[src[i][1]], 16)
                if i >= 2:
                    act.wait_ge(sq_done, i - 1)
                act.activation(junk[:, i % 2, :], src[i][0], ACT.Square, accum_out=ss[:, i:i + 1]).then_inc(sq_done, 1)
            act.wait_ge(var_done, 1)
            act.activation(std[:, :], var[:, :], ACT.Sqrt).then_inc(std_done, 1)
            for i in range(n):
                act.wait_ge(tr_done, i + 1)
                act.activation(aT[:, :, i * P:(i + 1) * P], pT[i % 3][:, :, :], ACT.Copy).then_inc(copied, 1)
            act.wait_ge(copied, n)

        @block.vector
        def _(dve):
            dve.wait_ge(sq_done, n)
            dve.tensor_scalar(var[:, :], ss[:, :], 1.0 / D, EPS, ALU.mult, ALU.add).then_inc(var_done, 1)
            dve.wait_ge(std_done, 1)
            dve.reciprocal(rstd[:, :], std[:, :]).then_inc(rstd_done, 1)
            dve.wait_ge(rstd_done, 1)
            for i in range(n):
                if i >= 3:
                    dve.wait_ge(tr_done, i - 2)
                    if store is not None:
                        dve.wait_ge(stored[i % 3], 16 * (i // 3))
                shift, scale1 = tiles[i][1]
                av = a[:, i % 3, :]
                if permuted:
                    av = av.rearrange("q (k p) -> q p k", k=KD)
                    sv = src[i][0].rearrange("q (p k) -> q p k", k=KD)
                    hv, cv = shift.rearrange("q (p k) -> q p k", k=KD), scale1.rearrange("q (p k) -> q p k", k=KD)
                else:
                    sv, hv, cv = src[i][0], shift, scale1
                dve.scalar_tensor_tensor(av, sv, rstd[:, i:i + 1], cv, ALU.mult, ALU.mult).then_inc(scale_done, 1)
                dve.wait_ge(scale_done, i + 1)
                dve.tensor_tensor(av, av, hv, ALU.add).then_inc(a_done, 1)

        @block.tensor
        def _(pe):
            for i in range(n):
                pe.wait_ge(a_done, i + 1)
                if i >= 3:
                    pe.wait_ge(copied, i - 2)
                for k in range(KD):
                    tr = pe.transpose(pT[i % 3][:, k, :], a[:, i % 3, k * P:(k + 1) * P], ident[:, :])
                tr.then_inc(tr_done, 1)


def project(nc, ident, aT, w_in, q_gain, k_gain, u_dram, qT, kT, v_even, v_odd, v_ctx, bias_of):
    TG = [(0, NCH), (NCH, NCH), (2 * NCH, TOK - 2 * NCH)]
    NU = (W5 // P) * len(TG)
    w_v = w_in.rearrange("(p k) n -> p k n", k=KD)
    jobs = [(1, t) for t in range(CT, CT + TT)] + [(2, t) for t in range(CT + TT)] + [(3, t) for t in range(CT + TT)]
    NQK = TT + TT + CT
    last_of = {0: NU, 1: NU + TT, 2: NU + NQK, 3: NU + NQK + TT + CT}
    with Phase(nc, "proj") as ph:
        w = ph.sb("w", [P, 2, KD, NCH])
        uT = ph.sb("uT", [P, 2, LCH, NCK])
        sq = ph.sb("sq", [P, 2, NCH])
        ss = ph.sb("ss", [P, 2, HEADS])
        var = ph.sb("var", [P, 2, HEADS])
        std = ph.sb("std", [P, 2, HEADS])
        rstd = ph.sb("rstd", [P, 2, HEADS])
        qn = ph.sb("qn", [P, 2, NCH])
        gain = ph.sb("gain", [P, 2, HD])
        pz = [ph.ps(f"pz{i}", [P, NCH]) for i in range(4)]
        pt = [ph.ps(f"pt{i}", [P, HP, P]) for i in range(2)]
        w_got = [ph.sem(f"w_got{g}") for g in range(4)]
        gain_got, gain_scaled = ph.sem("gain_got"), ph.sem("gain_scaled")
        mm_done, z_used = ph.sem("mm_done"), ph.sem("z_used")
        u_out = [ph.sem(f"u_out{i}") for i in range(2)]
        sq_done, dve_step, std_done, n_done = ph.sem("sq_done"), ph.sem("dve_step"), ph.sem("std_done"), ph.sem("n_done")
        t_done, t_copied = ph.sem("t_done"), ph.sem("t_copied")
        v_done = ph.sem("v_done")
        odd_lo, odd_hi = ph.sem("odd_lo"), ph.sem("odd_hi")
        bias = bias_of(ph)
        block = ph.block()

        @block.gpsimd
        def _(pool):
            bias.mask(pool)

        @block.sync
        def _(sp):
            for g in range(4):
                if g >= 2:
                    sp.wait_ge(mm_done, last_of[g - 2])
                sp.dma_start(w[:, g % 2, :, :], w_v[:, :, g * NCH:(g + 1) * NCH]).then_inc(w_got[g], 16)
                if g == 0:
                    sp.dma_start(gain[:, 0, :], q_gain[None, :].to_broadcast([P, HD])).then_inc(gain_got, 16)
                    sp.dma_start(gain[:, 1, :], k_gain[None, :].to_broadcast([P, HD])).then_inc(gain_got, 16)
                    bias.load(sp)
                if g == 1:
                    bias.spread(sp)
                    for c in range(W5 // P):
                        sp.wait_ge(z_used, (c + 1) * len(TG))
                        sp.dma_start(u_dram[c * P:(c + 1) * P, :], uT[:, c % 2, :, :]).then_inc(u_out[c % 2], 16)
            sp.wait_ge(v_done, CT + TT)
            sp.dma_start(v_odd[0:64, :, :], v_even[64:128, 0:TT - 1, :]).then_inc(odd_lo, 16)
            sp.dma_start(v_odd[64:128, :, :], v_even[0:64, 1:TT, :]).then_inc(odd_hi, 16)
            sp.wait_ge(odd_lo, 16)
            sp.wait_ge(odd_hi, 16)
            for j in range(2):
                sp.wait_ge(u_out[j], 16 * (W5 // P // 2))

        @block.tensor
        def _(pe):
            n = 0
            pe.wait_ge(w_got[0], 16)
            for c in range(W5 // P):
                for t0, tn in TG:
                    if n >= 4:
                        pe.wait_ge(z_used, n - 3)
                    for k in range(KD):
                        mm = pe.matmul(pz[n % 4][:, 0:tn], w[:, 0, k, c * P:(c + 1) * P], aT[:, k, t0:t0 + tn],
                                       start=k == 0, stop=k == KD - 1)
                    mm.then_inc(mm_done, 1)
                    n += 1

            def turn(j):
                pe.wait_ge(n_done, j + 1)
                if j >= 2:
                    pe.wait_ge(t_copied, j - 1)
                for h in range(HP):
                    tr = pe.transpose(pt[j % 2][:, h, :], qn[:, j % 2, h * P:(h + 1) * P], ident[:, :])
                tr.then_inc(t_done, 1)

            for j, (g, t) in enumerate(jobs):
                pe.wait_ge(w_got[g], 16)
                pe.wait_ge(z_used, n - 3)
                for k in range(KD):
                    mm = pe.matmul(pz[n % 4][:, :], aT[:, k, t * P:(t + 1) * P], w[:, g % 2, k, :],
                                   start=k == 0, stop=k == KD - 1)
                mm.then_inc(mm_done, 1)
                n += 1
                if 2 <= j < NQK + 2:
                    turn(j - 2)

        @block.scalar
        def _(act):
            for j, (g, t) in enumerate(jobs):
                n = NU + j
                if g < 3:
                    act.wait_ge(mm_done, n + 1)
                    if j >= 2:
                        act.wait_ge(dve_step, 5 * (j - 2) + 1)
                    act.activation(sq[:, j % 2, :], pz[n % 4][:, :], ACT.Square).then_inc(sq_done, 1)
                    act.wait_ge(dve_step, 5 * j + 2)
                    act.activation(std[:, j % 2, :], var[:, j % 2, :], ACT.Sqrt).then_inc(std_done, 1)
                if g == 3 or j >= 2:
                    i = j - 2
                    if i < NQK:
                        gi, ti = jobs[i]
                        act.wait_ge(t_done, i + 1)
                        dst = qT[:, :, (ti - CT) * P:(ti - CT + 1) * P] if gi == 1 else kT[:, :, ti * P:(ti + 1) * P]
                        act.activation(dst, pt[i % 2][:, :, :], ACT.Copy).then_inc(t_copied, 1)
            act.wait_ge(t_copied, NQK)

        @block.vector
        def _(dve):
            bias.pad_rows(dve)
            dve.wait_ge(gain_got, 32)
            dve.tensor_scalar(gain[:, 0, :], gain[:, 0, :], HD ** -0.5, None, ALU.mult).then_inc(gain_scaled, 1)
            n = 0
            for c in range(W5 // P):
                for t0, tn in TG:
                    dve.wait_ge(mm_done, n + 1)
                    if c >= 2 and t0 == 0:
                        dve.wait_ge(u_out[c % 2], 16 * (c // 2))
                    m0, mn = t0 // LCH, tn // LCH
                    dve.tensor_copy(uT[:, c % 2, :, m0:m0 + mn],
                                    pz[n % 4][:, 0:tn].rearrange("p (m j) -> p j m", j=LCH)).then_inc(z_used, 1)
                    n += 1
            dve.wait_ge(gain_scaled, 1)
            for j, (g, t) in enumerate(jobs):
                n = NU + j
                z = pz[n % 4]
                if g == 3:
                    dve.wait_ge(mm_done, n + 1)
                    dst = v_ctx[:, t, :] if t < CT else v_even[:, t - CT, :]
                    cp = dve.tensor_copy(dst, z[:, :])
                    cp.then_inc(v_done, 1)
                    dve.wait_ge(v_done, j - NQK + 1)
                    dve.sem_inc(z_used, 1)
                    continue
                b = j % 2
                dve.wait_ge(sq_done, j + 1)
                dve.tensor_reduce(ss[:, b, :], sq[:, b, :].rearrange("p (h d) -> p h d", d=HD), AX.X, ALU.add).then_inc(dve_step, 1)
                dve.wait_ge(dve_step, 5 * j + 1)
                dve.tensor_scalar(var[:, b, :], ss[:, b, :], 1.0 / HD, EPS, ALU.mult, ALU.add).then_inc(dve_step, 1)
                dve.wait_ge(std_done, j + 1)
                dve.reciprocal(rstd[:, b, :], std[:, b, :]).then_inc(dve_step, 1)
                dve.wait_ge(dve_step, 5 * j + 3)
                if j >= 2:
                    dve.wait_ge(t_done, j - 1)
                q3 = qn[:, b, :].rearrange("p (h d) -> p h d", d=HD)
                dve.tensor_tensor(q3, z[:, :].rearrange("p (h d) -> p h d", d=HD),
                                  rstd[:, b, :, None].to_broadcast([P, HEADS, HD]), ALU.mult).then_inc(dve_step, 1)
                dve.wait_ge(dve_step, 5 * j + 4)
                dve.sem_inc(z_used, 1)
                dve.tensor_tensor(q3, q3, gain[:, g - 1, None, :].to_broadcast([P, HEADS, HD]), ALU.mult).then_inc(dve_step, 1)
                dve.wait_ge(dve_step, 5 * j + 5)
                dve.sem_inc(n_done, 1)


class BiasTable:

    def __init__(self, ph, rpb, pad_dram, bt):
        self.rpb, self.pad_dram, self.bt = rpb, pad_dram, bt
        self.W = 2 * GRID_W - 1
        self.table = ph.sb("table", [HEADS * RPB_R, RPB_C])
        self.pad = ph.sb("pad", [HEADS * RPB_R, self.W])
        self.cleared, self.rpb_got, self.pad_ready, self.pad_out, self.table_in = (
            ph.sem(s) for s in ("cleared", "rpb_got", "pad_ready", "pad_out", "table_in"))
        self.low, self.high = ph.sem("low"), ph.sem("high")

    def load(self, sp):
        sp.dma_start(self.table[:, :], self.rpb.rearrange("h r c -> (h r) c")).then_inc(self.rpb_got, 16)

    def pad_rows(self, dve):
        dve.wait_ge(self.rpb_got, 16)
        dve.wait_ge(self.cleared, 1)
        first = GRID_W - 1 - (KW - 1)
        dve.tensor_copy(self.pad[:, first:first + RPB_C], self.table[:, RPB_C - 1::-1]).then_inc(self.pad_ready, 1)

    def spread(self, sp):
        sp.wait_ge(self.pad_ready, 1)
        sp.dma_start(self.pad_dram, self.pad[:, :]).then_inc(self.pad_out, 16)
        sp.wait_ge(self.pad_out, 16)
        for a in range(2):
            for h in range(HP):
                src = bass.AP(tensor=self.pad_dram.tensor, offset=(2 * h + a) * RPB_R * self.W,
                              ap=[[1, GRID_W], [self.W, RPB_R], [1, GRID_W]])
                sp.dma_start(self.bt[a * 64:(a + 1) * 64, h, :, :], src).then_inc(self.table_in, 16)

    def mask(self, pool):
        pool.memset(self.pad[:, :], NEG).then_inc(self.cleared, 1)
        pool.wait_ge(self.table_in, 16 * 2 * HP)
        last = GRID_W - KW
        for a in range(2):
            t = self.bt[a * 64:(a + 1) * 64, :, :, GRID_W - last:GRID_W].rearrange("p h r c -> p (h r) c")
            pool.affine_select(out=t, in_=t, compare_op=ALU.is_ge, fill=NEG, base=KW // 2 + last - 1,
                               pattern=[[0, HP * RPB_R], [-1, last]], channel_multiplier=-1).then_inc(self.low, 1)
        pool.wait_ge(self.low, 2)
        for a in range(2):
            t = self.bt[a * 64:(a + 1) * 64, :, :, 0:GRID_W - KW].rearrange("p h r c -> p (h r) c")
            pool.affine_select(out=t, in_=t, compare_op=ALU.is_ge, fill=NEG, base=KW // 2 - GRID_W,
                               pattern=[[0, HP * RPB_R], [1, GRID_W - KW]], channel_multiplier=1).then_inc(self.high, 1)
        pool.wait_ge(self.high, 2)


def attention(nc, ident, qT, kT, v_even, v_odd, v_ctx, bt, out_dram):
    units = [(h, r) for h in range(HP) for r in range(ROWS)]
    N = len(units)
    NL = KH * GRID_W
    NK = NL + CTX
    NKT = NK // P
    first_row = [min(max(r - KH // 2, 0), ROWS - KH) for r in range(ROWS)]
    with Phase(nc, "att") as ph:
        qbd = ph.sb("qbd", [P, 2, P])
        sl = ph.sb("sl", [P, 2, NL])
        m = ph.sb("m", [P, 2, 4])
        nm = ph.sb("nm", [P, 2])
        sums = ph.sb("sums", [P, 2, 2])
        den = ph.sb("den", [P, 2])
        rden = ph.sb("rden", [P, 2])
        pr = ph.sb("pr", [P, 2, NK])
        prT = ph.sb("prT", [P, 2, NKT, P])
        obd = ph.sb("obd", [P, 2, P])
        oT = ph.sb("oT", [P, HP, SEQ])
        stored = ph.sem("stored")
        p_loc = [ph.ps(f"p_loc{i}", [P, NL]) for i in range(2)]
        p_ctx = [ph.ps(f"p_ctx{i}", [P, NCH]) for i in range(2)]
        p_t = [ph.ps(f"p_t{i}", [P, 4, P]) for i in range(2)]
        p_o = ph.ps("p_o", [P, NCH])
        p_ot = ph.ps("p_ot", [P, NCH])
        zeroed = ph.sem("zeroed")
        q_ready, s_done, max_done, nm_done, exp_done = (ph.sem(s) for s in ("q_ready", "s_done", "max_done", "nm_done", "exp_done"))
        pt_done, ptc_act, ptc_dve = ph.sem("pt_done"), ph.sem("ptc_act"), ph.sem("ptc_dve")
        den_done, rden_done, pv_done, o_ready, ot_done, o_out = (ph.sem(s) for s in ("den_done", "rden_done", "pv_done", "o_ready", "ot_done", "o_out"))
        block = ph.block()

        @block.sync
        def _(sp):
            for h in range(HP):
                sp.wait_ge(o_out, 2 * ROWS * (h + 1))
                sp.dma_start(out_dram[h * P:(h + 1) * P, :], oT[:, h, :]).then_inc(stored, 16)
            sp.wait_ge(stored, 16 * HP)

        @block.gpsimd
        def _(pool):
            pool.memset(qbd[:, :, :], 0.0).then_inc(zeroed, 1)
            pool.memset(obd[:, :, :], 0.0).then_inc(zeroed, 1)
            pool.wait_ge(zeroed, 2)
            for n, (h, r) in enumerate(units):
                if n >= 2:
                    pool.wait_ge(s_done, n - 1)
                for a in range(2):
                    pool.tensor_copy(qbd[a * 64:(a + 1) * 64, n % 2, a * 64:(a + 1) * 64],
                                     qT[a * 64:(a + 1) * 64, h, r * 64:(r + 1) * 64]).then_inc(q_ready, 1)

        @block.tensor
        def _(pe):
            def scores(n):
                h, r = units[n]
                b = n % 2
                pe.wait_ge(q_ready, 2 * n + 2)
                if n >= 2:
                    pe.wait_ge(max_done, 2 * (n - 1))
                    pe.wait_ge(exp_done, 2 * (n - 1))
                k0 = CTX + first_row[r] * GRID_W
                pe.matmul(p_loc[b][:, :], qbd[:, b, :], kT[:, h, k0:k0 + NL], start=True, stop=True)
                pe.matmul(p_ctx[b][:, 0:CTX], qbd[:, b, :], kT[:, h, 0:CTX], start=True, stop=True).then_inc(s_done, 1)

            def turn(n):
                b = n % 2
                pe.wait_ge(exp_done, 2 * n + 2)
                if n >= 1:
                    pe.wait_ge(ptc_act, n)
                    pe.wait_ge(ptc_dve, n)
                for t in range(NKT):
                    tr = pe.transpose(p_t[t // 3][:, t % 3, :], pr[:, b, t * P:(t + 1) * P], ident[:, :])
                tr.then_inc(pt_done, 1)

            def values(n):
                h, r = units[n]
                b = n % 2
                pe.wait_ge(ptc_act, n + 1)
                pe.wait_ge(ptc_dve, n + 1)
                if n >= 1:
                    pe.wait_ge(o_ready, 2 * n)
                r0 = first_row[r]
                v_loc = v_odd if r0 % 2 else v_even
                for t in range(NKT):
                    v = v_loc[:, r0 // 2 + t, h * P:(h + 1) * P] if t < NL // P else v_ctx[:, t - NL // P, h * P:(h + 1) * P]
                    mm = pe.matmul(p_o[:, 0:P], prT[:, b, t, :], v, start=t == 0, stop=t == NKT - 1)
                mm.then_inc(pv_done, 1)

            def turn_out(n):
                b = n % 2
                pe.wait_ge(o_ready, 2 * n + 2)
                if n >= 1:
                    pe.wait_ge(o_out, 2 * n)
                pe.transpose(p_ot[:, 0:P], obd[:, b, :], ident[:, :]).then_inc(ot_done, 1)

            pe.wait_ge(zeroed, 2)
            for i in range(N + 3):
                if i < N:
                    scores(i)
                if 1 <= i <= N:
                    turn(i - 1)
                if 2 <= i <= N + 1:
                    values(i - 2)
                if 3 <= i:
                    turn_out(i - 3)

        @block.vector
        def _(dve):
            def maxima(n):
                h, r = units[n]
                b = n % 2
                rel = first_row[r] - r + KH - 1
                dve.wait_ge(s_done, n + 1)
                if n >= 2:
                    dve.wait_ge(exp_done, 2 * (n - 1))
                rows = lambda t: t.rearrange("p (r c) -> p r c", r=KH)
                dve.tensor_tensor_reduce(rows(sl[:, b, :]), rows(p_loc[b][:, :]), bt[:, h, rel:rel + KH, GRID_W - 1::-1],
                                         1.0, -3e38, ALU.add, ALU.max, m[:, b, 0:1]).then_inc(max_done, 1)
                dve.tensor_reduce(m[:, b, 1:2], p_ctx[b][:, 0:CTX], AX.X, ALU.max).then_inc(max_done, 1)
                dve.wait_ge(max_done, 2 * n + 2)
                dve.tensor_scalar(nm[:, b:b + 1], m[:, b, 0:1], m[:, b, 1:2], -1.0, ALU.max, ALU.mult).then_inc(nm_done, 1)

            def copy_half(n):
                b = n % 2
                dve.wait_ge(pt_done, n + 1)
                if n >= 2:
                    dve.wait_ge(pv_done, n - 1)
                dve.tensor_copy(prT[:, b, 3:NKT, :], p_t[1][:, 0:3, :]).then_inc(ptc_dve, 1)
                dve.wait_ge(exp_done, 2 * n + 2)
                dve.tensor_tensor(den[:, b:b + 1], sums[:, b, 0:1], sums[:, b, 1:2], ALU.add).then_inc(den_done, 1)
                dve.wait_ge(den_done, n + 1)
                dve.reciprocal(rden[:, b:b + 1], den[:, b:b + 1]).then_inc(rden_done, 1)

            def scale(n):
                b = n % 2
                dve.wait_ge(pv_done, n + 1)
                dve.wait_ge(rden_done, n + 1)
                if n >= 2:
                    dve.wait_ge(ot_done, n - 1)
                for a in range(2):
                    s = slice(a * 64, (a + 1) * 64)
                    dve.tensor_scalar(obd[s, b, s], p_o[s, s], rden[s, b:b + 1], None, ALU.mult).then_inc(o_ready, 1)

            dve.wait_ge(zeroed, 2)
            for i in range(N + 2):
                if i < N:
                    maxima(i)
                if 1 <= i <= N:
                    copy_half(i - 1)
                if 2 <= i:
                    scale(i - 2)

        @block.scalar
        def _(act):
            def exps(n):
                b = n % 2
                act.wait_ge(nm_done, n + 1)
                if n >= 2:
                    act.wait_ge(pt_done, n - 1)
                    act.wait_ge(den_done, n - 1)
                act.activation(pr[:, b, 0:NL], sl[:, b, :], ACT.Exp, bias=nm[:, b:b + 1], accum_out=sums[:, b, 0:1]).then_inc(exp_done, 1)
                act.activation(pr[:, b, NL:NK], p_ctx[b][:, 0:CTX], ACT.Exp, bias=nm[:, b:b + 1], accum_out=sums[:, b, 1:2]).then_inc(exp_done, 1)

            def copy_half(n):
                b = n % 2
                act.wait_ge(pt_done, n + 1)
                if n >= 2:
                    act.wait_ge(pv_done, n - 1)
                act.activation(prT[:, b, 0:3, :], p_t[0][:, 0:3, :], ACT.Copy).then_inc(ptc_act, 1)

            def out(n):
                h, r = units[n]
                b = n % 2
                act.wait_ge(ot_done, n + 1)
                for a in range(2):
                    s = slice(a * 64, (a + 1) * 64)
                    act.activation(oT[s, h, r * 64:(r + 1) * 64], p_ot[s, s], ACT.Copy).then_inc(o_out, 1)

            for i in range(N + 3):
                if i < N:
                    exps(i)
                if 1 <= i <= N:
                    copy_half(i - 1)
                if 3 <= i:
                    out(i - 3)
            act.wait_ge(o_out, 2 * N)


GS = G5 // 8
NP9 = LCH + 1
TAUS = 2 * LCH - 1
TWO_PI = 2 * math.pi
PI_A = 6.28125
PI_B = 0.0019350051879882812
PI_C = TWO_PI - PI_A - PI_B
ROUND = 1.5 * 2.0 ** 23


def s5_matrices(nc, ident, lam_re, lam_im, log_dt, b_re, b_im, c_re, c_im, d, mats, k_dram, rot_dram, decay):
    with Phase(nc, "mats") as ph:
        nat = ph.sb("nat", [G5, 2, 2, S5])
        ldt = ph.sb("ldt", [G5, 2])
        edt = ph.sb("edt", [G5, 2])
        dtn = ph.sb("dtn", [G5, 2, S5])
        ones = ph.sb("ones", [P, S5])
        base = ph.sb("base", [P, 3, G5])
        sm = ph.sb("sm", [P, 24, G5])
        pw = ph.sb("pw", [P, 2, NP9, G5])
        tp = ph.sb("tp", [P, 4, 4, G5])
        pg = ph.sb("pg", [P, 2, LCH, G5])
        pw9 = ph.sb("pw9", [P, 2, NP9, G5])
        bn = ph.sb("bn", [P, 2, G5, C5])
        bb = ph.sb("bb", [P, 2, G5, C5])
        cn = ph.sb("cn", [P, 2, GS, 2, S5])
        cc = ph.sb("cc", [P, 2, W5])
        g = ph.sb("g", [P, 8, LCH, C5])
        g2 = ph.sb("g2", [P, 8, LCH, C5])
        w9 = ph.sb("w9", [P, 2, G5, NP9, C5])
        big = ph.sb("big", [P, 2, 8, NP9, C5])
        winT = ph.sb("winT", [P, 2, 8, P])
        bpad = ph.sb("bpad", [P, 2, G5, P])
        dcol = ph.sb("dcol", [P, GS])
        eye16 = ph.sb("eye16", [P, C5])
        kall = ph.sb("kall", [P, GS, TAUS, C5])
        toep = ph.sb("toep", [P, G5, P])
        rot = ph.sb("rot", [P, 2, G5, NCK])
        rt = toep[:, :, :].rearrange("p (i a) c -> p i (a c)", i=4)
        p_in = ph.ps("p_in", [P, NCH])
        p_c = ph.ps("p_c", [P, 4, P])
        p_g = [ph.ps(f"p_g{i}", [P, 4, P]) for i in range(2)]
        p_k = [[ph.ps(f"p_k{b}{i}", [P, NCH]) for i in range(2)] for b in range(2)]
        got_lam, got_b, got_c, got_d = (ph.sem(s) for s in ("got_lam", "got_b", "got_c", "got_d"))
        exp_done, dtn_done, base_tr, act_done = (ph.sem(s) for s in ("exp_done", "dtn_done", "base_tr", "act_done"))
        step = ph.sem("step")
        angles, c_tr, c_copied = ph.sem("angles"), ph.sem("c_tr"), ph.sem("c_copied")
        g_ready, g_tr, g_copied, g_out = ph.sem("g_ready"), ph.sem("g_tr"), ph.sem("g_copied"), ph.sem("g_out")
        w9_ready, w9_out, bpad_ready, k_done, k_read = (ph.sem(s) for s in ("w9_ready", "w9_out", "bpad_ready", "k_done", "k_read"))
        zeroed, kall_ready, k_out, toep_in, toep_out = (ph.sem(s) for s in ("zeroed", "kall_ready", "k_out", "toep_in", "toep_out"))
        rot_ready, rot_out = ph.sem("rot_ready"), ph.sem("rot_out")
        block = ph.block()

        @block.sync
        def _(sp):
            sp.dma_start(nat[:, 0, :, :], lam_re.rearrange("s g p -> g s p")).then_inc(got_lam, 16)
            sp.dma_start(nat[:, 1, :, :], lam_im.rearrange("s g p -> g s p")).then_inc(got_lam, 16)
            sp.dma_start(ldt[:, :], log_dt.rearrange("s g -> g s"), allow_slow_non_contiguous=True).then_inc(got_lam, 16)
            for i, src in enumerate((c_re, c_im)):
                for s in range(2):
                    sp.dma_start(cn[:, i, :, s, :], src[s].rearrange("(q e) c p -> (e c) q p", e=8)).then_inc(got_c, 16)
            for i, src in enumerate((b_re, b_im)):
                for s in range(2):
                    sp.dma_start(bn[s * 64:(s + 1) * 64, i, :, :], src[s].rearrange("g p c -> p g c")).then_inc(got_b, 16)
            sp.dma_start(dcol[:, :], d.rearrange("(q e) c -> (e c) q", e=8), allow_slow_non_contiguous=True).then_inc(got_d, 16)
            for q in range(GS):
                sp.wait_ge(g_copied, 4 * (q + 1))
                for i in range(2):
                    sp.dma_start(mats[:, i, 8 * q:8 * q + 8, :], winT[:, i, :, :]).then_inc(g_out, 16)
            sp.wait_ge(w9_ready, GS)
            for i in range(2):
                sp.dma_start(mats[:, 2 + i, :, :], w9[:, i, :, 0:LCH, :].rearrange("p g j c -> p g (j c)")).then_inc(w9_out, 16)
            sp.wait_ge(rot_ready, 1)
            sp.dma_start(rot_dram, rot[:, :, :, :]).then_inc(rot_out, 16)
            sp.wait_ge(kall_ready, GS)
            sp.dma_start(k_dram.rearrange("(q e c) t -> (e c) q t", e=8, c=C5), kall[:, :, :, :].rearrange("p q t c -> p q (t c)")).then_inc(k_out, 16)
            sp.wait_ge(k_out, 16)
            for i in range(LCH):
                src = k_dram.rearrange("(g c) t -> c g t", c=C5)[:, :, (LCH - 1 - i) * C5:(2 * LCH - 1 - i) * C5]
                sp.dma_start(toep[i * C5:(i + 1) * C5, :, :], src).then_inc(toep_in, 16)
            sp.wait_ge(toep_in, 16 * LCH)
            sp.dma_start(mats[:, 4, :, :], toep[:, :, :]).then_inc(toep_out, 16)
            sp.wait_ge(g_out, 16 * 2 * GS)
            sp.wait_ge(w9_out, 32)
            sp.wait_ge(toep_out, 16)
            sp.wait_ge(rot_out, 16)

        @block.scalar
        def _(act):
            act.wait_ge(got_lam, 48)
            act.activation(edt[:, :], ldt[:, :], ACT.Exp).then_inc(exp_done, 1)
            act.wait_ge(angles, 1)
            act.activation(sm[:, 4, :], sm[:, 2, :], ACT.Exp).then_inc(act_done, 1)
            act.activation(decay[:, :], sm[:, 2, :], ACT.Exp, scale=float(LCH)).then_inc(act_done, 1)
            act.wait_ge(angles, 2)
            act.activation(sm[:, 8, :], sm[:, 5, :], ACT.Sin).then_inc(act_done, 1)
            act.activation(sm[:, 9, :], sm[:, 7, :], ACT.Sin).then_inc(act_done, 1)
            for q in range(GS):
                for i in range(2):
                    for h in range(2):
                        n = 4 * q + 2 * i + h
                        act.wait_ge(g_tr, n + 1)
                        if q >= 1:
                            act.wait_ge(g_out, 16 * 2 * q)
                        act.activation(winT[:, i, 4 * h:4 * h + 4, :], p_g[n % 2][:, :, :], ACT.Copy).then_inc(g_copied, 1)
            act.wait_ge(g_copied, 4 * GS)

        @block.gpsimd
        def _(pool):
            pool.memset(bpad[:, :, :, :], 0.0).then_inc(zeroed, 1)

        @block.tensor
        def _(pe):
            pe.wait_ge(dtn_done, 2)
            for i, src in enumerate((nat[:, 0, :, :], nat[:, 1, :, :], dtn[:, :, :])):
                tr = pe.transpose(p_in[:, i * G5:(i + 1) * G5], src.rearrange("g s p -> g (s p)"), ident[0:G5, 0:G5])
            tr.then_inc(base_tr, 1)
            pe.wait_ge(got_c, 64)
            for i in range(2):
                if i == 1:
                    pe.wait_ge(c_copied, 1)
                for q in range(GS):
                    tr = pe.transpose(p_c[:, q, :], cn[:, i, q, :, :].rearrange("p s c -> p (s c)"), ident[:, :])
                tr.then_inc(c_tr, 1)
            for q in range(GS):
                for i in range(2):
                    pe.wait_ge(g_ready, 2 * q + i + 1)
                    for h in range(2):
                        n = 4 * q + 2 * i + h
                        if n >= 2:
                            pe.wait_ge(g_copied, n - 1)
                        for e in range(4):
                            tr = pe.transpose(p_g[n % 2][:, e, :], (g, g2)[i][:, 4 * h + e, :, :].rearrange("p j c -> p (j c)"), ident[:, :])
                        tr.then_inc(g_tr, 1)
            pe.wait_ge(bpad_ready, 1)
            pe.wait_ge(w9_ready, GS)
            for q in range(GS):
                for s in range(2):
                    if q >= 2:
                        pe.wait_ge(k_read, q - 1)
                    r = slice(s * 64, (s + 1) * 64)
                    for e in range(8):
                        for i in range(2):
                            mm = pe.matmul(p_k[q % 2][s][:, 0:NP9 * C5], bpad[r, i, 8 * q + e, :],
                                           w9[r, i, 8 * q + e, :, :].rearrange("p j c -> p (j c)"),
                                           start=e == 0 and i == 0, stop=e == 7 and i == 1)
                    mm.then_inc(k_done, 1)

        @block.vector
        def _(dve):
            link = Chain(dve, step)

            def cmul(o_re, o_im, a_re, a_im, b_re_, b_im_, t):
                dve.tensor_tensor(t[0], a_re, b_re_, ALU.mult).then_inc(step, 1)
                dve.tensor_tensor(t[1], a_im, b_im_, ALU.mult).then_inc(step, 1)
                dve.tensor_tensor(t[2], a_re, b_im_, ALU.mult).then_inc(step, 1)
                dve.tensor_tensor(t[3], a_im, b_re_, ALU.mult).then_inc(step, 1)
                link.n += 4
                dve.wait_ge(step, link.n)
                dve.tensor_tensor(o_re, t[0], t[1], ALU.subtract).then_inc(step, 1)
                dve.tensor_tensor(o_im, t[2], t[3], ALU.add).then_inc(step, 1)
                link.n += 2
                dve.wait_ge(step, link.n)

            dve.wait_ge(exp_done, 1)
            link(dve.memset(ones[:, :], 1.0))
            for s in range(2):
                dve.tensor_scalar(dtn[:, s, :], ones[0:G5, :], edt[:, s:s + 1], None, ALU.mult).then_inc(dtn_done, 1)
            dve.wait_ge(base_tr, 1)
            link(dve.tensor_copy(base[:, :, :], p_in[:, 0:3 * G5].rearrange("p (i g) -> p i g", i=3)))
            re, im, dt = base[:, 0, :], base[:, 1, :], base[:, 2, :]
            T = lambda i: sm[:, i, :]
            link(dve.tensor_scalar(T(0), re, -1e-4, None, ALU.min))
            link(dve.tensor_tensor(T(1), im, dt, ALU.mult))
            dve.tensor_tensor(T(2), T(0), dt, ALU.mult).then_inc(angles, 1)
            link(dve.tensor_scalar(T(3), T(1), 1.0 / TWO_PI, None, ALU.mult))
            link(dve.tensor_scalar(T(3), T(3), ROUND, None, ALU.add))
            link(dve.tensor_scalar(T(3), T(3), ROUND, None, ALU.subtract))
            link(dve.scalar_tensor_tensor(T(5), T(3), -PI_A, T(1), ALU.mult, ALU.add))
            link(dve.scalar_tensor_tensor(T(5), T(3), -PI_B, T(5), ALU.mult, ALU.add))
            link(dve.scalar_tensor_tensor(T(5), T(3), -PI_C, T(5), ALU.mult, ALU.add))
            link(dve.tensor_scalar(T(6), T(5), math.pi / 2, None, ALU.add))
            link(dve.tensor_scalar(T(7), T(6), math.pi, -TWO_PI, ALU.is_gt, ALU.mult))
            link(dve.tensor_tensor(T(7), T(6), T(7), ALU.add))
            link(dve.tensor_scalar(T(5), T(5), 3.1415925, -3.1415925, ALU.min, ALU.max))
            link(dve.tensor_scalar(T(7), T(7), 3.1415925, -3.1415925, ALU.min, ALU.max))
            dve.sem_inc(angles, 1)
            dve.wait_ge(act_done, 4)
            link(dve.memset(pw[:, 0, 0, :], 1.0))
            link(dve.memset(pw[:, 1, 0, :], 0.0))
            link(dve.tensor_tensor(pw[:, 1, 1, :], T(8), T(4), ALU.mult))
            link(dve.tensor_tensor(pw[:, 0, 1, :], T(9), T(4), ALU.mult))
            for m in (1, 2, 4):
                x = [tp[:, i, 0:m, :] for i in range(4)]
                top = [pw[:, i, m, None, :].to_broadcast([P, m, G5]) for i in range(2)]
                cmul(pw[:, 0, m + 1:2 * m + 1, :], pw[:, 1, m + 1:2 * m + 1, :],
                     pw[:, 0, 1:m + 1, :], pw[:, 1, 1:m + 1, :], top[0], top[1], x)
            f, b = slice(0, 64), slice(64, P)
            for i in range(2):
                link(dve.tensor_copy(pg[f, i, :, :], pw[f, i, LCH - 1::-1, :]))
                link(dve.tensor_copy(pg[b, i, :, :], pw[b, i, 0:LCH, :]))
                link(dve.tensor_copy(pw9[f, i, 0:LCH, :], pw[f, i, 1:NP9, :]))
                link(dve.tensor_copy(pw9[b, i, 0:LCH, :], pw[b, i, LCH:0:-1, :]))
                link(dve.tensor_copy(pw9[:, i, LCH, :], pw[:, i, 0, :]))
            link(dve.tensor_scalar(T(10), pw[:, 0, 1, :], -1.0, None, ALU.add))
            link(dve.tensor_tensor(T(11), T(0), T(0), ALU.mult))
            link(dve.tensor_tensor(T(12), im, im, ALU.mult))
            link(dve.tensor_tensor(T(11), T(11), T(12), ALU.add))
            link(dve.reciprocal(T(12), T(11)))
            link(dve.tensor_tensor(T(13), T(0), T(12), ALU.mult))
            link(dve.tensor_tensor(T(14), im, T(12), ALU.mult))
            link(dve.tensor_scalar(T(14), T(14), -1.0, None, ALU.mult))
            cmul(T(15), T(16), T(10), pw[:, 1, 1, :], T(13), T(14), [T(17), T(18), T(19), T(20)])
            dve.wait_ge(got_b, 64)
            fr, fi = (T(i)[:, :, None].to_broadcast([P, G5, C5]) for i in (15, 16))
            tb = [big[:, i, :, :, :].rearrange("p e j c -> p (e j c)")[:, 0:G5 * C5].rearrange("p (g c) -> p g c", g=G5) for i in range(2)]
            tc = [big[:, i, :, :, :].rearrange("p e j c -> p (e j c)")[:, G5 * C5:2 * G5 * C5].rearrange("p (g c) -> p g c", g=G5) for i in range(2)]
            cmul(bb[:, 0, :, :], bb[:, 1, :, :], bn[:, 0, :, :], bn[:, 1, :, :], fr, fi, [tb[0], tb[1], tc[0], tc[1]])
            for i in range(2):
                dve.wait_ge(c_tr, i + 1)
                dve.tensor_copy(cc[:, i, :], p_c[:, :, :].rearrange("p q c -> p (q c)")).then_inc(c_copied, 1)
            dve.wait_ge(c_copied, 2)
            dve.wait_ge(zeroed, 1)
            for i in range(2):
                for e in range(8):
                    link(dve.tensor_copy(bpad[:, i, e::8, e * C5:(e + 1) * C5], bb[:, i, e::8, :]))
            dve.sem_inc(bpad_ready, 1)
            for q in range(GS):
                e8 = slice(8 * q, 8 * q + 8)
                sh = [P, 8, LCH, C5]
                pr = [pg[:, i, :, e8].rearrange("p j g -> p g j")[:, :, :, None].to_broadcast(sh) for i in range(2)]
                br = [bb[:, i, e8, None, :].to_broadcast(sh) for i in range(2)]
                t0, t1 = big[:, 0, :, 0:LCH, :], big[:, 1, :, 0:LCH, :]
                if q >= 1:
                    dve.wait_ge(g_tr, 4 * q)
                link(dve.tensor_tensor(t0, pr[0], br[0], ALU.mult))
                link(dve.tensor_tensor(t1, pr[1], br[1], ALU.mult))
                link(dve.tensor_tensor(g[:, :, :, :], t0, t1, ALU.subtract))
                dve.sem_inc(g_ready, 1)
                link(dve.tensor_tensor(t0, pr[0], br[1], ALU.mult))
                link(dve.tensor_tensor(t1, pr[1], br[0], ALU.mult))
                link(dve.tensor_tensor(g2[:, :, :, :], t0, t1, ALU.add))
                dve.sem_inc(g_ready, 1)
                sh = [P, 8, NP9, C5]
                pr = [pw9[:, i, :, e8].rearrange("p j g -> p g j")[:, :, :, None].to_broadcast(sh) for i in range(2)]
                cr = [cc[:, i, 8 * q * C5:8 * (q + 1) * C5].rearrange("p (g c) -> p g c", g=8)[:, :, None, :].to_broadcast(sh) for i in range(2)]
                t0, t1 = big[:, 0, :, :, :], big[:, 1, :, :, :]
                link(dve.tensor_tensor(t0, pr[0], cr[0], ALU.mult))
                link(dve.tensor_tensor(t1, pr[1], cr[1], ALU.mult))
                link(dve.tensor_tensor(w9[:, 0, e8, :, :], t0, t1, ALU.subtract))
                link(dve.tensor_tensor(t0, pr[0], cr[1], ALU.mult))
                link(dve.tensor_tensor(t1, pr[1], cr[0], ALU.mult))
                link(dve.tensor_tensor(t0, t0, t1, ALU.add))
                link(dve.tensor_scalar(w9[:, 1, e8, :, :], t0, -1.0, None, ALU.mult))
                dve.sem_inc(w9_ready, 1)
            link(dve.tensor_reduce(eye16[:, :], ident[:, :].rearrange("p (q c) -> p c q", c=C5), AX.X, ALU.add))
            dve.wait_ge(got_d, 16)

            def lag_kernels(q):
                dve.wait_ge(k_done, 2 * q + 2)
                kf = p_k[q % 2][0][:, 0:NP9 * C5].rearrange("p (t c) -> p t c", c=C5)
                kb = p_k[q % 2][1][:, 0:NP9 * C5].rearrange("p (t c) -> p t c", c=C5)
                link(dve.tensor_copy(kall[:, q, 0:LCH - 1, :], kb[:, 1:LCH, :]))
                link(dve.tensor_copy(kall[:, q, LCH:TAUS, :], kf[:, 0:LCH - 1, :]))
                link(dve.scalar_tensor_tensor(kall[:, q, LCH - 1, :], eye16[:, :], dcol[:, q:q + 1], kf[:, LCH, :], ALU.mult, ALU.add))
                link(dve.tensor_tensor(kall[:, q, LCH - 1, :], kall[:, q, LCH - 1, :], kb[:, LCH, :], ALU.add))
                dve.sem_inc(k_read, 1)
                dve.sem_inc(kall_ready, 1)

            u = [(T(9), T(8))]
            spare = iter([(T(21), T(22)), (T(4), T(23)), (T(21), T(22))])
            for _ in range(3):
                nre, nim = next(spare)
                cmul(nre, nim, u[-1][0], u[-1][1], u[-1][0], u[-1][1], [T(17), T(18), T(19), T(20)])
                u.append((nre, nim))
            link(dve.memset(rot[:, 0, :, 0], 1.0))
            link(dve.memset(rot[:, 1, :, 0], 0.0))
            link(dve.tensor_copy(rot[:, 0, :, 1], u[-1][0]))
            link(dve.tensor_copy(rot[:, 1, :, 1], u[-1][1]))
            m = 1
            while m < NCK - 1:
                n = min(m, NCK - 1 - m, 32)
                w = n * G5
                x = [rt[:, i, 0:w].rearrange("p (g n) -> p g n", g=G5) for i in range(4)]
                top = [rot[:, i, :, m:m + 1].to_broadcast([P, G5, n]) for i in range(2)]
                cmul(rot[:, 0, :, m + 1:m + 1 + n], rot[:, 1, :, m + 1:m + 1 + n],
                     rot[:, 0, :, 1:1 + n], rot[:, 1, :, 1:1 + n], top[0], top[1], x)
                m += n
                if m == 3 * 32:
                    lag_kernels(0)
            dve.sem_inc(rot_ready, 1)
            for q in range(1, GS):
                lag_kernels(q)


def s5_scan_readout(nc, ident, u_dram, mats, rot_dram, decay, y_dram, w_glu, b_glu, out_dram):
    NX = NCK + NCC
    SC = 8
    L0 = NCC - 1
    with Phase(nc, "scan") as ph:
        u = ph.sb("u", [P, G5, NX])
        mt = ph.sb("mt", [P, 3, 5, 2, P])
        bs = ph.sb("bs", [P, 2, SC, NCK])
        xs = ph.sb("xs", [P, 2, SC, NCK])
        tmp = ph.sb("tmp", [P, 4, SC, NCK])
        dk = ph.sb("dk", [P, SC, NCK])
        ones = ph.sb("ones", [P, NCK])
        rot = ph.sb("rot", [P, 2, 2, SC, NCK])
        rot_in = [ph.sem(f"rot_in{i}") for i in range(2)]
        st = ph.sb("st", [P, 2, SC, NCL])
        y = ph.sb("y", [P, 2, SC, NCL])
        p_b = [[ph.ps(f"p_b{i}{n}", [P, 2, NCK]) for n in range(2)] for i in range(2)]
        p_y = [ph.ps(f"p_y{n}", [P, 2, NCL]) for n in range(2)]
        u_in, m_in = ph.sem("u_in"), [ph.sem(f"m_in{i}") for i in range(3)]
        b_mm, b_out, step, st_ready, y_mm, y_out = (ph.sem(s) for s in ("b_mm", "b_out", "step", "st_ready", "y_mm", "y_out"))
        y_st = [ph.sem(f"y_st{i}") for i in range(2)]
        step_a = ph.sem("step_a")
        dk_ready = ph.sem("dk_ready")
        block = ph.block()
        NPAIR = SC // 2
        TOTAL = GS * NPAIR

        order = []
        for q in range(GS + 1):
            if q < GS:
                order += [(0, q, e) for e in range(NPAIR)]
            if q >= 1:
                order += [(1, q - 1, e) for e in range(NPAIR)]

        @block.sync
        def _(sp):
            for j in range(LCH):
                src = u_dram.rearrange("(g c) (j m) -> j c g m", c=C5, j=LCH)[j]
                sp.dma_start(u[j * C5:(j + 1) * C5, :, 0:NCK], src).then_inc(u_in, 16)
                sp.dma_start(u[j * C5:(j + 1) * C5, :, NCK:NX], src[:, :, 0:NCC]).then_inc(u_in, 16)
            for q in range(2):
                sp.dma_start(rot[:, q, :, :, :], rot_dram[:, :, SC * q:SC * (q + 1), :]).then_inc(rot_in[q], 16)
            nb, ny, users = 0, 0, []
            for n, (s, q, e) in enumerate(order):
                if n >= 3:
                    k, v = users[n - 3]
                    sp.wait_ge((b_mm, y_mm)[k], v)
                if s == 0:
                    nb += 1
                    users.append((0, nb))
                else:
                    ny += 1
                    users.append((1, ny))
                g0 = SC * q + 2 * e
                sel = slice(0, 2) if s == 0 else slice(2, 5)
                if s == 1 and e == 0 and q < GS - 2:
                    sp.wait_ge(st_ready, q + 1)
                    sp.dma_start(rot[:, q % 2, :, :, :], rot_dram[:, :, SC * (q + 2):SC * (q + 3), :]).then_inc(rot_in[q % 2], 16)
                sp.dma_start(mt[:, n % 3, sel, :, :], mats[:, sel, g0:g0 + 2, :]).then_inc(m_in[n % 3], 16)

        @block.gpsimd
        def _(pool):
            for q in range(GS):
                pool.wait_ge(y_out, NPAIR * (q + 1))
                for j in range(LCH):
                    dst = y_dram.rearrange("(g c) (j m) -> j c g m", c=C5, j=LCH)[j][:, SC * q:SC * (q + 1), :]
                    pool.dma_start(dst, y[j * C5:(j + 1) * C5, q % 2, :, :]).then_inc(y_st[q % 2], 16)
            for i in range(2):
                pool.wait_ge(y_st[i], 16 * LCH * GS // 2)

        @block.tensor
        def _(pe):
            pe.wait_ge(u_in, 16 * 2 * LCH)
            nb = ny = 0
            f, b = slice(0, 64), slice(64, P)
            for n, (s, q, e) in enumerate(order):
                pe.wait_ge(m_in[n % 3], 16 * (n // 3 + 1))
                m = mt[:, n % 3]
                if s == 0:
                    if nb >= 2:
                        pe.wait_ge(b_out, 2 * (nb - 1))
                    for i in range(2):
                        for k in range(2):
                            g = SC * q + 2 * e + k
                            pe.matmul(p_b[i][nb % 2][f, k, :], m[:, i, k, f], u[:, g, 0:NCK], start=True, stop=True)
                            mm = pe.matmul(p_b[i][nb % 2][b, k, :], m[:, i, k, b], u[:, g, NX - 1:NCC - 1:-1], start=True, stop=True)
                    nb += 1
                    mm.then_inc(b_mm, 1)
                else:
                    if ny >= 2:
                        pe.wait_ge(y_out, ny - 1)
                    pe.wait_ge(st_ready, q + 1)
                    for k in range(2):
                        g, l = SC * q + 2 * e + k, 2 * e + k
                        o = p_y[ny % 2][:, k, :]
                        pe.matmul(o, m[:, 4, k, :], u[:, g, NCC:NCK], start=True, stop=False)
                        pe.matmul(o, m[:, 2, k, :], st[:, 0, l, :], start=False, stop=False)
                        mm = pe.matmul(o, m[:, 3, k, :], st[:, 1, l, :], start=False, stop=True)
                    mm.then_inc(y_mm, 1)
                    ny += 1

        @block.scalar
        def _(act):
            nb = ny = 0
            for n, (s, q, e) in enumerate(order):
                if s == 0:
                    act.wait_ge(b_mm, nb + 1)
                    if e == 0 and q >= 1:
                        act.wait_ge(step_a, 4 * q)
                    for i in range(2):
                        act.activation(bs[:, i, 2 * e:2 * e + 2, :], p_b[i][nb % 2][:, :, :], ACT.Copy).then_inc(b_out, 1)
                    nb += 1
                else:
                    act.wait_ge(y_mm, ny + 1)
                    if e == 0 and q >= 2:
                        act.wait_ge(y_st[q % 2], 16 * LCH * (q // 2))
                    act.activation(y[:, q % 2, 2 * e:2 * e + 2, :], p_y[ny % 2][:, :, :], ACT.Copy).then_inc(y_out, 1)
                    ny += 1

        @block.vector
        def _(dve):
            link = Chain(dve, step)
            link(dve.memset(ones[:, :], 1.0))
            for q in range(GS):
                c, s = rot[:, q % 2, 0, :, :], rot[:, q % 2, 1, :, :]
                dve.wait_ge(rot_in[q % 2], 16 * (q // 2 + 1))
                for e in range(SC):
                    dve.tensor_scalar(dk[:, e, :], ones[:, :], decay[:, SC * q + e:SC * q + e + 1], None, ALU.mult).then_inc(step, 1)
                link.n += SC
                dve.wait_ge(step, link.n)
                link(dve.memset(dk[:, :, 0:1], 0.0))
                dve.wait_ge(b_out, 2 * NPAIR * (q + 1))
                dve.tensor_tensor(tmp[:, 0, :, :], bs[:, 0, :, :], c, ALU.mult).then_inc(step_a, 1)
                dve.tensor_tensor(tmp[:, 1, :, :], bs[:, 1, :, :], s, ALU.mult).then_inc(step_a, 1)
                dve.tensor_tensor(tmp[:, 2, :, :], bs[:, 1, :, :], c, ALU.mult).then_inc(step_a, 1)
                dve.tensor_tensor(tmp[:, 3, :, :], bs[:, 0, :, :], s, ALU.mult).then_inc(step_a, 1)
                dve.wait_ge(step_a, 4 * (q + 1))
                dve.tensor_tensor(tmp[:, 0, :, :], tmp[:, 0, :, :], tmp[:, 1, :, :], ALU.add).then_inc(step, 1)
                dve.tensor_tensor(tmp[:, 2, :, :], tmp[:, 2, :, :], tmp[:, 3, :, :], ALU.subtract).then_inc(step, 1)
                link.n += 2
                dve.wait_ge(step, link.n)
                flat = lambda t: t.rearrange("p g m -> p (g m)")
                for i in range(2):
                    dve.tensor_tensor_scan(flat(xs[:, i, :, :]), flat(dk[:, :, :]), flat(tmp[:, 2 * i, :, :]),
                                           0.0, ALU.mult, ALU.add).then_inc(step, 1)
                link.n += 2
                dve.wait_ge(step, link.n)
                w = slice(L0, L0 + NCL)
                x0, x1, cw, sw = xs[:, 0, :, w], xs[:, 1, :, w], c[:, :, w], s[:, :, w]
                t = [tmp[:, i, :, 0:NCL] for i in range(4)]
                for o, a, r in ((0, x0, cw), (1, x1, sw), (2, x1, cw), (3, x0, sw)):
                    dve.tensor_tensor(t[o], a, r, ALU.mult).then_inc(step, 1)
                link.n += 4
                dve.wait_ge(step, link.n)
                if q >= 1:
                    dve.wait_ge(y_mm, NPAIR * q)
                for r, back in ((slice(0, 64), 1), (slice(64, P), -1)):
                    dve.tensor_tensor(st[r, 0, :, ::back], t[0][r], t[1][r], ALU.subtract).then_inc(step, 1)
                    dve.tensor_tensor(st[r, 1, :, ::back], t[2][r], t[3][r], ALU.add).then_inc(step, 1)
                link.n += 4
                dve.wait_ge(step, link.n)
                dve.sem_inc(st_ready, 1)

    NT = W5 // P
    with Phase(nc, "glu") as ph:
        yT = ph.sb("yT", [P, NT, LCH, NCL])
        gT = ph.sb("gT", [P, NT, SEQ])
        w = ph.sb("w", [P, NT, W5])
        bias = ph.sb("bias", [P, NT])
        sg = ph.sb("sg", [P, 2, NCH])
        oT = ph.sb("oT", [P, NT, SEQ])
        stored = ph.sem("stored")
        pz = [ph.ps(f"pz{i}", [P, NCH]) for i in range(2)]
        y_in, w_in = [ph.sem(f"y_in{i}") for i in range(NT)], ph.sem("w_in")
        gelu_done, mm_done, sg_done, out_done = (ph.sem(s) for s in ("gelu_done", "mm_done", "sg_done", "out_done"))
        block = ph.block()

        @block.sync
        def _(sp):
            for i in range(NT):
                sp.dma_start(yT[:, i, :, :].rearrange("p j m -> p (j m)"), y_dram[i * P:(i + 1) * P, :]).then_inc(y_in[i], 16)
            sp.dma_start(w[:, :, :], w_glu.rearrange("(k p) n -> p k n", p=P)).then_inc(w_in, 16)
            sp.dma_start(bias[:, :], b_glu.rearrange("(k p) -> p k", p=P), allow_slow_non_contiguous=True).then_inc(w_in, 16)
            for i in range(NT):
                sp.wait_ge(out_done, 2 * i + 2)
                sp.dma_start(out_dram[i * P:(i + 1) * P, :], oT[:, i, :]).then_inc(stored, 16)
            sp.wait_ge(stored, 16 * NT)

        @block.scalar
        def _(act):
            for i in range(NT):
                act.wait_ge(y_in[i], 16)
                act.activation(gT[:, i, :].rearrange("p (m j) -> p j m", j=LCH), yT[:, i, :, :], ACT.Gelu_apprx_tanh).then_inc(gelu_done, 1)
            act.wait_ge(w_in, 32)
            for n in range(2 * NT):
                act.wait_ge(mm_done, n + 1)
                if n >= 2:
                    act.wait_ge(out_done, n - 1)
                act.activation(sg[:, n % 2, :], pz[n % 2][:, :], ACT.Sigmoid, bias=bias[:, n // 2:n // 2 + 1]).then_inc(sg_done, 1)

        @block.tensor
        def _(pe):
            pe.wait_ge(w_in, 32)
            pe.wait_ge(gelu_done, NT)
            for n in range(2 * NT):
                if n >= 2:
                    pe.wait_ge(sg_done, n - 1)
                for k in range(NT):
                    mm = pe.matmul(pz[n % 2][:, :], w[:, k, (n // 2) * P:(n // 2 + 1) * P], gT[:, k, (n % 2) * NCH:(n % 2 + 1) * NCH],
                                   start=k == 0, stop=k == NT - 1)
                mm.then_inc(mm_done, 1)

        @block.vector
        def _(dve):
            for n in range(2 * NT):
                dve.wait_ge(sg_done, n + 1)
                s = slice((n % 2) * NCH, (n % 2 + 1) * NCH)
                dve.tensor_tensor(oT[:, n // 2, s], sg[:, n % 2, :], gT[:, n // 2, s], ALU.mult).then_inc(out_done, 1)
            dve.wait_ge(out_done, 2 * NT)

NIDX = P + 3
PAD_ROWS = P
SCALE = 2.5


def residual(nc, tag, srcT, w, bias, gate, h, x=None, src_dram=None):
    with Phase(nc, tag) as ph:
        wb = ph.sb("w", [P, KD, D])
        row = ph.sb("row", [1, D]) if bias is not None else None
        ones = ph.sb("ones", [1, P])
        tmp = ph.sb("tmp", [P, 2, NCH])
        pz = [ph.ps(f"pz{i}", [P, NCH]) for i in range(4)]
        w_in, b_in, ones_done = [ph.sem(f"w_in{i}") for i in range(2)], ph.sem("b_in"), ph.sem("ones_done")
        x_in = ph.sem("x_in")
        s_in = ph.sem("s_in")
        mm_done, gated, added = ph.sem("mm_done"), ph.sem("gated"), ph.sem("added")
        jobs = [(t, n) for n in range(2) for t in range(TT)]
        w_v = w.rearrange("(k p) n -> p k n", p=P)
        block = ph.block()

        @block.sync
        def _(sp):
            if src_dram is not None:
                sp.dma_start(srcT[:, :, :], src_dram.rearrange("(k p) n -> p k n", p=P)).then_inc(s_in, 16)
            for n in range(2):
                sp.dma_start(wb[:, :, n * NCH:(n + 1) * NCH], w_v[:, :, n * NCH:(n + 1) * NCH]).then_inc(w_in[n], 16)
                if n == 0 and x is not None:
                    sp.dma_start(h[:, :, :], x.rearrange("(t p) d -> p t d", p=P)).then_inc(x_in, 16)
            if bias is not None:
                sp.dma_start(row[:, :], bias[None, :]).then_inc(b_in, 16)

        @block.tensor
        def _(pe):
            if src_dram is not None:
                pe.wait_ge(s_in, 16)
            if bias is not None:
                pe.wait_ge(b_in, 16)
                pe.wait_ge(ones_done, 1)
            for j, (t, n) in enumerate(jobs):
                pe.wait_ge(w_in[n], 16)
                if j >= 4:
                    pe.wait_ge(gated, j - 3)
                s = slice(n * NCH, (n + 1) * NCH)
                for k in range(KD):
                    mm = pe.matmul(pz[j % 4][:, :], srcT[:, k, t * P:(t + 1) * P], wb[:, k, s],
                                   start=k == 0, stop=k == KD - 1 and bias is None)
                if bias is not None:
                    mm = pe.matmul(pz[j % 4][:, :], ones[:, :], row[:, s], start=False, stop=True)
                mm.then_inc(mm_done, 1)

        @block.vector
        def _(dve):
            dve.memset(ones[:, :], 1.0).then_inc(ones_done, 1)
            if x is not None:
                dve.wait_ge(x_in, 16)
            for j, (t, n) in enumerate(jobs):
                dve.wait_ge(mm_done, j + 1)
                if j >= 2:
                    dve.wait_ge(added, j - 1)
                s = slice(n * NCH, (n + 1) * NCH)
                dve.tensor_tensor(tmp[:, j % 2, :], pz[j % 4][:, :], gate[:, s], ALU.mult).then_inc(gated, 1)
                dve.wait_ge(gated, j + 1)
                dve.tensor_tensor(h[:, t, s], h[:, t, s], tmp[:, j % 2, :], ALU.add).then_inc(added, 1)
            dve.wait_ge(added, len(jobs))


def route_and_share(nc, tag, ident, fT, w_router, r_bias, w_sg, w_su, w_sd, f_dram, acc_dram, idx, wslot, bounds, slot_of):
    with Phase(nc, tag) as ph:
        wr = ph.sb("wr", [P, KD, NE])
        rb = ph.sb("rb", [P, NE])
        wg = ph.sb("wg", [P, KD, FF])
        wu = ph.sb("wu", [P, KD, FF])
        wd = ph.sb("wd", [P, 2, D])
        zero = ph.sb("zero", [P, D])
        sil, up = ph.sb("sil", [P, 2, FF]), ph.sb("up", [P, 2, FF])
        hid, hidT = ph.sb("hid", [P, 2, FF]), ph.sb("hidT", [P, 2, 2, P])
        yo = ph.sb("yo", [P, 2, D])
        sc, sel, ms, mr, M = (ph.sb(s, [P, TT, NE]) for s in ("sc", "sel", "ms", "mr", "M"))
        t1, t2, gate, slot = (ph.sb(s, [P, TT, NE]) for s in ("t1", "t2", "gate", "slot"))
        gm = ph.sb("gm", [P, 8, TT, NG])
        low = ph.sb("low", [P, NG, NG])
        tri, ones, iota_f = ph.sb("tri", [P, P]), ph.sb("ones", [P, P]), ph.sb("iota_f", [P, P])
        iota_i = ph.sb("iota_i", [P, P], I32)
        col_i, col = ph.sb("col_i", [P, 1], I32), ph.sb("col", [P, 1])
        tok = ph.sb("tok", [P, TT])
        top = ph.sb("top", [P, TT, 8])
        s8, q8, r8, w8 = (ph.sb(s, [P, TT, TOPK]) for s in ("s8", "q8", "r8", "w8"))
        s8i, q8i, r8i = (ph.sb(s, [P, TT, TOPK], I32) for s in ("s8i", "q8i", "r8i"))
        den, rden = ph.sb("den", [P, TT]), ph.sb("rden", [P, TT])
        nbk = ph.sb("nbk", [P, 4, NE])
        thr = ph.sb("thr", [P, NE, KD])
        ebc, eb = ph.sb("ebc", [P, 2]), ph.sb("eb", [1, P], I32)
        HB = 2 * TOPK
        hot_r = ph.sb("hot_r", [P, HB, P])
        hot_q = ph.sb("hot_q", [P, HB, 2, P])
        tabf = ph.sb("tabf", [P, 2, P])
        p_l, p_pos = ph.ps("p_l", [P, TT, NE]), ph.ps("p_pos", [P, TT, NE])
        p_misc = ph.ps("p_misc", [P, NCH])
        p_g, p_u, p_h = ph.ps("p_g", [P, NCH]), ph.ps("p_u", [P, NCH]), ph.ps("p_h", [P, NCH])
        p_d = [ph.ps(f"p_d{i}", [P, NCH]) for i in range(2)]
        got_r, got_w, got_b = ph.sem("got_r"), ph.sem("got_w"), ph.sem("got_b")
        zeroed, zero_out, consts, made, step = (ph.sem(s) for s in ("zeroed", "zero_out", "consts", "made", "step"))
        logits, scored, masked, counted, placed = (ph.sem(s) for s in ("logits", "scored", "masked", "counted", "placed"))
        hot_ready, hot_row, slots_ready, hot_mm, eb_ready, eb_mm, tri_ready, ones_ready = (ph.sem(s) for s in ("hot_ready", "hot_row", "slots_ready", "hot_mm", "eb_ready", "eb_mm", "tri_ready", "ones_ready"))
        gu_done, sil_done, hid_ready, h_tr, h_out, d_done, y_ready = (ph.sem(s) for s in ("gu_done", "sil_done", "hid_ready", "h_tr", "h_out", "d_done", "y_ready"))
        y_st = [ph.sem(f"y_st{i}") for i in range(2)]
        block = ph.block()

        @block.sync
        def _(sp):
            sp.dma_start(wr[:, :, :], w_router.rearrange("(p k) e -> p k e", k=KD)).then_inc(got_r, 16)
            sp.dma_start(rb[:, :], r_bias[None, :].to_broadcast([P, NE])).then_inc(got_b, 16)
            sp.dma_start(wg[:, :, :], w_sg.rearrange("(p k) f -> p k f", k=KD)).then_inc(got_w, 16)
            sp.dma_start(wu[:, :, :], w_su.rearrange("(p k) f -> p k f", k=KD)).then_inc(got_w, 16)
            sp.dma_start(wd[:, :, :], w_sd.rearrange("(j p) n -> p j n", p=P)).then_inc(got_w, 16)
            sp.wait_ge(zeroed, 1)
            sp.dma_start(f_dram[SEQ:SEQ + PAD_ROWS, :], zero[:, :]).then_inc(zero_out, 16)
            sp.dma_start(acc_dram[SEQ:SEQ + PAD_ROWS, :], zero[:, :]).then_inc(zero_out, 16)
            for t in range(TT):
                sp.wait_ge(y_ready, 2 * t + 2)
                sp.dma_start(acc_dram[t * P:(t + 1) * P, :], yo[:, t % 2, :]).then_inc(y_st[t % 2], 16)
            sp.wait_ge(zero_out, 32)
            for i in range(2):
                sp.wait_ge(y_st[i], 16 * TT // 2)

        @block.gpsimd
        def _(pool):
            pool.memset(zero[:, :], 0.0).then_inc(zeroed, 1)
            pool.memset(ones[:, :], 1.0).then_inc(ones_ready, 1)
            pool.memset(tri[:, :], 1.0).then_inc(made, 1)
            pool.memset(low[:, :, :], 1.0).then_inc(made, 1)
            pool.iota(iota_i[:, :], [[1, P]], base=0, channel_multiplier=0).then_inc(consts, 1)
            pool.iota(col_i[:, :], [[0, 1]], base=0, channel_multiplier=1).then_inc(consts, 1)
            pool.wait_ge(made, 2)
            pool.affine_select(out=tri[:, :], in_=tri[:, :], compare_op=ALU.is_gt, fill=0.0, base=0,
                               pattern=[[1, P]], channel_multiplier=-1).then_inc(tri_ready, 1)
            pool.affine_select(out=low[:, :, :], in_=low[:, :, :], compare_op=ALU.is_gt, fill=0.0, base=0,
                               pattern=[[1, NG], [-1, NG]], channel_multiplier=0).then_inc(consts, 1)
            for t in range(TT):
                pool.wait_ge(sil_done, 2 * t + 2)
                if t >= 2:
                    pool.wait_ge(h_tr, t - 1)
                pool.tensor_tensor(hid[:, t % 2, :], sil[:, t % 2, :], up[:, t % 2, :], ALU.mult).then_inc(hid_ready, 1)
                if t >= TT // 2:
                    pool.wait_ge(slots_ready, 1)
                    n = TT * TOPK // (TT // 2)
                    for j in range((t - TT // 2) * n, (t - TT // 2 + 1) * n):
                        if j >= HB:
                            pool.wait_ge(hot_mm, j - HB + 1)
                        pool.tensor_scalar(hot_r[:, j % HB, :], iota_f[:, :], r8[:, j // TOPK, j % TOPK:j % TOPK + 1], None, ALU.is_equal).then_inc(hot_row, 1)

        @block.tensor
        def _(pe):
            pe.wait_ge(got_r, 16)
            for t in range(TT):
                for k in range(KD):
                    mm = pe.matmul(p_l[:, t, :], fT[:, k, t * P:(t + 1) * P], wr[:, k, :], start=k == 0, stop=k == KD - 1)
            mm.then_inc(logits, 1)
            pe.wait_ge(got_w, 48)

            def gate_up(t):
                if t >= 1:
                    pe.wait_ge(sil_done, 2 * t)
                for k in range(KD):
                    pe.matmul(p_g[:, 0:FF], fT[:, k, t * P:(t + 1) * P], wg[:, k, :], start=k == 0, stop=k == KD - 1)
                for k in range(KD):
                    mm = pe.matmul(p_u[:, 0:FF], fT[:, k, t * P:(t + 1) * P], wu[:, k, :], start=k == 0, stop=k == KD - 1)
                mm.then_inc(gu_done, 1)

            def turn(t):
                pe.wait_ge(hid_ready, t + 1)
                if t >= 1:
                    pe.wait_ge(h_out, t)
                for j in range(2):
                    tr = pe.transpose(p_h[:, j * P:(j + 1) * P], hid[:, t % 2, j * P:(j + 1) * P], ident[:, :])
                tr.then_inc(h_tr, 1)

            def down(t):
                pe.wait_ge(h_out, t + 1)
                for n in range(2):
                    if t >= 1:
                        pe.wait_ge(y_ready, 2 * (t - 1) + n + 1)
                    for j in range(2):
                        mm = pe.matmul(p_d[n][:, :], hidT[:, t % 2, j, :], wd[:, j, n * NCH:(n + 1) * NCH], start=j == 0, stop=j == 1)
                    mm.then_inc(d_done, 1)

            def positions():
                pe.wait_ge(ones_ready, 1)
                pe.wait_ge(tri_ready, 1)
                pe.wait_ge(masked, 1)
                for t in range(TT):
                    mm = pe.matmul(p_misc[:, 0:NE], ones[:, :], M[:, t, :], start=t == 0, stop=t == TT - 1)
                mm.then_inc(counted, 1)
                for t in range(TT):
                    for s in range(t):
                        pe.matmul(p_pos[:, t, :], ones[:, :], M[:, s, :], start=s == 0, stop=False)
                    mm = pe.matmul(p_pos[:, t, :], tri[:, :], M[:, t, :], start=t == 0, stop=True)
                mm.then_inc(placed, 1)

            def tables(part):
                n = TT * TOPK // (TT // 2)
                for j in range(part * n, (part + 1) * n):
                    pe.wait_ge(hot_row, j + 1)
                    pe.wait_ge(hot_ready, 2 * (j + 1))
                    mm = pe.matmul(p_l[:, 0:4, :].rearrange("p a e -> p (a e)"), hot_r[:, j % HB, :], hot_q[:, j % HB, :, :].rearrange("p a b -> p (a b)"),
                                   start=j == 0, stop=j == TT * TOPK - 1)
                    mm.then_inc(hot_mm, 1)

            for t in range(TT):
                gate_up(t)
                if t >= 1:
                    down(t - 1)
                turn(t)
                if t == 1:
                    positions()
                if t >= TT // 2:
                    tables(t - TT // 2)
            down(TT - 1)
            pe.wait_ge(eb_ready, 1)
            pe.matmul(p_pos[0:1, 0:2, :].rearrange("p a e -> p (a e)"), ebc[:, 0:1], ident[:, :], start=True, stop=True).then_inc(eb_mm, 1)

        @block.scalar
        def _(act):
            act.wait_ge(logits, 1)
            act.activation(sc[:, :, :], p_l[:, :, :], ACT.Sigmoid).then_inc(scored, 1)
            for t in range(TT + 1):
                if t < TT:
                    act.wait_ge(gu_done, t + 1)
                    if t >= 2:
                        act.wait_ge(hid_ready, t - 1)
                    act.activation(sil[:, t % 2, :], p_g[:, 0:FF], ACT.Silu).then_inc(sil_done, 1)
                    act.activation(up[:, t % 2, :], p_u[:, 0:FF], ACT.Copy).then_inc(sil_done, 1)
                if t >= 1:
                    for n in range(2):
                        act.wait_ge(d_done, 2 * (t - 1) + n + 1)
                        if t >= 3 and n == 0:
                            act.wait_ge(y_st[(t - 1) % 2], 16 * ((t - 1) // 2))
                        act.activation(yo[:, (t - 1) % 2, n * NCH:(n + 1) * NCH], p_d[n][:, :], ACT.Copy).then_inc(y_ready, 1)
                if t < TT:
                    act.wait_ge(h_tr, t + 1)
                    act.activation(hidT[:, t % 2, :, :], p_h[:, 0:2 * P].rearrange("p (j c) -> p j c", j=2), ACT.Copy).then_inc(h_out, 1)

        @block.vector
        def _(dve):
            link = Chain(dve, step)
            dve.wait_ge(consts, 3)
            link(dve.tensor_copy(iota_f[:, :], iota_i[:, :]))
            link(dve.tensor_copy(col[:, :], col_i[:, :]))
            for t in range(TT):
                link(dve.tensor_scalar(tok[:, t:t + 1], col[:, :], float(t * P + 1), None, ALU.add))
                link(dve.memset(thr[:, :, t], float(t * P)))
            dve.wait_ge(got_b, 16)
            dve.wait_ge(scored, 1)
            link(dve.tensor_tensor(sel[:, :, :], sc[:, :, :], rb[:, None, :].to_broadcast([P, TT, NE]), ALU.add))
            g64 = lambda t: t[:, :, :].rearrange("p t (g e) -> p (t g) e", e=EG)
            col64 = lambda i: gm[:, i, :, :].rearrange("p t g -> p (t g)")
            bc64 = lambda i: col64(i)[:, :, None].to_broadcast([P, TT * NG, EG])
            link(dve.tensor_reduce(col64(0), g64(sel), AX.X, ALU.max))
            link(dve.tensor_tensor(g64(t1), g64(sel), bc64(0), ALU.is_equal))
            link(dve.tensor_reduce(col64(1), g64(t1), AX.X, ALU.add))
            link(dve.scalar_tensor_tensor(t2[:, :, :], t1[:, :, :], NEG, sel[:, :, :], ALU.mult, ALU.add))
            link(dve.tensor_reduce(col64(2), g64(t2), AX.X, ALU.max))
            link(dve.tensor_scalar(col64(3), col64(1), 1.5, -2 * NEG, ALU.is_gt, ALU.mult))
            link(dve.tensor_scalar(col64(3), col64(3), NEG, None, ALU.add))
            link(dve.tensor_tensor(col64(2), col64(2), col64(3), ALU.max))
            link(dve.tensor_tensor(col64(2), col64(2), col64(0), ALU.min))
            link(dve.tensor_tensor(col64(4), col64(0), col64(2), ALU.add))
            other = gm[:, 4, :, None, :].to_broadcast([P, TT, NG, NG])
            own = gm[:, 4, :, :, None].to_broadcast([P, TT, NG, NG])
            sq = lambda t: t[:, :, :].rearrange("p t (g e) -> p t g e", e=NG)
            link(dve.tensor_tensor(sq(t1), other, own, ALU.is_gt))
            link(dve.tensor_tensor(sq(t2), other, own, ALU.is_equal))
            link(dve.tensor_tensor(sq(t2), sq(t2), low[:, None, :, :].to_broadcast([P, TT, NG, NG]), ALU.mult))
            link(dve.tensor_tensor(t1[:, :, :], t1[:, :, :], t2[:, :, :], ALU.add))
            link(dve.tensor_reduce(col64(5), g64(t1), AX.X, ALU.add))
            link(dve.tensor_scalar(col64(6), col64(5), TOPG - 0.5, None, ALU.is_lt))
            link(dve.tensor_scalar(col64(7), col64(6), 1.0, -NEG, ALU.subtract, ALU.mult))
            link(dve.tensor_tensor(g64(ms), g64(sel), bc64(6), ALU.mult))
            link(dve.tensor_tensor(g64(ms), g64(ms), bc64(7), ALU.add))
            for t in range(TT):
                dve.max(top[:, t, :], ms[:, t, :]).then_inc(step, 1)
            link.n += TT
            dve.wait_ge(step, link.n)
            for t in range(TT):
                dve.match_replace(mr[:, t, :], top[:, t, :], ms[:, t, :], -3e38).then_inc(step, 1)
            link.n += TT
            dve.wait_ge(step, link.n)
            link(dve.tensor_tensor(M[:, :, :], mr[:, :, :], ms[:, :, :], ALU.not_equal))
            dve.sem_inc(masked, 1)
            link(dve.tensor_tensor(t1[:, :, :], M[:, :, :], sc[:, :, :], ALU.mult))
            link(dve.tensor_reduce(den[:, :], t1[:, :, :], AX.X, ALU.add))
            link(dve.reciprocal(rden[:, :], den[:, :]))
            link(dve.scalar_tensor_tensor(gate[:, :, :], t1[:, :, :], SCALE, rden[:, :, None].to_broadcast([P, TT, NE]), ALU.mult, ALU.mult))
            dve.wait_ge(counted, 1)
            link(dve.tensor_copy(nbk[:, 0, :], p_misc[:, 0:NE]))
            th = t2[:, :, :].rearrange("p t e -> p (t e)").rearrange("p (e j) -> p e j", j=KD)
            link(dve.tensor_tensor(th, nbk[:, 0, :, None].to_broadcast([P, NE, KD]), thr[:, :, :], ALU.is_gt))
            link(dve.tensor_reduce(nbk[:, 1, :], th, AX.X, ALU.add))
            link(dve.tensor_scalar(nbk[:, 1, :], nbk[:, 1, :], 1.0, None, ALU.max))
            link(dve.tensor_tensor_scan(nbk[:, 2, :], ones[:, 0:NE], nbk[:, 1, :], 0.0, ALU.mult, ALU.add))
            link(dve.tensor_tensor(nbk[:, 3, :], nbk[:, 2, :], nbk[:, 1, :], ALU.subtract))
            link(dve.tensor_scalar(nbk[:, 3, :], nbk[:, 3, :], float(P), None, ALU.mult))
            link(dve.tensor_scalar(t1[:, 0, :], nbk[:, 2, :], col[:, 0:1], None, ALU.is_lt))
            link(dve.tensor_reduce(ebc[:, 1:2], t1[:, 0, :], AX.X, ALU.add))
            link(dve.tensor_scalar(ebc[:, 0:1], ebc[:, 1:2], float(NE - 1), None, ALU.min))
            dve.sem_inc(eb_ready, 1)
            link(dve.memset(bounds[0:1, 0:1], 0))
            link(dve.tensor_copy(bounds[0:1, 1:NE + 1], nbk[0:1, 2, :]))
            dve.wait_ge(placed, 1)
            link(dve.tensor_tensor(slot[:, :, :], p_pos[:, :, :], nbk[:, 3, None, :].to_broadcast([P, TT, NE]), ALU.add))
            link(dve.scalar_tensor_tensor(slot[:, :, :], slot[:, :, :], 1.0, M[:, :, :], ALU.add, ALU.mult))
            for t in range(TT):
                dve.max(s8[:, t, :], slot[:, t, :]).then_inc(step, 1)
            link.n += TT
            dve.wait_ge(step, link.n)
            for t in range(TT):
                sh = [P, TOPK, NE]
                link(dve.tensor_tensor(t1[:, :, :], slot[:, t, None, :].to_broadcast(sh), s8[:, t, :, None].to_broadcast(sh), ALU.is_equal))
                link(dve.tensor_tensor(t1[:, :, :], t1[:, :, :], gate[:, t, None, :].to_broadcast(sh), ALU.mult))
                link(dve.tensor_reduce(w8[:, t, :], t1[:, :, :], AX.X, ALU.add))
            link(dve.tensor_scalar(s8[:, :, :], s8[:, :, :], 1.0, None, ALU.subtract))
            link(dve.tensor_copy(s8i[:, :, :], s8[:, :, :]))
            link(dve.tensor_scalar(q8i[:, :, :], s8i[:, :, :], 7, None, ALU.logical_shift_right))
            link(dve.tensor_scalar(r8i[:, :, :], s8i[:, :, :], P - 1, None, ALU.bitwise_and))
            link(dve.tensor_copy(q8[:, :, :], q8i[:, :, :]))
            link(dve.tensor_copy(r8[:, :, :], r8i[:, :, :]))
            dve.sem_inc(slots_ready, 1)
            for j in range(TT * TOPK):
                t, k = j // TOPK, j % TOPK
                if j >= HB:
                    dve.wait_ge(hot_mm, j - HB + 1)
                dve.tensor_scalar(hot_q[:, j % HB, 0, :], iota_f[:, :], q8[:, t, k:k + 1], tok[:, t:t + 1], ALU.is_equal, ALU.mult).then_inc(hot_ready, 1)
                dve.tensor_scalar(hot_q[:, j % HB, 1, :], iota_f[:, :], q8[:, t, k:k + 1], w8[:, t, k:k + 1], ALU.is_equal, ALU.mult).then_inc(hot_ready, 1)
            dve.wait_ge(hot_mm, TT * TOPK)
            tab = p_l[:, 0:4, :].rearrange("p a e -> p (a e)")
            link(dve.tensor_copy(wslot[:, 0:P], tab[:, P:2 * P]))
            link(dve.tensor_copy(tabf[:, 0, :], tab[:, 0:P]))
            link(dve.tensor_scalar(col[:, :], col[:, :], float(SEQ + 1), None, ALU.add))
            link(dve.tensor_scalar(tabf[:, 1, :], tabf[:, 0, :], 0.5, col[:, 0:1], ALU.is_lt, ALU.mult))
            link(dve.scalar_tensor_tensor(tabf[:, 0, :], tabf[:, 0, :], 1.0, tabf[:, 1, :], ALU.subtract, ALU.add))
            link(dve.tensor_copy(idx[:, 1:P + 1], tabf[:, 0, :]))
            link(dve.tensor_scalar(tabf[:, 1, 0:1], col[:, :], 1.0, None, ALU.subtract))
            for j in (0, P + 1, P + 2):
                link(dve.tensor_copy(idx[:, j:j + 1], tabf[:, 1, 0:1]))
            dve.wait_ge(eb_mm, 1)
            link(dve.tensor_copy(eb[0:1, :], p_pos[0:1, 0:2, :].rearrange("p a e -> p (a e)")))
            link(dve.tensor_scalar(slot_of[0:1, :], eb[0:1, :], 1, None, ALU.bitwise_and))


def experts(nc, tag, w_gate, w_up, w_down, f_dram, acc_dram, ident, idx, wslot, bounds, slot_of):
    QG, QD = 4, 2
    KP = KD // QG
    with Phase(nc, tag) as ph:
        raw = ph.sb("raw", [P, KD, 2 * FF])
        raw_d = ph.sb("raw_d", [P, 2, D])
        wh, wl = ph.sb("wh", [P, 2, KD, 2 * FF], F32R), ph.sb("wl", [P, 2, KD, 2 * FF], F32R)
        dh, dl = ph.sb("dh", [P, 2, 2, D], F32R), ph.sb("dl", [P, 2, 2, D], F32R)
        xg = ph.sb("xg", [P, D])
        xh, xl = ph.sb("xh", [P, KD, P], F32R), ph.sb("xl", [P, KD, P], F32R)
        sil, hid = ph.sb("sil", [P, FF]), ph.sb("hid", [P, FF])
        hh, hl = ph.sb("hh", [P, 2, P], F32R), ph.sb("hl", [P, 2, P], F32R)
        hz = ph.sb("hz", [P, 2, P])
        yo = ph.sb("yo", [P, D])
        ig, isc = ph.sb("ig", [P, 1], U32), ph.sb("isc", [P, 1], U32)
        p_x = [ph.ps(f"p_x{i}", [P, 4, P]) for i in range(2)]
        p_gu, p_h = ph.ps("p_gu", [P, NCH]), ph.ps("p_h", [P, 2, P])
        p_d = [ph.ps(f"p_d{i}", [P, NCH]) for i in range(2)]
        gu_in, d_in = [ph.sem(f"gu_in{i}") for i in range(2)], ph.sem("d_in")
        gu_head, gu_split, d_head, d_split = (ph.sem(s) for s in ("gu_head", "gu_split", "d_head", "d_split"))
        x_in, x_tr, x_head, x_split = (ph.sem(s) for s in ("x_in", "x_tr", "x_head", "x_split"))
        gu_mm, sil_done, hid_done, h_tr, h_head, h_split = (ph.sem(s) for s in ("gu_mm", "sil_done", "hid_done", "h_tr", "h_head", "h_split"))
        zero_h, d_mm, y_act, y_dve, added = (ph.sem(s) for s in ("zero_h", "d_mm", "y_act", "y_dve", "added"))
        y_free, tick, copied = ph.sem("y_free"), ph.sem("tick"), ph.sem("copied")
        block = ph.block()

        def bound(eng, e):
            return eng.value_load(bounds[0:1, e:e + 1] if isinstance(e, int) else bounds[0:1, bass.ds(e, 1)], min_val=0, max_val=P - 1)

        def each_expert(eng, body):
            with eng.Fori(0, NE // 2 - 1) as i:
                for u in range(2):
                    body(i * 2 + u, u, True)
            body(NE - 2, 0, True)
            body(NE - 1, 1, False)

        @block.sync
        def _(sp):
            def load_d(e):
                w = w_down[e:e + 1] if isinstance(e, int) else w_down[bass.ds(e, 1), :, :]
                sp.dma_start(raw_d[:, :, :], w.rearrange("a (j p) n -> p (a j) n", p=P)).then_inc(d_in, 16)

            def load_gu(e, half):
                for i, w in enumerate((w_gate, w_up)):
                    w = w[e:e + 1] if isinstance(e, int) else w[bass.ds(e, 1), :, :]
                    ks = slice(half * KD // 2, (half + 1) * KD // 2)
                    sp.dma_start(raw[:, ks, i * FF:(i + 1) * FF],
                                 w.rearrange("a (p k) f -> p (a k) f", k=KD)[:, ks, :]).then_inc(gu_in[half], 16)

            for half in range(2):
                load_gu(0, half)
            load_d(0)

            def refill(e):
                for half in range(2):
                    sp.wait_ge(gu_split, e * QG - QG + (half + 1) * QG // 2)
                    load_gu(e, half)
                sp.wait_ge(d_split, e * QD)
                load_d(e)

            with sp.Fori(1, NE) as e:
                refill(e)

        @block.gpsimd
        def _(pool):
            blocks = bound(pool, NE)

            def gather(n, count):
                if not isinstance(n, int) or n > 0:
                    pool.wait_ge(x_tr, n)
                    pool.sem_inc(tick, 1)
                c = idx[:, n + 1:n + 2] if isinstance(n, int) else idx[:, bass.ds(n + 1, 1)]
                pool.tensor_copy(ig[:, :], c).then_inc(copied, 1)
                pool.wait_ge(copied, count)
                pool.sem_inc(tick, 1)
                pool.indirect_dma_start(xg[:, :], None, f_dram, bass.IndirectOffsetOnAxis(ap=ig[:, :], axis=0)).then_inc(x_in, 16)

            def scatter(n, count):
                if not isinstance(n, int):
                    pool.wait_ge(added, n * 16)
                pool.sem_inc(y_free, 1)
                pool.tensor_copy(isc[:, :], idx[:, n:n + 1] if isinstance(n, int) else idx[:, bass.ds(n, 1)]).then_inc(copied, 1)
                pool.wait_ge(copied, count)
                pool.sem_inc(tick, 1)
                pool.wait_ge(y_act, n + 2)
                pool.sem_inc(tick, 1)
                pool.wait_ge(y_dve, n + 2)
                pool.sem_inc(tick, 1)
                pool.indirect_dma_start(acc_dram, bass.IndirectOffsetOnAxis(ap=isc[:, :], axis=0), yo[:, :], None,
                                        compute_op=ALU.add).then_inc(added, 16)

            pool.memset(hz[:, :, :], 0.0).then_inc(zero_h, 1)
            gather(0, 1)
            gather(1, 2)
            gather(2, 3)
            scatter(0, 4)
            with pool.Fori(1, blocks) as n:
                gather(n + 2, n * 2 + 3)
                scatter(n, n * 2 + 4)
            scatter(pool.snap(blocks * 1), blocks * 2 + 3)
            pool.wait_ge(added, blocks * 16 + 16)
            pool.wait_ge(x_in, blocks * 16 + 32)
            pool.sem_inc(tick, 1)

        @block.tensor
        def _(pe):
            def turn_x(n):
                pe.wait_ge(x_in, n * 16 + 16)
                for k in range(KD):
                    tr = pe.transpose(p_x[k // 4][:, k % 4, :], xg[:, k * P:(k + 1) * P], ident[:, :])
                tr.then_inc(x_tr, 1)

            def gate_up(n, u):
                pe.wait_ge(x_split, n * 2 + 2)
                pe.wait_ge(hid_done, n + 1)
                for k in range(KD):
                    pe.matmul(p_gu[:, :], xh[:, k, :], wh[:, u, k, :], start=k == 0, stop=False)
                    pe.matmul(p_gu[:, :], xh[:, k, :], wl[:, u, k, :], start=False, stop=False)
                    mm = pe.matmul(p_gu[:, :], xl[:, k, :], wh[:, u, k, :], start=False, stop=k == KD - 1)
                mm.then_inc(gu_mm, 1)

            def turn_h(n):
                pe.wait_ge(hid_done, n + 2)
                for j in range(2):
                    tr = pe.transpose(p_h[:, j, :], hid[:, j * P:(j + 1) * P], ident[:, :])
                tr.then_inc(h_tr, 1)

            def down(n, u):
                pe.wait_ge(h_split, n + 1)
                pe.wait_ge(y_act, n + 1)
                pe.wait_ge(y_dve, n + 1)
                pick = lambda t, j, c: t[:, u, j, c * NCH:(c + 1) * NCH] if isinstance(u, int) else t[:, bass.ds(u, 1), j, c * NCH:(c + 1) * NCH]
                for c in range(2):
                    for j in range(2):
                        pe.matmul(p_d[c][:, :], hh[:, j, :], pick(dh, j, c), start=j == 0, stop=False)
                        pe.matmul(p_d[c][:, :], hh[:, j, :], pick(dl, j, c), start=False, stop=False)
                        mm = pe.matmul(p_d[c][:, :], hl[:, j, :], pick(dh, j, c), start=False, stop=j == 1)
                    mm.then_inc(d_mm, 1)

            def expert(e, u, more):
                first, end = bound(pe, e), bound(pe, e + 1)
                with pe.Fori(first, end) as n:
                    before = pe.value_load(slot_of[0:1, bass.ds(n, 1)], min_val=0, max_val=1)
                    pe.wait_ge(gu_split, e * QG + QG)
                    gate_up(n, u)
                    turn_x(n + 1)
                    pe.wait_ge(d_split, e * QD + QD)
                    down(n, before)
                    turn_h(n)

            turn_x(0)
            each_expert(pe, expert)
            down(bound(pe, NE), (NE - 1) % 2)

        @block.scalar
        def _(act):
            def head_gu(e, u):
                for q in range(QG):
                    if q % (QG // 2) == 0:
                        act.wait_ge(gu_in[q // (QG // 2)], e * 32 + 32)
                    act.activation(wh[:, u, q * KP:(q + 1) * KP, :], raw[:, q * KP:(q + 1) * KP, :], ACT.Copy).then_inc(gu_head, 1)

            def head_d(e, u):
                act.wait_ge(d_in, e * 16 + 16)
                for q in range(QD):
                    act.activation(dh[:, u, q, :], raw_d[:, q, :], ACT.Copy).then_inc(d_head, 1)

            def head_x(n):
                act.wait_ge(x_tr, n + 1)
                for i in range(2):
                    act.activation(xh[:, 4 * i:4 * i + 4, :], p_x[i][:, :, :], ACT.Copy).then_inc(x_head, 1)

            def out(n):
                act.wait_ge(d_mm, n * 2 + 1)
                act.wait_ge(y_free, n + 1)
                act.activation(yo[:, 0:NCH], p_d[0][:, :], ACT.Copy).then_inc(y_act, 1)

            def expert(e, u, more):
                head_d(e, u)
                if more:
                    head_gu(e + 1, 1 - u)
                first, end = bound(act, e), bound(act, e + 1)
                with act.Fori(first, end) as n:
                    act.wait_ge(gu_mm, n + 1)
                    act.activation(sil[:, :], p_gu[:, 0:FF], ACT.Silu).then_inc(sil_done, 1)
                    head_x(n + 1)
                    out(n)
                    act.wait_ge(h_tr, n + 1)
                    act.activation(hh[:, :, :], p_h[:, :, :], ACT.Copy).then_inc(h_head, 1)

            act.sem_inc(y_act, 1)
            act.wait_ge(zero_h, 1)
            act.activation(hh[:, :, :], hz[:, :, :], ACT.Copy).then_inc(h_head, 1)
            head_x(0)
            head_gu(0, 0)
            each_expert(act, expert)
            out(bound(act, NE))

        @block.vector
        def _(dve):
            def rest_gu(e, u):
                for q in range(QG):
                    s = slice(q * KP, (q + 1) * KP)
                    dve.wait_ge(gu_head, e * QG + q + 1)
                    dve.tensor_tensor(wl[:, u, s, :], raw[:, s, :], wh[:, u, s, :], ALU.subtract).then_inc(gu_split, 1)

            def rest_d(e, u):
                for q in range(QD):
                    dve.wait_ge(d_head, e * QD + q + 1)
                    dve.tensor_tensor(dl[:, u, q, :], raw_d[:, q, :], dh[:, u, q, :], ALU.subtract).then_inc(d_split, 1)

            def rest_x(n):
                for i in range(2):
                    dve.wait_ge(x_head, n * 2 + i + 1)
                    dve.tensor_tensor(xl[:, 4 * i:4 * i + 4, :], p_x[i][:, :, :], xh[:, 4 * i:4 * i + 4, :], ALU.subtract).then_inc(x_split, 1)

            def out(n):
                dve.wait_ge(d_mm, n * 2 + 2)
                dve.wait_ge(y_free, n + 1)
                dve.tensor_copy(yo[:, NCH:D], p_d[1][:, :]).then_inc(y_dve, 1)

            def expert(e, u, more):
                rest_d(e, u)
                if more:
                    rest_gu(e + 1, 1 - u)
                first, end = bound(dve, e), bound(dve, e + 1)
                with dve.Fori(first, end) as n:
                    dve.wait_ge(sil_done, n + 1)
                    dve.scalar_tensor_tensor(hid[:, :], sil[:, :], wslot[:, bass.ds(n, 1)], p_gu[:, FF:2 * FF], ALU.mult, ALU.mult).then_inc(hid_done, 1)
                    rest_x(n + 1)
                    out(n)
                    dve.wait_ge(h_head, n + 2)
                    dve.tensor_tensor(hl[:, :, :], p_h[:, :, :], hh[:, :, :], ALU.subtract).then_inc(h_split, 1)

            dve.sem_inc(y_dve, 1)
            dve.sem_inc(hid_done, 1)
            dve.wait_ge(h_head, 1)
            dve.tensor_tensor(hl[:, :, :], hz[:, :, :], hh[:, :, :], ALU.subtract).then_inc(h_split, 1)
            rest_x(0)
            rest_gu(0, 0)
            each_expert(dve, expert)
            out(bound(dve, NE))

FG = 4
FW = D // FG


def add_gated(nc, tag, acc_dram, gate, h, out=None):
    with Phase(nc, tag) as ph:
        a = ph.sb("a", [P, TT, D])
        a_in = [ph.sem(f"a_in{t}") for t in range(TT)]
        gated, added, stored = ph.sem("gated"), ph.sem("added"), ph.sem("stored")
        block = ph.block()

        @block.sync
        def _(sp):
            for t in range(TT):
                sp.dma_start(a[:, t, :], acc_dram[t * P:(t + 1) * P, :]).then_inc(a_in[t], 16)
            if out is not None:
                for t in range(TT):
                    sp.wait_ge(added, t + 1)
                    sp.dma_start(out[t * P:(t + 1) * P, :], h[:, t, :]).then_inc(stored, 16)
                sp.wait_ge(stored, 16 * TT)

        @block.vector
        def _(dve):
            for t in range(TT):
                dve.wait_ge(a_in[t], 16)
                dve.tensor_tensor(a[:, t, :], a[:, t, :], gate, ALU.mult).then_inc(gated, 1)
                dve.wait_ge(gated, t + 1)
                dve.tensor_tensor(h[:, t, :], h[:, t, :], a[:, t, :], ALU.add).then_inc(added, 1)
            dve.wait_ge(added, TT)


def fourier(nc, tag, aT, cs_feat, cos_tok, sin_tok, alt, fT):
    HT = SEQ // 2
    HK = HT // P
    with Phase(nc, tag) as ph:
        cf = ph.sb("cf", [P, 2, 2 * FW])
        odd = ph.sb("odd", [P, KD, HT])
        y = ph.sb("y", [P, HK, 2, D])
        mid = ph.sb("mid", [1, D])
        ct = ph.sb("ct", [P, HK, HT])
        st = ph.sb("st", [P, HK, HT])
        alt_row, alt_col = ph.sb("alt_row", [1, HT]), ph.sb("alt_col", [P, HK])
        one = ph.sb("one", [1, 1])
        py = [ph.ps(f"py{i}", [P, NCH]) for i in range(4)]
        pe_, po = ([ph.ps(f"{s}{i}", [P, NCH]) for i in range(2)] for s in ("even", "odd"))
        c_in, t_in = ph.sem("c_in"), ph.sem("t_in")
        odd_ready, even_ready, one_set = ph.sem("odd_ready"), ph.sem("even_ready"), ph.sem("one_set")
        y_mm, mid_mm, mid_out = ph.sem("y_mm"), ph.sem("mid_mm"), ph.sem("mid_out")
        copied = [ph.sem(f"copied{i}") for i in range(2)]
        z_mm, c_mm, even_out, sums, c_out = (ph.sem(s) for s in ("z_mm", "c_mm", "even_out", "sums", "c_out"))
        ev = ph.sb("ev", [P, 2, HT])
        jobs = [(t, g) for t in range(HK) for g in range(FG)]
        NJ = len(jobs)
        block = ph.block()

        @block.sync
        def _(sp):
            sp.dma_start(cf[:, :, :], cs_feat).then_inc(c_in, 16)
            for buf, src in ((ct, cos_tok), (st, sin_tok)):
                sp.dma_start(buf[:, :, :], src.rearrange("(k p) n -> p k n", p=P)).then_inc(t_in, 16)
            sp.dma_start(alt_row[:, :], alt[None, :]).then_inc(t_in, 16)
            sp.dma_start(alt_col[:, :], alt.rearrange("(k p) -> p k", p=P), allow_slow_non_contiguous=True).then_inc(t_in, 16)

        @block.gpsimd
        def _(pool):
            pool.memset(one[:, :], 1.0).then_inc(one_set, 1)

        @block.tensor
        def _(pe):
            pe.wait_ge(c_in, 16)
            for g in range(FG):
                for k in range(2):
                    mm = pe.matmul(py[g // 2][0:1, (g % 2) * FW:(g % 2 + 1) * FW], aT[:, 2 * g + k, HT:HT + 1], cf[:, k, 0:FW], start=k == 0, stop=k == 1)
            mm.then_inc(mid_mm, 1)
            for j, (t, g) in enumerate(jobs):
                pe.wait_ge(odd_ready, g + 1)
                pe.wait_ge(even_ready, g + 1)
                if j < 2:
                    pe.wait_ge(mid_out, 2)
                if j >= 4:
                    pe.wait_ge(copied[j % 2], (j - 4) // 2 + 1)
                for i, src in enumerate((aT, odd)):
                    for k in range(2):
                        mm = pe.matmul(py[j % 4][:, i * FW:(i + 1) * FW], src[:, 2 * g + k, t * P:(t + 1) * P], cf[:, k, i * FW:(i + 1) * FW],
                                       start=k == 0, stop=k == 1)
                mm.then_inc(y_mm, 1)
            for i in range(2):
                pe.wait_ge(copied[i], NJ // 2)
            pe.wait_ge(t_in, 64)
            pe.wait_ge(one_set, 1)
            for f in range(KD):
                fs = slice(f * P, (f + 1) * P)
                if f >= 2:
                    pe.wait_ge(even_out, f - 1)
                for k in range(HK):
                    pe.matmul(pe_[f % 2][:, :], y[:, k, 0, fs], ct[:, k, :], start=k == 0, stop=False)
                pe.matmul(pe_[f % 2][:, :], mid[:, fs], alt_row[:, :], start=False, stop=True).then_inc(z_mm, 1)
                if f >= 2:
                    pe.wait_ge(sums, 2 * (f - 1))
                for k in range(HK):
                    mm = pe.matmul(po[f % 2][:, :], y[:, k, 1, fs], st[:, k, :], start=k == 0, stop=k == HK - 1)
                mm.then_inc(z_mm, 1)
            for f in range(KD):
                fs = slice(f * P, (f + 1) * P)
                for k in range(HK):
                    pe.matmul(py[0][:, f:f + 1], y[:, k, 0, fs], alt_col[:, k:k + 1], start=k == 0, stop=False)
                mm = pe.matmul(py[0][:, f:f + 1], mid[:, fs], one[:, :], start=False, stop=True)
            mm.then_inc(c_mm, 1)

        @block.scalar
        def _(act):
            act.wait_ge(mid_mm, 1)
            for i in range(2):
                act.activation(mid[:, i * NCH:(i + 1) * NCH], py[i][0:1, :], ACT.Copy).then_inc(mid_out, 1)
            for j in range(0, NJ, 2):
                t, g = jobs[j]
                act.wait_ge(y_mm, j + 1)
                act.activation(y[:, t, :, g * FW:(g + 1) * FW], py[j % 4][:, :].rearrange("p (s f) -> p s f", s=2), ACT.Copy).then_inc(copied[0], 1)
            for f in range(KD):
                act.wait_ge(z_mm, 2 * f + 1)
                if f >= 2:
                    act.wait_ge(sums, 2 * (f - 1))
                act.activation(ev[:, f % 2, :], pe_[f % 2][:, :], ACT.Copy).then_inc(even_out, 1)
            act.wait_ge(c_mm, 1)
            act.activation(fT[:, :, HT:HT + 1].rearrange("p k o -> p (k o)"), py[0][:, 0:KD], ACT.Copy).then_inc(c_out, 1)
            act.wait_ge(c_out, 1)

        @block.vector
        def _(dve):
            for g in range(FG):
                ks = slice(2 * g, 2 * g + 2)
                near, far = aT[:, ks, 1:HT], aT[:, ks, SEQ - 1:HT:-1]
                dve.tensor_copy(odd[:, ks, 0:1], aT[:, ks, 0:1])
                dve.tensor_tensor(odd[:, ks, 1:HT], near, far, ALU.subtract).then_inc(odd_ready, 1)
                dve.wait_ge(odd_ready, g + 1)
                dve.tensor_tensor(near, near, far, ALU.add).then_inc(even_ready, 1)
            for j in range(1, NJ, 2):
                t, g = jobs[j]
                dve.wait_ge(y_mm, j + 1)
                dve.tensor_copy(y[:, t, :, g * FW:(g + 1) * FW], py[j % 4][:, :].rearrange("p (s f) -> p s f", s=2)).then_inc(copied[1], 1)
            for f in range(KD):
                dve.wait_ge(even_out, f + 1)
                dve.wait_ge(z_mm, 2 * f + 2)
                dve.tensor_tensor(fT[:, f, 0:HT], ev[:, f % 2, :], po[f % 2][:, :], ALU.add).then_inc(sums, 1)
                dve.tensor_tensor(fT[:, f, HT + 1:SEQ], ev[:, f % 2, HT - 1:0:-1], po[f % 2][:, HT - 1:0:-1], ALU.subtract).then_inc(sums, 1)
            dve.wait_ge(sums, 2 * KD)
def program(nc, x, c, ctx, c_ctx, w_ada, b_ada, w_in, s5_lam_re, s5_lam_im, s5_log_dt, s5_b_re, s5_b_im,
            s5_c_re, s5_c_im, s5_d, s5_w_glu, s5_b_glu, na_q_gain, na_k_gain, na_rpb, w_mix_out,
            w_fourier_out, b_fourier_out, w_router, router_bias, w_exp_gate, w_exp_up, w_exp_down,
            w_sh_gate, w_sh_up, w_sh_down, cs_feat, cos_tok, sin_tok, alt, out):
    def scratch(name, shape):
        return nc.dram_tensor(f"scratch_{name}", shape, F32, kind="Internal").ap()

    mats, rot, k_lags = scratch("mats", (P, 5, G5, P)), scratch("rot", (P, 2, G5, NCK)), scratch("lags", (W5, TAUS * C5))
    mix_dram = scratch("mix", (D, SEQ))
    u_dram, y_dram = scratch("u", (W5, TOK)), scratch("y", (W5, SEQ))
    pad = scratch("pad", (HEADS * RPB_R, 2 * GRID_W - 1))
    f_dram, acc_dram = scratch("f", (SEQ + PAD_ROWS, D)), scratch("acc", (SEQ + PAD_ROWS, D))
    xr = x[0]
    rows = lambda t, n: [t[i * P:(i + 1) * P, :] for i in range(n)]

    def moe(layer, mod, h, ident, last):
        tag = f"moe{layer}"
        with Phase(nc, tag) as ph:
            idx, wslot = ph.sb("idx", [P, NIDX], U32), ph.sb("wslot", [P, NIDX])
            bounds, slot_of = ph.sb("bounds", [1, NE + 1], I32), ph.sb("slot_of", [1, P], I32)
            with Phase(nc, tag + "in") as ph2:
                fT = ph2.sb("fT", [P, KD, SEQ])
                tiles = [(h[:, t, :], (mod[:, 3 * D:4 * D], mod[:, 4 * D:5 * D]), False) for t in range(TT)]
                norm_modulate_transpose(nc, tag + "norm", ident, tiles, fT, True, store=rows(f_dram, TT))
                route_and_share(nc, tag + "route", ident, fT, w_router[layer], router_bias[layer], w_sh_gate[layer],
                                w_sh_up[layer], w_sh_down[layer], f_dram, acc_dram, idx, wslot, bounds, slot_of)
            experts(nc, tag + "exp", w_exp_gate[layer], w_exp_up[layer], w_exp_down[layer], f_dram, acc_dram,
                    ident, idx, wslot, bounds, slot_of)
        add_gated(nc, tag + "add", acc_dram, mod[:, 5 * D:6 * D], h, out[0] if last else None)

    with Phase(nc, "main") as main:
        ident = main.sb("ident", [P, P])
        decay = main.sb("decay", [P, G5])
        make_identity(nc, ident)
        s5_matrices(nc, ident, s5_lam_re[0], s5_lam_im[0], s5_log_dt[0], s5_b_re[0], s5_b_im[0], s5_c_re[0],
                    s5_c_im[0], s5_d[0], mats, k_lags, rot, decay)
        mod = main.sb("mod", [P, ADA])
        with Phase(nc, "attn") as at:
            bt = at.sb("bt", [P, HP, RPB_R, GRID_W])
            qT, kT = at.sb("qT", [P, HP, SEQ]), at.sb("kT", [P, HP, TOK])
            v_even, v_odd, v_ctx = at.sb("v_even", [P, TT, NCH]), at.sb("v_odd", [P, TT - 1, NCH]), at.sb("v_ctx", [P, CT, NCH])
            with Phase(nc, "pre") as pre:
                aT = pre.sb("aT", [P, KD, TOK])
                with Phase(nc, "cond") as cond:
                    mod_ctx = cond.sb("mod_ctx", [P, 2 * D])
                    conditioning(nc, "ada0", c.rearrange("a (p k) -> p (a k)", k=KD), w_ada[0], b_ada[0], mod,
                                 c_ctx.rearrange("(p k) -> p k", k=KD), mod_ctx)
                    norm_modulate_transpose(nc, "norm_ctx", ident,
                                            [(r, (mod_ctx[:, 0:D], mod_ctx[:, D:2 * D]), True) for r in rows(ctx[0], CT)],
                                            aT[:, :, 0:CTX], True)
                for part in range(2):
                    n = TT // 2
                    norm_modulate_transpose(nc, f"norm_x{part}", ident,
                                            [(r, (mod[:, 0:D], mod[:, D:2 * D]), True) for r in rows(xr, TT)[n * part:n * part + n]],
                                            aT[:, :, CTX + part * n * P:CTX + (part + 1) * n * P], True)
                project(nc, ident, aT, w_in[0], na_q_gain[0], na_k_gain[0], u_dram, qT, kT, v_even, v_odd, v_ctx,
                        lambda ph: BiasTable(ph, na_rpb[0], pad, bt))
            attention(nc, ident, qT, kT, v_even, v_odd, v_ctx, bt, mix_dram[W5:, :])
        s5_scan_readout(nc, ident, u_dram, mats, rot, decay, y_dram, s5_w_glu[0], s5_b_glu[0], mix_dram[0:W5, :])
        h = main.sb("h", [P, TT, D])
        with Phase(nc, "mixed") as mx:
            residual(nc, "mix", mx.sb("mixT", [P, KD, SEQ]), w_mix_out[0], None, mod[:, 2 * D:3 * D], h, x=xr, src_dram=mix_dram)
        moe(0, mod, h, ident, False)

        conditioning(nc, "ada1", c.rearrange("a (p k) -> p (a k)", k=KD), w_ada[1], b_ada[1], mod)
        with Phase(nc, "four") as fo:
            aT = fo.sb("aT", [P, KD, SEQ])
            norm_modulate_transpose(nc, "norm_f", ident, [(h[:, t, :], (mod[:, 0:D], mod[:, D:2 * D]), False) for t in range(TT)], aT, False)
            fourier(nc, "fft", aT, cs_feat, cos_tok, sin_tok, alt, aT)
            residual(nc, "fout", aT, w_fourier_out[0], b_fourier_out[0], mod[:, 2 * D:3 * D], h)
        moe(1, mod, h, ident, True)


INPUTS = ["x", "c", "ctx", "c_ctx", "w_ada", "b_ada", "w_in", "s5_lam_re", "s5_lam_im", "s5_log_dt", "s5_b_re", "s5_b_im",
          "s5_c_re", "s5_c_im", "s5_d", "s5_w_glu", "s5_b_glu", "na_q_gain", "na_k_gain", "na_rpb", "w_mix_out",
          "w_fourier_out", "b_fourier_out", "w_router", "router_bias", "w_exp_gate", "w_exp_up", "w_exp_down",
          "w_sh_gate", "w_sh_up", "w_sh_down"]


def transform_constants():
    import numpy as np

    i = np.arange(FW)
    a = 2 * np.pi * ((i[:, None] * i[None, :]) % FW) / FW
    feat = np.concatenate([np.cos(a), np.sin(a)], axis=1) / np.sqrt(SEQ * FW)
    t = np.arange(SEQ // 2)
    b = 2 * np.pi * ((t[:, None] * t[None, :]) % SEQ) / SEQ
    return {
        "cs_feat": np.ascontiguousarray(feat.reshape(2, P, 2 * FW).transpose(1, 0, 2), dtype=np.float32),
        "cos_tok": np.cos(b).astype(np.float32),
        "sin_tok": (-np.sin(b)).astype(np.float32),
        "alt": np.where(t % 2 == 0, 1, -1).astype(np.float32),
    }


def kernel(**inputs):
    import numpy as np
    import concourse.bacc as bacc
    from concourse.bass_utils import run_bass_kernel_spmd

    nc = bacc.Bacc("TRN2", target_bir_lowering=False, num_devices=1)
    arrays, args = {}, []
    for name, a in [(n, inputs[n]) for n in INPUTS] + list(transform_constants().items()):
        a = np.ascontiguousarray(a)
        arrays[f"in_{name}"] = a
        args.append(nc.dram_tensor(f"in_{name}", a.shape, mybir.dt.from_np(a.dtype), kind="ExternalInput").ap())
    out = nc.dram_tensor("out_h", (1, SEQ, D), F32, kind="ExternalOutput").ap()
    program(nc, *args, out)
    r = run_bass_kernel_spmd(nc, [arrays], core_ids=[0])
    return r.results[0]["out_h"]
```

```python
import math
from contextlib import ExitStack

import concourse.bass as bass
from concourse import mybir

F32 = mybir.dt.float32
I32 = mybir.dt.int32
U32 = mybir.dt.uint32
F32R = mybir.dt.float32r
ALU = mybir.AluOpType
ACT = mybir.ActivationFunctionType
AX = mybir.AxisListType

P = 128
D = 1024
KD = D // P
SEQ = 1024
CTX = 256
TOK = CTX + SEQ
TT = SEQ // P
CT = CTX // P
EPS = 1e-6
GRID_W = 64
ROWS = SEQ // GRID_W
NCH = 512
ADA = 6 * D
G5, C5, S5 = 32, 16, 64
W5 = G5 * C5
LCH = 8
NCK = TOK // LCH
NCC = CTX // LCH
NCL = SEQ // LCH
HEADS, HD = 8, 64
HP = HEADS // 2
KH, KW = 8, 16
RPB_R, RPB_C = 2 * KH - 1, 2 * KW - 1
NE, NG, EG = 64, 8, 8
TOPG, TOPK = 4, 8
FF = 256
NEG = -1e30


class Phase:

    def __init__(self, nc, name):
        self.nc, self.name, self.stack, self.sems = nc, name, ExitStack(), []

    def __enter__(self):
        self.stack.__enter__()
        return self

    def __exit__(self, *a):
        self.stack.__exit__(*a)
        if self.sems:
            self.nc.clear_and_free_semaphores(self.sems)
            self.nc.all_engine_barrier()

    def sb(self, name, shape, dt=F32):
        return self.stack.enter_context(self.nc.sbuf_tensor(f"{self.name}_{name}", shape, dt))

    def ps(self, name, shape, dt=F32):
        return self.stack.enter_context(self.nc.psum_tensor(f"{self.name}_{name}", shape, dt))

    def sem(self, name):
        self.sems.append(self.nc.alloc_semaphore(name=f"{self.name}_{name}"))
        return self.sems[-1]

    def block(self):
        return self.stack.enter_context(self.nc.Block())


class Chain:

    def __init__(self, eng, sem):
        self.eng, self.sem, self.n = eng, sem, 0

    def __call__(self, ins):
        self.n += 1
        ins.then_inc(self.sem, 1)
        self.eng.wait_ge(self.sem, self.n)


def make_identity(nc, ident):
    with Phase(nc, "ident") as ph:
        zero = ph.sem("zero")
        done = ph.sem("done")
        block = ph.block()

        @block.gpsimd
        def _(pool):
            pool.memset(ident[:, :], 0.0).then_inc(zero, 1)
            pool.wait_ge(zero, 1)
            pool.affine_select(out=ident[:, :], in_=ident[:, :], compare_op=ALU.not_equal, fill=1.0,
                               base=0, pattern=[[-1, P]], channel_multiplier=1).then_inc(done, 1)
            pool.wait_ge(done, 1)


def conditioning(nc, tag, c_col, w, b, mod, ctx_col, mod_ctx):
    CW, BUF = NCH // 2, 4
    NB = ADA // CW
    NC = 2 * D // CW
    PE_ROWS = (KD // 2, 0)
    with Phase(nc, tag) as ph:
        col = ph.sb("col", [P, 2, KD])
        act = ph.sb("act", [P, 2, KD])
        ones = ph.sb("ones", [P, P])
        rep = ph.sb("rep", [P, KD // 2, P])
        part = ph.sb("part", [P, BUF, 2, CW])
        wbuf = ph.sb("w", [P, BUF, KD, CW])
        banks = [[ph.ps(f"p{s}{i}", [P, NCH]) for i in range(BUF)] for s in ("mod", "ctx")]
        col_in, bias_in = ph.sem("col_in"), ph.sem("bias_in")
        w_in = [ph.sem(f"w_in{i}") for i in range(BUF)]
        silu_done, ones_done, rep_done = ph.sem("silu_done"), ph.sem("ones_done"), ph.sem("rep_done")
        summed = [ph.sem("summed"), ph.sem("summed_ctx")]
        product = [ph.sem("product"), ph.sem("product_ctx")]
        copied = [ph.sem("copied"), ph.sem("copied_ctx")]
        scaled = ph.sem("scaled")
        w_v = w.rearrange("(p k) n -> p k n", k=KD)
        chunk = lambda i: slice(i * CW, (i + 1) * CW)
        kinds = lambda i: (1, 0) if i < NC else (0,)
        block = ph.block()

        @block.sync
        def _(sp):
            sp.dma_start(col[:, 0, :], c_col).then_inc(col_in, 16)
            sp.dma_start(col[:, 1, :], ctx_col).then_inc(col_in, 16)
            sp.dma_start(mod[0:1, :], b[None, :]).then_inc(bias_in, 16)
            for i in range(NB):
                if i >= BUF:
                    sp.wait_ge(product[0], i - BUF + 1)
                sp.dma_start(wbuf[:, i % BUF, :, :], w_v[:, :, chunk(i)]).then_inc(w_in[i % BUF], 16)

        @block.tensor
        def _(pe):
            pe.wait_ge(rep_done, KD // 2)
            pe.wait_ge(bias_in, 16)
            for i in range(NB):
                for s in kinds(i):
                    bank = banks[s][i % BUF][:, 0:CW]
                    if i >= BUF:
                        pe.wait_ge(copied[s], i - BUF + 1)
                    pe.matmul(bank, ones[0:1, :], mod[0:1, chunk(i)], start=True, stop=False)
                    if PE_ROWS[s]:
                        pe.wait_ge(w_in[i % BUF], 16 * (i // BUF + 1))
                    for k in range(PE_ROWS[s]):
                        pe.matmul(bank, rep[:, k, :], wbuf[:, i % BUF, k, :], start=False, stop=False)
                    pe.wait_ge(summed[s], (i + 1) * (KD - PE_ROWS[s]))
                    pe.matmul(bank, ones[:, :], part[:, i % BUF, s, :], start=False, stop=True).then_inc(product[s], 1)

        @block.scalar
        def _(act_e):
            act_e.wait_ge(col_in, 32)
            act_e.activation(act[:, :, :], col[:, :, :], ACT.Silu).then_inc(silu_done, 1)
            for i in range(NB):
                for s in kinds(i):
                    act_e.wait_ge(product[s], i + 1)
                    act_e.activation((mod, mod_ctx)[s][:, chunk(i)], banks[s][i % BUF][:, 0:CW], ACT.Copy).then_inc(copied[s], 1)

        @block.vector
        def _(dve):
            dve.memset(ones[:, :], 1.0).then_inc(ones_done, 1)
            dve.wait_ge(ones_done, 1)
            dve.wait_ge(silu_done, 1)
            for k in range(KD // 2):
                dve.tensor_scalar(rep[:, k, :], ones[:, :], act[:, 0, k:k + 1], None, ALU.mult).then_inc(rep_done, 1)

            def add_one(t, s, count):
                dve.wait_ge(copied[s], count)
                dve.tensor_scalar(t, t, 1.0, None, ALU.add).then_inc(scaled, 1)

            for i in range(NB):
                dve.wait_ge(w_in[i % BUF], 16 * (i // BUF + 1))
                for s in kinds(i):
                    if i >= BUF:
                        dve.wait_ge(product[s], i - BUF + 1)
                    n = KD - PE_ROWS[s]
                    for j in range(n):
                        k = PE_ROWS[s] + j
                        if j == 0:
                            dve.tensor_scalar(part[:, i % BUF, s, :], wbuf[:, i % BUF, k, :], act[:, s, k:k + 1], None, ALU.mult).then_inc(summed[s], 1)
                        else:
                            dve.wait_ge(summed[s], i * n + j)
                            dve.scalar_tensor_tensor(part[:, i % BUF, s, :], wbuf[:, i % BUF, k, :], act[:, s, k:k + 1], part[:, i % BUF, s, :],
                                                     ALU.mult, ALU.add).then_inc(summed[s], 1)
                if i == NC + 1:
                    add_one(mod[:, D:2 * D], 0, NC)
                    add_one(mod_ctx[:, D:2 * D], 1, NC)
            add_one(mod[:, 4 * D:5 * D], 0, 5 * D // CW)
            dve.wait_ge(scaled, 3)


class RowSums:

    def __init__(self, ph, c_col, w, sums_dram):
        self.c_col, self.w, self.sums_dram = c_col, w.rearrange("(p k) n -> p k n", k=KD), sums_dram
        self.col, self.act = ph.sb("col", [P, KD]), ph.sb("act", [P, KD])
        self.wbuf, self.part = ph.sb("wada", [P, 2, KD, NCH]), ph.sb("part", [P, 2, NCH])
        self.col_in, self.silu_done, self.summed = ph.sem("col_in"), ph.sem("silu_done"), ph.sem("summed")
        self.w_in, self.kept = ([ph.sem(f"{s}{i}") for i in range(2)] for s in ("wada_in", "kept"))
        self.steps = [(i, k) for i in range(ADA // NCH) for k in range(KD)]

    def begin(self, sp):
        sp.dma_start(self.col[:, :], self.c_col).then_inc(self.col_in, 16)
        for i in range(2):
            self.load(sp, i)

    def load(self, sp, i):
        sp.dma_start(self.wbuf[:, i % 2, :, :], self.w[:, :, i * NCH:(i + 1) * NCH]).then_inc(self.w_in[i % 2], 16)

    def keep(self, sp, i):
        sp.wait_ge(self.summed, (i + 1) * KD)
        if i + 2 < ADA // NCH:
            self.load(sp, i + 2)
        sp.dma_start(self.sums_dram[:, i * NCH:(i + 1) * NCH], self.part[:, i % 2, :]).then_inc(self.kept[i % 2], 16)

    def end(self, sp):
        for i in range(2):
            sp.wait_ge(self.kept[i], 16 * (ADA // NCH // 2))

    def silu(self, act_e):
        act_e.wait_ge(self.col_in, 16)
        act_e.activation(self.act[:, :], self.col[:, :], ACT.Silu).then_inc(self.silu_done, 1)

    def row(self, dve, step):
        i, k = self.steps[step]
        dst, c = self.part[:, i % 2, :], self.act[:, k:k + 1]
        if step == 0:
            dve.wait_ge(self.silu_done, 1)
        if k == 0:
            dve.wait_ge(self.w_in[i % 2], 16 * (i // 2 + 1))
            if i >= 2:
                dve.wait_ge(self.kept[i % 2], 16 * (i // 2))
            dve.tensor_scalar(dst, self.wbuf[:, i % 2, k, :], c, None, ALU.mult).then_inc(self.summed, 1)
        else:
            dve.wait_ge(self.summed, step)
            dve.scalar_tensor_tensor(dst, self.wbuf[:, i % 2, k, :], c, dst, ALU.mult, ALU.add).then_inc(self.summed, 1)


class Norm:
    RING = 4

    def __init__(self, ph, ident, tiles, aT, permuted, store=None, ready=None, buffers=3):
        self.ident, self.tiles, self.aT, self.permuted, self.store, self.ready = ident, tiles, aT, permuted, store, ready
        self.n, self.nb = len(tiles), buffers
        n = self.n
        self.loaded = tiles[0][2]
        self.xin = ph.sb("xin", [P, self.RING, D]) if self.loaded else None
        self.junk = ph.sb("junk", [P, 2, D])
        self.ss, self.var, self.std, self.rstd = (ph.sb(s, [P, n]) for s in ("ss", "var", "std", "rstd"))
        self.a = ph.sb("a", [P, 3, D])
        self.pT = [ph.ps(f"pT{i}", [P, KD, P]) for i in range(buffers)]
        self.x_in = [ph.sem(f"x_in{i}") for i in range(self.RING)] if self.loaded else []
        self.sq_done, self.var_done, self.std_done, self.rstd_done = (ph.sem(s) for s in ("sq_done", "var_done", "std_done", "rstd_done"))
        self.scale_done, self.a_done, self.tr_done, self.copied = (ph.sem(s) for s in ("scale_done", "a_done", "tr_done", "copied"))
        self.stored = [ph.sem(f"stored{i}") for i in range(3)]

    def source(self, i):
        return self.xin[:, i % self.RING, :] if self.loaded else self.tiles[i][0]

    def load(self, sp, i):
        if i >= self.RING:
            sp.wait_ge(self.scale_done, i - self.RING + 1)
        sp.dma_start(self.source(i), self.tiles[i][0]).then_inc(self.x_in[i % self.RING], 16)

    def keep(self, sp, i):
        sp.wait_ge(self.a_done, i + 1)
        sp.dma_start(self.store[i], self.a[:, i % 3, :]).then_inc(self.stored[i % 3], 16)

    def kept(self, sp):
        for j in range(min(3, self.n)):
            sp.wait_ge(self.stored[j], 16 * len(range(j, self.n, 3)))

    def square(self, act, i):
        if self.loaded:
            act.wait_ge(self.x_in[i % self.RING], 16 * (i // self.RING + 1))
        elif self.ready is not None:
            act.wait_ge(self.ready, 2 * i + 2)
        if i >= 2:
            act.wait_ge(self.sq_done, i - 1)
        act.activation(self.junk[:, i % 2, :], self.source(i), ACT.Square, accum_out=self.ss[:, i:i + 1]).then_inc(self.sq_done, 1)

    def root(self, act, i):
        act.wait_ge(self.var_done, i + 1)
        act.activation(self.std[:, i:i + 1], self.var[:, i:i + 1], ACT.Sqrt).then_inc(self.std_done, 1)

    def copy(self, act, i):
        act.wait_ge(self.tr_done, i + 1)
        act.activation(self.aT[:, :, i * P:(i + 1) * P], self.pT[i % self.nb][:, :, :], ACT.Copy).then_inc(self.copied, 1)

    def variance(self, dve, i):
        dve.wait_ge(self.sq_done, i + 1)
        dve.tensor_scalar(self.var[:, i:i + 1], self.ss[:, i:i + 1], 1.0 / D, EPS, ALU.mult, ALU.add).then_inc(self.var_done, 1)

    def modulate(self, dve, i):
        dve.wait_ge(self.std_done, i + 1)
        dve.reciprocal(self.rstd[:, i:i + 1], self.std[:, i:i + 1]).then_inc(self.rstd_done, 1)
        dve.wait_ge(self.rstd_done, i + 1)
        if i >= 3:
            dve.wait_ge(self.tr_done, i - 2)
            if self.store is not None:
                dve.wait_ge(self.stored[i % 3], 16 * (i // 3))
        shift, scale1 = self.tiles[i][1]
        av, sv, hv, cv = self.a[:, i % 3, :], self.source(i), shift, scale1
        if self.permuted:
            av = av.rearrange("q (k p) -> q p k", k=KD)
            sv, hv, cv = (t.rearrange("q (p k) -> q p k", k=KD) for t in (sv, hv, cv))
        dve.scalar_tensor_tensor(av, sv, self.rstd[:, i:i + 1], cv, ALU.mult, ALU.mult).then_inc(self.scale_done, 1)
        dve.wait_ge(self.scale_done, i + 1)
        dve.tensor_tensor(av, av, hv, ALU.add).then_inc(self.a_done, 1)

    def turn(self, pe, i):
        pe.wait_ge(self.a_done, i + 1)
        if i >= self.nb:
            pe.wait_ge(self.copied, i - self.nb + 1)
        for k in range(KD):
            tr = pe.transpose(self.pT[i % self.nb][:, k, :], self.a[:, i % 3, k * P:(k + 1) * P], self.ident[:, :])
        tr.then_inc(self.tr_done, 1)


def norm_modulate_transpose(nc, tag, ident, tiles, aT, permuted, store=None):
    n = len(tiles)
    with Phase(nc, tag) as ph:
        norm = Norm(ph, ident, tiles, aT, permuted, store)
        block = ph.block()

        @block.sync
        def _(sp):
            for i in range(n):
                if norm.loaded:
                    norm.load(sp, i)
                if store is not None:
                    norm.keep(sp, i)
            if store is not None:
                norm.kept(sp)

        @block.scalar
        def _(act):
            norm.square(act, 0)
            norm.square(act, 1)
            norm.root(act, 0)
            for i in range(n):
                if i + 2 < n:
                    norm.square(act, i + 2)
                if i + 1 < n:
                    norm.root(act, i + 1)
                if i >= 1:
                    norm.copy(act, i - 1)
            norm.copy(act, n - 1)
            act.wait_ge(norm.copied, n)

        @block.vector
        def _(dve):
            norm.variance(dve, 0)
            for i in range(n):
                if i + 1 < n:
                    norm.variance(dve, i + 1)
                norm.modulate(dve, i)

        @block.tensor
        def _(pe):
            for i in range(n):
                norm.turn(pe, i)


def project(nc, ident, aT, w_in, q_gain, k_gain, u_dram, qT, kT, v_even, v_odd, v_ctx, bias_of):
    TG = [(0, NCH), (NCH, NCH), (2 * NCH, TOK - 2 * NCH)]
    NU = (W5 // P) * len(TG)
    w_v = w_in.rearrange("(p k) n -> p k n", k=KD)
    jobs = [(1, t) for t in range(CT, CT + TT)] + [(2, t) for t in range(CT + TT)] + [(3, t) for t in range(CT + TT)]
    NQK = TT + TT + CT
    last_of = {0: NU, 1: NU + TT, 2: NU + NQK, 3: NU + NQK + TT + CT}
    with Phase(nc, "proj") as ph:
        w = ph.sb("w", [P, 2, KD, NCH])
        uT = ph.sb("uT", [P, 2, LCH, NCK])
        sq = ph.sb("sq", [P, 2, NCH])
        ss = ph.sb("ss", [P, 2, HEADS])
        var = ph.sb("var", [P, 2, HEADS])
        std = ph.sb("std", [P, 2, HEADS])
        rstd = ph.sb("rstd", [P, 2, HEADS])
        qn = ph.sb("qn", [P, 2, NCH])
        gain = ph.sb("gain", [P, 2, HD])
        pz = [ph.ps(f"pz{i}", [P, NCH]) for i in range(4)]
        pt = [ph.ps(f"pt{i}", [P, HP, P]) for i in range(2)]
        w_got = [ph.sem(f"w_got{g}") for g in range(4)]
        gain_got, gain_scaled = ph.sem("gain_got"), ph.sem("gain_scaled")
        mm_done, z_used = ph.sem("mm_done"), ph.sem("z_used")
        u_out = [ph.sem(f"u_out{i}") for i in range(2)]
        sq_done, dve_step, std_done, n_done = ph.sem("sq_done"), ph.sem("dve_step"), ph.sem("std_done"), ph.sem("n_done")
        t_done, t_copied = ph.sem("t_done"), ph.sem("t_copied")
        v_done = ph.sem("v_done")
        odd_lo, odd_hi = ph.sem("odd_lo"), ph.sem("odd_hi")
        bias = bias_of(ph)
        block = ph.block()

        @block.gpsimd
        def _(pool):
            bias.mask(pool)

        @block.sync
        def _(sp):
            for g in range(4):
                if g >= 2:
                    sp.wait_ge(mm_done, last_of[g - 2])
                sp.dma_start(w[:, g % 2, :, :], w_v[:, :, g * NCH:(g + 1) * NCH]).then_inc(w_got[g], 16)
                if g == 0:
                    sp.dma_start(gain[:, 0, :], q_gain[None, :].to_broadcast([P, HD])).then_inc(gain_got, 16)
                    sp.dma_start(gain[:, 1, :], k_gain[None, :].to_broadcast([P, HD])).then_inc(gain_got, 16)
                    bias.load(sp)
                if g == 1:
                    bias.spread(sp)
                    for c in range(W5 // P):
                        sp.wait_ge(z_used, (c + 1) * len(TG))
                        sp.dma_start(u_dram[c * P:(c + 1) * P, :], uT[:, c % 2, :, :]).then_inc(u_out[c % 2], 16)
            sp.wait_ge(v_done, CT + TT)
            sp.dma_start(v_odd[0:64, :, :], v_even[64:128, 0:TT - 1, :]).then_inc(odd_lo, 16)
            sp.dma_start(v_odd[64:128, :, :], v_even[0:64, 1:TT, :]).then_inc(odd_hi, 16)
            sp.wait_ge(odd_lo, 16)
            sp.wait_ge(odd_hi, 16)
            for j in range(2):
                sp.wait_ge(u_out[j], 16 * (W5 // P // 2))

        @block.tensor
        def _(pe):
            n = 0
            pe.wait_ge(w_got[0], 16)
            for c in range(W5 // P):
                for t0, tn in TG:
                    if n >= 4:
                        pe.wait_ge(z_used, n - 3)
                    for k in range(KD):
                        mm = pe.matmul(pz[n % 4][:, 0:tn], w[:, 0, k, c * P:(c + 1) * P], aT[:, k, t0:t0 + tn],
                                       start=k == 0, stop=k == KD - 1)
                    mm.then_inc(mm_done, 1)
                    n += 1

            def turn(j):
                pe.wait_ge(n_done, j + 1)
                if j >= 2:
                    pe.wait_ge(t_copied, j - 1)
                for h in range(HP):
                    tr = pe.transpose(pt[j % 2][:, h, :], qn[:, j % 2, h * P:(h + 1) * P], ident[:, :])
                tr.then_inc(t_done, 1)

            for j, (g, t) in enumerate(jobs):
                pe.wait_ge(w_got[g], 16)
                pe.wait_ge(z_used, n - 3)
                for k in range(KD):
                    mm = pe.matmul(pz[n % 4][:, :], aT[:, k, t * P:(t + 1) * P], w[:, g % 2, k, :],
                                   start=k == 0, stop=k == KD - 1)
                mm.then_inc(mm_done, 1)
                n += 1
                if 2 <= j < NQK + 2:
                    turn(j - 2)

        @block.scalar
        def _(act):
            for j, (g, t) in enumerate(jobs):
                n = NU + j
                if g < 3:
                    act.wait_ge(mm_done, n + 1)
                    if j >= 2:
                        act.wait_ge(dve_step, 5 * (j - 2) + 1)
                    act.activation(sq[:, j % 2, :], pz[n % 4][:, :], ACT.Square).then_inc(sq_done, 1)
                    act.wait_ge(dve_step, 5 * j + 2)
                    act.activation(std[:, j % 2, :], var[:, j % 2, :], ACT.Sqrt).then_inc(std_done, 1)
                if g == 3 or j >= 2:
                    i = j - 2
                    if i < NQK:
                        gi, ti = jobs[i]
                        act.wait_ge(t_done, i + 1)
                        dst = qT[:, :, (ti - CT) * P:(ti - CT + 1) * P] if gi == 1 else kT[:, :, ti * P:(ti + 1) * P]
                        act.activation(dst, pt[i % 2][:, :, :], ACT.Copy).then_inc(t_copied, 1)
            act.wait_ge(t_copied, NQK)

        @block.vector
        def _(dve):
            bias.pad_rows(dve)
            dve.wait_ge(gain_got, 32)
            dve.tensor_scalar(gain[:, 0, :], gain[:, 0, :], HD ** -0.5, None, ALU.mult).then_inc(gain_scaled, 1)
            n = 0
            for c in range(W5 // P):
                for t0, tn in TG:
                    dve.wait_ge(mm_done, n + 1)
                    if c >= 2 and t0 == 0:
                        dve.wait_ge(u_out[c % 2], 16 * (c // 2))
                    m0, mn = t0 // LCH, tn // LCH
                    dve.tensor_copy(uT[:, c % 2, :, m0:m0 + mn],
                                    pz[n % 4][:, 0:tn].rearrange("p (m j) -> p j m", j=LCH)).then_inc(z_used, 1)
                    n += 1
            dve.wait_ge(gain_scaled, 1)
            for j, (g, t) in enumerate(jobs):
                n = NU + j
                z = pz[n % 4]
                if g == 3:
                    dve.wait_ge(mm_done, n + 1)
                    dst = v_ctx[:, t, :] if t < CT else v_even[:, t - CT, :]
                    cp = dve.tensor_copy(dst, z[:, :])
                    cp.then_inc(v_done, 1)
                    dve.wait_ge(v_done, j - NQK + 1)
                    dve.sem_inc(z_used, 1)
                    continue
                b = j % 2
                dve.wait_ge(sq_done, j + 1)
                dve.tensor_reduce(ss[:, b, :], sq[:, b, :].rearrange("p (h d) -> p h d", d=HD), AX.X, ALU.add).then_inc(dve_step, 1)
                dve.wait_ge(dve_step, 5 * j + 1)
                dve.tensor_scalar(var[:, b, :], ss[:, b, :], 1.0 / HD, EPS, ALU.mult, ALU.add).then_inc(dve_step, 1)
                dve.wait_ge(std_done, j + 1)
                dve.reciprocal(rstd[:, b, :], std[:, b, :]).then_inc(dve_step, 1)
                dve.wait_ge(dve_step, 5 * j + 3)
                if j >= 2:
                    dve.wait_ge(t_done, j - 1)
                q3 = qn[:, b, :].rearrange("p (h d) -> p h d", d=HD)
                dve.tensor_tensor(q3, z[:, :].rearrange("p (h d) -> p h d", d=HD),
                                  rstd[:, b, :, None].to_broadcast([P, HEADS, HD]), ALU.mult).then_inc(dve_step, 1)
                dve.wait_ge(dve_step, 5 * j + 4)
                dve.sem_inc(z_used, 1)
                dve.tensor_tensor(q3, q3, gain[:, g - 1, None, :].to_broadcast([P, HEADS, HD]), ALU.mult).then_inc(dve_step, 1)
                dve.wait_ge(dve_step, 5 * j + 5)
                dve.sem_inc(n_done, 1)


class BiasTable:

    def __init__(self, ph, rpb, pad_dram, bt):
        self.rpb, self.pad_dram, self.bt = rpb, pad_dram, bt
        self.W = 2 * GRID_W - 1
        self.table = ph.sb("table", [HEADS * RPB_R, RPB_C])
        self.pad = ph.sb("pad", [HEADS * RPB_R, self.W])
        self.cleared, self.rpb_got, self.pad_ready, self.pad_out, self.table_in = (
            ph.sem(s) for s in ("cleared", "rpb_got", "pad_ready", "pad_out", "table_in"))
        self.low, self.high = ph.sem("low"), ph.sem("high")

    def load(self, sp):
        sp.dma_start(self.table[:, :], self.rpb.rearrange("h r c -> (h r) c")).then_inc(self.rpb_got, 16)

    def pad_rows(self, dve):
        dve.wait_ge(self.rpb_got, 16)
        dve.wait_ge(self.cleared, 1)
        first = GRID_W - 1 - (KW - 1)
        dve.tensor_copy(self.pad[:, first:first + RPB_C], self.table[:, RPB_C - 1::-1]).then_inc(self.pad_ready, 1)

    def spread(self, sp):
        sp.wait_ge(self.pad_ready, 1)
        sp.dma_start(self.pad_dram, self.pad[:, :]).then_inc(self.pad_out, 16)
        sp.wait_ge(self.pad_out, 16)
        for a in range(2):
            for h in range(HP):
                src = bass.AP(tensor=self.pad_dram.tensor, offset=(2 * h + a) * RPB_R * self.W,
                              ap=[[1, GRID_W], [self.W, RPB_R], [1, GRID_W]])
                sp.dma_start(self.bt[a * 64:(a + 1) * 64, h, :, :], src).then_inc(self.table_in, 16)

    def mask(self, pool):
        pool.memset(self.pad[:, :], NEG).then_inc(self.cleared, 1)
        pool.wait_ge(self.table_in, 16 * 2 * HP)
        last = GRID_W - KW
        for a in range(2):
            t = self.bt[a * 64:(a + 1) * 64, :, :, GRID_W - last:GRID_W].rearrange("p h r c -> p (h r) c")
            pool.affine_select(out=t, in_=t, compare_op=ALU.is_ge, fill=NEG, base=KW // 2 + last - 1,
                               pattern=[[0, HP * RPB_R], [-1, last]], channel_multiplier=-1).then_inc(self.low, 1)
        pool.wait_ge(self.low, 2)
        for a in range(2):
            t = self.bt[a * 64:(a + 1) * 64, :, :, 0:GRID_W - KW].rearrange("p h r c -> p (h r) c")
            pool.affine_select(out=t, in_=t, compare_op=ALU.is_ge, fill=NEG, base=KW // 2 - GRID_W,
                               pattern=[[0, HP * RPB_R], [1, GRID_W - KW]], channel_multiplier=1).then_inc(self.high, 1)
        pool.wait_ge(self.high, 2)


def attention(nc, ident, qT, kT, v_even, v_odd, v_ctx, bt, out_dram, sums_of):
    units = [(h, r) for h in range(HP) for r in range(ROWS)]
    N = len(units)
    NL = KH * GRID_W
    NK = NL + CTX
    NKT = NK // P
    first_row = [min(max(r - KH // 2, 0), ROWS - KH) for r in range(ROWS)]
    with Phase(nc, "att") as ph:
        qbd = ph.sb("qbd", [P, 2, P])
        sl = ph.sb("sl", [P, 2, NL])
        m = ph.sb("m", [P, 2, 4])
        nm = ph.sb("nm", [P, 2])
        sums = ph.sb("sums", [P, 2, 2])
        den = ph.sb("den", [P, 2])
        rden = ph.sb("rden", [P, 2])
        pr = ph.sb("pr", [P, 2, NK])
        prT = ph.sb("prT", [P, 2, NKT, P])
        obd = ph.sb("obd", [P, 2, P])
        oT = ph.sb("oT", [P, HP, SEQ])
        stored = ph.sem("stored")
        p_loc = [ph.ps(f"p_loc{i}", [P, NL]) for i in range(2)]
        p_ctx = [ph.ps(f"p_ctx{i}", [P, NCH]) for i in range(2)]
        p_t = [ph.ps(f"p_t{i}", [P, 4, P]) for i in range(2)]
        p_o = ph.ps("p_o", [P, NCH])
        p_ot = ph.ps("p_ot", [P, NCH])
        zeroed = ph.sem("zeroed")
        q_ready, s_done, max_done, nm_done, exp_done = (ph.sem(s) for s in ("q_ready", "s_done", "max_done", "nm_done", "exp_done"))
        pt_done, ptc_act, ptc_dve = ph.sem("pt_done"), ph.sem("ptc_act"), ph.sem("ptc_dve")
        den_done, rden_done, pv_done, o_ready, ot_done, o_out = (ph.sem(s) for s in ("den_done", "rden_done", "pv_done", "o_ready", "ot_done", "o_out"))
        ada = sums_of(ph)
        NSTEP = len(ada.steps)
        block = ph.block()

        @block.sync
        def _(sp):
            ada.begin(sp)
            chunks = NSTEP // KD
            for i in range(chunks):
                ada.keep(sp, i)
                if (i + 1) % (chunks // HP) == 0:
                    h = i // (chunks // HP)
                    sp.wait_ge(o_out, 2 * ROWS * (h + 1))
                    sp.dma_start(out_dram[h * P:(h + 1) * P, :], oT[:, h, :]).then_inc(stored, 16)
            sp.wait_ge(stored, 16 * HP)
            ada.end(sp)

        @block.gpsimd
        def _(pool):
            pool.memset(qbd[:, :, :], 0.0).then_inc(zeroed, 1)
            pool.memset(obd[:, :, :], 0.0).then_inc(zeroed, 1)
            pool.wait_ge(zeroed, 2)
            for n, (h, r) in enumerate(units):
                if n >= 2:
                    pool.wait_ge(s_done, n - 1)
                for a in range(2):
                    pool.tensor_copy(qbd[a * 64:(a + 1) * 64, n % 2, a * 64:(a + 1) * 64],
                                     qT[a * 64:(a + 1) * 64, h, r * 64:(r + 1) * 64]).then_inc(q_ready, 1)

        @block.tensor
        def _(pe):
            def scores(n):
                h, r = units[n]
                b = n % 2
                pe.wait_ge(q_ready, 2 * n + 2)
                if n >= 2:
                    pe.wait_ge(max_done, 2 * (n - 1))
                    pe.wait_ge(exp_done, 2 * (n - 1))
                k0 = CTX + first_row[r] * GRID_W
                pe.matmul(p_loc[b][:, :], qbd[:, b, :], kT[:, h, k0:k0 + NL], start=True, stop=True)
                pe.matmul(p_ctx[b][:, 0:CTX], qbd[:, b, :], kT[:, h, 0:CTX], start=True, stop=True).then_inc(s_done, 1)

            def turn(n):
                b = n % 2
                pe.wait_ge(exp_done, 2 * n + 2)
                if n >= 1:
                    pe.wait_ge(ptc_act, n)
                    pe.wait_ge(ptc_dve, n)
                for t in range(NKT):
                    tr = pe.transpose(p_t[t // 3][:, t % 3, :], pr[:, b, t * P:(t + 1) * P], ident[:, :])
                tr.then_inc(pt_done, 1)

            def values(n):
                h, r = units[n]
                b = n % 2
                pe.wait_ge(ptc_act, n + 1)
                pe.wait_ge(ptc_dve, n + 1)
                if n >= 1:
                    pe.wait_ge(o_ready, 2 * n)
                r0 = first_row[r]
                v_loc = v_odd if r0 % 2 else v_even
                for t in range(NKT):
                    v = v_loc[:, r0 // 2 + t, h * P:(h + 1) * P] if t < NL // P else v_ctx[:, t - NL // P, h * P:(h + 1) * P]
                    mm = pe.matmul(p_o[:, 0:P], prT[:, b, t, :], v, start=t == 0, stop=t == NKT - 1)
                mm.then_inc(pv_done, 1)

            def turn_out(n):
                b = n % 2
                pe.wait_ge(o_ready, 2 * n + 2)
                if n >= 1:
                    pe.wait_ge(o_out, 2 * n)
                pe.transpose(p_ot[:, 0:P], obd[:, b, :], ident[:, :]).then_inc(ot_done, 1)

            pe.wait_ge(zeroed, 2)
            for i in range(N + 3):
                if i < N:
                    scores(i)
                if 1 <= i <= N:
                    turn(i - 1)
                if 2 <= i <= N + 1:
                    values(i - 2)
                if 3 <= i:
                    turn_out(i - 3)

        @block.vector
        def _(dve):
            def maxima(n):
                h, r = units[n]
                b = n % 2
                rel = first_row[r] - r + KH - 1
                dve.wait_ge(s_done, n + 1)
                if n >= 2:
                    dve.wait_ge(exp_done, 2 * (n - 1))
                rows = lambda t: t.rearrange("p (r c) -> p r c", r=KH)
                dve.tensor_tensor_reduce(rows(sl[:, b, :]), rows(p_loc[b][:, :]), bt[:, h, rel:rel + KH, GRID_W - 1::-1],
                                         1.0, -3e38, ALU.add, ALU.max, m[:, b, 0:1]).then_inc(max_done, 1)
                dve.tensor_reduce(m[:, b, 1:2], p_ctx[b][:, 0:CTX], AX.X, ALU.max).then_inc(max_done, 1)
                dve.wait_ge(max_done, 2 * n + 2)
                dve.tensor_scalar(nm[:, b:b + 1], m[:, b, 0:1], m[:, b, 1:2], -1.0, ALU.max, ALU.mult).then_inc(nm_done, 1)

            def copy_half(n):
                b = n % 2
                dve.wait_ge(pt_done, n + 1)
                if n >= 2:
                    dve.wait_ge(pv_done, n - 1)
                dve.tensor_copy(prT[:, b, 3:NKT, :], p_t[1][:, 0:3, :]).then_inc(ptc_dve, 1)
                dve.wait_ge(exp_done, 2 * n + 2)
                dve.tensor_tensor(den[:, b:b + 1], sums[:, b, 0:1], sums[:, b, 1:2], ALU.add).then_inc(den_done, 1)
                dve.wait_ge(den_done, n + 1)
                dve.reciprocal(rden[:, b:b + 1], den[:, b:b + 1]).then_inc(rden_done, 1)

            def scale(n):
                b = n % 2
                dve.wait_ge(pv_done, n + 1)
                dve.wait_ge(rden_done, n + 1)
                if n >= 2:
                    dve.wait_ge(ot_done, n - 1)
                for a in range(2):
                    s = slice(a * 64, (a + 1) * 64)
                    dve.tensor_scalar(obd[s, b, s], p_o[s, s], rden[s, b:b + 1], None, ALU.mult).then_inc(o_ready, 1)

            dve.wait_ge(zeroed, 2)
            for i in range(N + 2):
                if i < N:
                    maxima(i)
                if 1 <= i <= N:
                    copy_half(i - 1)
                if 2 <= i:
                    scale(i - 2)
                if i < N:
                    for step in range(i * NSTEP // N, (i + 1) * NSTEP // N):
                        ada.row(dve, step)

        @block.scalar
        def _(act):
            def exps(n):
                b = n % 2
                act.wait_ge(nm_done, n + 1)
                if n >= 2:
                    act.wait_ge(pt_done, n - 1)
                    act.wait_ge(den_done, n - 1)
                act.activation(pr[:, b, 0:NL], sl[:, b, :], ACT.Exp, bias=nm[:, b:b + 1], accum_out=sums[:, b, 0:1]).then_inc(exp_done, 1)
                act.activation(pr[:, b, NL:NK], p_ctx[b][:, 0:CTX], ACT.Exp, bias=nm[:, b:b + 1], accum_out=sums[:, b, 1:2]).then_inc(exp_done, 1)

            def copy_half(n):
                b = n % 2
                act.wait_ge(pt_done, n + 1)
                if n >= 2:
                    act.wait_ge(pv_done, n - 1)
                act.activation(prT[:, b, 0:3, :], p_t[0][:, 0:3, :], ACT.Copy).then_inc(ptc_act, 1)

            def out(n):
                h, r = units[n]
                b = n % 2
                act.wait_ge(ot_done, n + 1)
                for a in range(2):
                    s = slice(a * 64, (a + 1) * 64)
                    act.activation(oT[s, h, r * 64:(r + 1) * 64], p_ot[s, s], ACT.Copy).then_inc(o_out, 1)

            ada.silu(act)
            for i in range(N + 3):
                if i < N:
                    exps(i)
                if 1 <= i <= N:
                    copy_half(i - 1)
                if 3 <= i:
                    out(i - 3)
            act.wait_ge(o_out, 2 * N)


GS = G5 // 8
NP9 = LCH + 1
TAUS = 2 * LCH - 1
TWO_PI = 2 * math.pi
PI_A = 6.28125
PI_B = 0.0019350051879882812
PI_C = TWO_PI - PI_A - PI_B
ROUND = 1.5 * 2.0 ** 23


def s5_matrices(nc, ident, lam_re, lam_im, log_dt, b_re, b_im, c_re, c_im, d, mats, k_dram, rot_dram, decay):
    with Phase(nc, "mats") as ph:
        nat = ph.sb("nat", [G5, 2, 2, S5])
        ldt = ph.sb("ldt", [G5, 2])
        edt = ph.sb("edt", [G5, 2])
        dtn = ph.sb("dtn", [G5, 2, S5])
        ones = ph.sb("ones", [P, S5])
        base = ph.sb("base", [P, 3, G5])
        sm = ph.sb("sm", [P, 24, G5])
        pw = ph.sb("pw", [P, 2, NP9, G5])
        tp = ph.sb("tp", [P, 4, 4, G5])
        pg = ph.sb("pg", [P, 2, LCH, G5])
        pw9 = ph.sb("pw9", [P, 2, NP9, G5])
        bn = ph.sb("bn", [P, 2, G5, C5])
        bb = ph.sb("bb", [P, 2, G5, C5])
        cn = ph.sb("cn", [P, 2, GS, 2, S5])
        cc = ph.sb("cc", [P, 2, W5])
        g = ph.sb("g", [P, 8, LCH, C5])
        g2 = ph.sb("g2", [P, 8, LCH, C5])
        w9 = ph.sb("w9", [P, 2, G5, NP9, C5])
        big = ph.sb("big", [P, 2, 8, NP9, C5])
        winT = ph.sb("winT", [P, 2, 8, P])
        bpad = ph.sb("bpad", [P, 2, G5, P])
        dcol = ph.sb("dcol", [P, GS])
        eye16 = ph.sb("eye16", [P, C5])
        kall = ph.sb("kall", [P, GS, TAUS, C5])
        toep = ph.sb("toep", [P, G5, P])
        rot = ph.sb("rot", [P, 2, G5, NCK])
        rt = toep[:, :, :].rearrange("p (i a) c -> p i (a c)", i=4)
        p_in = ph.ps("p_in", [P, NCH])
        p_c = ph.ps("p_c", [P, 4, P])
        p_g = [ph.ps(f"p_g{i}", [P, 4, P]) for i in range(2)]
        p_k = [[ph.ps(f"p_k{b}{i}", [P, NCH]) for i in range(2)] for b in range(2)]
        got_lam, got_b, got_c, got_d = (ph.sem(s) for s in ("got_lam", "got_b", "got_c", "got_d"))
        exp_done, dtn_done, base_tr, act_done = (ph.sem(s) for s in ("exp_done", "dtn_done", "base_tr", "act_done"))
        step = ph.sem("step")
        angles, c_tr, c_copied = ph.sem("angles"), ph.sem("c_tr"), ph.sem("c_copied")
        g_ready, g_tr, g_copied, g_out = ph.sem("g_ready"), ph.sem("g_tr"), ph.sem("g_copied"), ph.sem("g_out")
        w9_ready, w9_out, bpad_ready, k_done, k_read = (ph.sem(s) for s in ("w9_ready", "w9_out", "bpad_ready", "k_done", "k_read"))
        zeroed, kall_ready, k_out, toep_in, toep_out = (ph.sem(s) for s in ("zeroed", "kall_ready", "k_out", "toep_in", "toep_out"))
        rot_ready, rot_out = ph.sem("rot_ready"), ph.sem("rot_out")
        block = ph.block()

        @block.sync
        def _(sp):
            sp.dma_start(nat[:, 0, :, :], lam_re.rearrange("s g p -> g s p")).then_inc(got_lam, 16)
            sp.dma_start(nat[:, 1, :, :], lam_im.rearrange("s g p -> g s p")).then_inc(got_lam, 16)
            sp.dma_start(ldt[:, :], log_dt.rearrange("s g -> g s"), allow_slow_non_contiguous=True).then_inc(got_lam, 16)
            for i, src in enumerate((c_re, c_im)):
                for s in range(2):
                    sp.dma_start(cn[:, i, :, s, :], src[s].rearrange("(q e) c p -> (e c) q p", e=8)).then_inc(got_c, 16)
            for i, src in enumerate((b_re, b_im)):
                for s in range(2):
                    sp.dma_start(bn[s * 64:(s + 1) * 64, i, :, :], src[s].rearrange("g p c -> p g c")).then_inc(got_b, 16)
            sp.dma_start(dcol[:, :], d.rearrange("(q e) c -> (e c) q", e=8), allow_slow_non_contiguous=True).then_inc(got_d, 16)
            for q in range(GS):
                sp.wait_ge(g_copied, 4 * (q + 1))
                for i in range(2):
                    sp.dma_start(mats[:, i, 8 * q:8 * q + 8, :], winT[:, i, :, :]).then_inc(g_out, 16)
            sp.wait_ge(w9_ready, GS)
            for i in range(2):
                sp.dma_start(mats[:, 2 + i, :, :], w9[:, i, :, 0:LCH, :].rearrange("p g j c -> p g (j c)")).then_inc(w9_out, 16)
            sp.wait_ge(rot_ready, 1)
            sp.dma_start(rot_dram, rot[:, :, :, :]).then_inc(rot_out, 16)
            sp.wait_ge(kall_ready, GS)
            sp.dma_start(k_dram.rearrange("(q e c) t -> (e c) q t", e=8, c=C5), kall[:, :, :, :].rearrange("p q t c -> p q (t c)")).then_inc(k_out, 16)
            sp.wait_ge(k_out, 16)
            for i in range(LCH):
                src = k_dram.rearrange("(g c) t -> c g t", c=C5)[:, :, (LCH - 1 - i) * C5:(2 * LCH - 1 - i) * C5]
                sp.dma_start(toep[i * C5:(i + 1) * C5, :, :], src).then_inc(toep_in, 16)
            sp.wait_ge(toep_in, 16 * LCH)
            sp.dma_start(mats[:, 4, :, :], toep[:, :, :]).then_inc(toep_out, 16)
            sp.wait_ge(g_out, 16 * 2 * GS)
            sp.wait_ge(w9_out, 32)
            sp.wait_ge(toep_out, 16)
            sp.wait_ge(rot_out, 16)

        @block.scalar
        def _(act):
            act.wait_ge(got_lam, 48)
            act.activation(edt[:, :], ldt[:, :], ACT.Exp).then_inc(exp_done, 1)
            act.wait_ge(angles, 1)
            act.activation(sm[:, 4, :], sm[:, 2, :], ACT.Exp).then_inc(act_done, 1)
            act.activation(decay[:, :], sm[:, 2, :], ACT.Exp, scale=float(LCH)).then_inc(act_done, 1)
            act.wait_ge(angles, 2)
            act.activation(sm[:, 8, :], sm[:, 5, :], ACT.Sin).then_inc(act_done, 1)
            act.activation(sm[:, 9, :], sm[:, 7, :], ACT.Sin).then_inc(act_done, 1)
            for q in range(GS):
                for i in range(2):
                    for h in range(2):
                        n = 4 * q + 2 * i + h
                        act.wait_ge(g_tr, n + 1)
                        if q >= 1:
                            act.wait_ge(g_out, 16 * 2 * q)
                        act.activation(winT[:, i, 4 * h:4 * h + 4, :], p_g[n % 2][:, :, :], ACT.Copy).then_inc(g_copied, 1)
            act.wait_ge(g_copied, 4 * GS)

        @block.gpsimd
        def _(pool):
            pool.memset(bpad[:, :, :, :], 0.0).then_inc(zeroed, 1)

        @block.tensor
        def _(pe):
            pe.wait_ge(dtn_done, 2)
            for i, src in enumerate((nat[:, 0, :, :], nat[:, 1, :, :], dtn[:, :, :])):
                tr = pe.transpose(p_in[:, i * G5:(i + 1) * G5], src.rearrange("g s p -> g (s p)"), ident[0:G5, 0:G5])
            tr.then_inc(base_tr, 1)
            pe.wait_ge(got_c, 64)
            for i in range(2):
                if i == 1:
                    pe.wait_ge(c_copied, 1)
                for q in range(GS):
                    tr = pe.transpose(p_c[:, q, :], cn[:, i, q, :, :].rearrange("p s c -> p (s c)"), ident[:, :])
                tr.then_inc(c_tr, 1)
            for q in range(GS):
                for i in range(2):
                    pe.wait_ge(g_ready, 2 * q + i + 1)
                    for h in range(2):
                        n = 4 * q + 2 * i + h
                        if n >= 2:
                            pe.wait_ge(g_copied, n - 1)
                        for e in range(4):
                            tr = pe.transpose(p_g[n % 2][:, e, :], (g, g2)[i][:, 4 * h + e, :, :].rearrange("p j c -> p (j c)"), ident[:, :])
                        tr.then_inc(g_tr, 1)
            pe.wait_ge(bpad_ready, 1)
            pe.wait_ge(w9_ready, GS)
            for q in range(GS):
                for s in range(2):
                    if q >= 2:
                        pe.wait_ge(k_read, q - 1)
                    r = slice(s * 64, (s + 1) * 64)
                    for e in range(8):
                        for i in range(2):
                            mm = pe.matmul(p_k[q % 2][s][:, 0:NP9 * C5], bpad[r, i, 8 * q + e, :],
                                           w9[r, i, 8 * q + e, :, :].rearrange("p j c -> p (j c)"),
                                           start=e == 0 and i == 0, stop=e == 7 and i == 1)
                    mm.then_inc(k_done, 1)

        @block.vector
        def _(dve):
            link = Chain(dve, step)

            def cmul(o_re, o_im, a_re, a_im, b_re_, b_im_, t):
                dve.tensor_tensor(t[0], a_re, b_re_, ALU.mult).then_inc(step, 1)
                dve.tensor_tensor(t[1], a_im, b_im_, ALU.mult).then_inc(step, 1)
                dve.tensor_tensor(t[2], a_re, b_im_, ALU.mult).then_inc(step, 1)
                dve.tensor_tensor(t[3], a_im, b_re_, ALU.mult).then_inc(step, 1)
                link.n += 4
                dve.wait_ge(step, link.n)
                dve.tensor_tensor(o_re, t[0], t[1], ALU.subtract).then_inc(step, 1)
                dve.tensor_tensor(o_im, t[2], t[3], ALU.add).then_inc(step, 1)
                link.n += 2
                dve.wait_ge(step, link.n)

            dve.wait_ge(exp_done, 1)
            link(dve.memset(ones[:, :], 1.0))
            for s in range(2):
                dve.tensor_scalar(dtn[:, s, :], ones[0:G5, :], edt[:, s:s + 1], None, ALU.mult).then_inc(dtn_done, 1)
            dve.wait_ge(base_tr, 1)
            link(dve.tensor_copy(base[:, :, :], p_in[:, 0:3 * G5].rearrange("p (i g) -> p i g", i=3)))
            re, im, dt = base[:, 0, :], base[:, 1, :], base[:, 2, :]
            T = lambda i: sm[:, i, :]
            link(dve.tensor_scalar(T(0), re, -1e-4, None, ALU.min))
            link(dve.tensor_tensor(T(1), im, dt, ALU.mult))
            dve.tensor_tensor(T(2), T(0), dt, ALU.mult).then_inc(angles, 1)
            link(dve.tensor_scalar(T(3), T(1), 1.0 / TWO_PI, None, ALU.mult))
            link(dve.tensor_scalar(T(3), T(3), ROUND, None, ALU.add))
            link(dve.tensor_scalar(T(3), T(3), ROUND, None, ALU.subtract))
            link(dve.scalar_tensor_tensor(T(5), T(3), -PI_A, T(1), ALU.mult, ALU.add))
            link(dve.scalar_tensor_tensor(T(5), T(3), -PI_B, T(5), ALU.mult, ALU.add))
            link(dve.scalar_tensor_tensor(T(5), T(3), -PI_C, T(5), ALU.mult, ALU.add))
            link(dve.tensor_scalar(T(6), T(5), math.pi / 2, None, ALU.add))
            link(dve.tensor_scalar(T(7), T(6), math.pi, -TWO_PI, ALU.is_gt, ALU.mult))
            link(dve.tensor_tensor(T(7), T(6), T(7), ALU.add))
            link(dve.tensor_scalar(T(5), T(5), 3.1415925, -3.1415925, ALU.min, ALU.max))
            link(dve.tensor_scalar(T(7), T(7), 3.1415925, -3.1415925, ALU.min, ALU.max))
            dve.sem_inc(angles, 1)
            dve.wait_ge(act_done, 4)
            link(dve.memset(pw[:, 0, 0, :], 1.0))
            link(dve.memset(pw[:, 1, 0, :], 0.0))
            link(dve.tensor_tensor(pw[:, 1, 1, :], T(8), T(4), ALU.mult))
            link(dve.tensor_tensor(pw[:, 0, 1, :], T(9), T(4), ALU.mult))
            for m in (1, 2, 4):
                x = [tp[:, i, 0:m, :] for i in range(4)]
                top = [pw[:, i, m, None, :].to_broadcast([P, m, G5]) for i in range(2)]
                cmul(pw[:, 0, m + 1:2 * m + 1, :], pw[:, 1, m + 1:2 * m + 1, :],
                     pw[:, 0, 1:m + 1, :], pw[:, 1, 1:m + 1, :], top[0], top[1], x)
            f, b = slice(0, 64), slice(64, P)
            for i in range(2):
                link(dve.tensor_copy(pg[f, i, :, :], pw[f, i, LCH - 1::-1, :]))
                link(dve.tensor_copy(pg[b, i, :, :], pw[b, i, 0:LCH, :]))
                link(dve.tensor_copy(pw9[f, i, 0:LCH, :], pw[f, i, 1:NP9, :]))
                link(dve.tensor_copy(pw9[b, i, 0:LCH, :], pw[b, i, LCH:0:-1, :]))
                link(dve.tensor_copy(pw9[:, i, LCH, :], pw[:, i, 0, :]))
            link(dve.tensor_scalar(T(10), pw[:, 0, 1, :], -1.0, None, ALU.add))
            link(dve.tensor_tensor(T(11), T(0), T(0), ALU.mult))
            link(dve.tensor_tensor(T(12), im, im, ALU.mult))
            link(dve.tensor_tensor(T(11), T(11), T(12), ALU.add))
            link(dve.reciprocal(T(12), T(11)))
            link(dve.tensor_tensor(T(13), T(0), T(12), ALU.mult))
            link(dve.tensor_tensor(T(14), im, T(12), ALU.mult))
            link(dve.tensor_scalar(T(14), T(14), -1.0, None, ALU.mult))
            cmul(T(15), T(16), T(10), pw[:, 1, 1, :], T(13), T(14), [T(17), T(18), T(19), T(20)])
            dve.wait_ge(got_b, 64)
            fr, fi = (T(i)[:, :, None].to_broadcast([P, G5, C5]) for i in (15, 16))
            tb = [big[:, i, :, :, :].rearrange("p e j c -> p (e j c)")[:, 0:G5 * C5].rearrange("p (g c) -> p g c", g=G5) for i in range(2)]
            tc = [big[:, i, :, :, :].rearrange("p e j c -> p (e j c)")[:, G5 * C5:2 * G5 * C5].rearrange("p (g c) -> p g c", g=G5) for i in range(2)]
            cmul(bb[:, 0, :, :], bb[:, 1, :, :], bn[:, 0, :, :], bn[:, 1, :, :], fr, fi, [tb[0], tb[1], tc[0], tc[1]])
            for i in range(2):
                dve.wait_ge(c_tr, i + 1)
                dve.tensor_copy(cc[:, i, :], p_c[:, :, :].rearrange("p q c -> p (q c)")).then_inc(c_copied, 1)
            dve.wait_ge(c_copied, 2)
            dve.wait_ge(zeroed, 1)
            for i in range(2):
                for e in range(8):
                    link(dve.tensor_copy(bpad[:, i, e::8, e * C5:(e + 1) * C5], bb[:, i, e::8, :]))
            dve.sem_inc(bpad_ready, 1)
            for q in range(GS):
                e8 = slice(8 * q, 8 * q + 8)
                sh = [P, 8, LCH, C5]
                pr = [pg[:, i, :, e8].rearrange("p j g -> p g j")[:, :, :, None].to_broadcast(sh) for i in range(2)]
                br = [bb[:, i, e8, None, :].to_broadcast(sh) for i in range(2)]
                t0, t1 = big[:, 0, :, 0:LCH, :], big[:, 1, :, 0:LCH, :]
                if q >= 1:
                    dve.wait_ge(g_tr, 4 * q)
                link(dve.tensor_tensor(t0, pr[0], br[0], ALU.mult))
                link(dve.tensor_tensor(t1, pr[1], br[1], ALU.mult))
                link(dve.tensor_tensor(g[:, :, :, :], t0, t1, ALU.subtract))
                dve.sem_inc(g_ready, 1)
                link(dve.tensor_tensor(t0, pr[0], br[1], ALU.mult))
                link(dve.tensor_tensor(t1, pr[1], br[0], ALU.mult))
                link(dve.tensor_tensor(g2[:, :, :, :], t0, t1, ALU.add))
                dve.sem_inc(g_ready, 1)
                sh = [P, 8, NP9, C5]
                pr = [pw9[:, i, :, e8].rearrange("p j g -> p g j")[:, :, :, None].to_broadcast(sh) for i in range(2)]
                cr = [cc[:, i, 8 * q * C5:8 * (q + 1) * C5].rearrange("p (g c) -> p g c", g=8)[:, :, None, :].to_broadcast(sh) for i in range(2)]
                t0, t1 = big[:, 0, :, :, :], big[:, 1, :, :, :]
                link(dve.tensor_tensor(t0, pr[0], cr[0], ALU.mult))
                link(dve.tensor_tensor(t1, pr[1], cr[1], ALU.mult))
                link(dve.tensor_tensor(w9[:, 0, e8, :, :], t0, t1, ALU.subtract))
                link(dve.tensor_tensor(t0, pr[0], cr[1], ALU.mult))
                link(dve.tensor_tensor(t1, pr[1], cr[0], ALU.mult))
                link(dve.tensor_tensor(t0, t0, t1, ALU.add))
                link(dve.tensor_scalar(w9[:, 1, e8, :, :], t0, -1.0, None, ALU.mult))
                dve.sem_inc(w9_ready, 1)
            link(dve.tensor_reduce(eye16[:, :], ident[:, :].rearrange("p (q c) -> p c q", c=C5), AX.X, ALU.add))
            dve.wait_ge(got_d, 16)

            def lag_kernels(q):
                dve.wait_ge(k_done, 2 * q + 2)
                kf = p_k[q % 2][0][:, 0:NP9 * C5].rearrange("p (t c) -> p t c", c=C5)
                kb = p_k[q % 2][1][:, 0:NP9 * C5].rearrange("p (t c) -> p t c", c=C5)
                link(dve.tensor_copy(kall[:, q, 0:LCH - 1, :], kb[:, 1:LCH, :]))
                link(dve.tensor_copy(kall[:, q, LCH:TAUS, :], kf[:, 0:LCH - 1, :]))
                link(dve.scalar_tensor_tensor(kall[:, q, LCH - 1, :], eye16[:, :], dcol[:, q:q + 1], kf[:, LCH, :], ALU.mult, ALU.add))
                link(dve.tensor_tensor(kall[:, q, LCH - 1, :], kall[:, q, LCH - 1, :], kb[:, LCH, :], ALU.add))
                dve.sem_inc(k_read, 1)
                dve.sem_inc(kall_ready, 1)

            u = [(T(9), T(8))]
            spare = iter([(T(21), T(22)), (T(4), T(23)), (T(21), T(22))])
            for _ in range(3):
                nre, nim = next(spare)
                cmul(nre, nim, u[-1][0], u[-1][1], u[-1][0], u[-1][1], [T(17), T(18), T(19), T(20)])
                u.append((nre, nim))
            link(dve.memset(rot[:, 0, :, 0], 1.0))
            link(dve.memset(rot[:, 1, :, 0], 0.0))
            link(dve.tensor_copy(rot[:, 0, :, 1], u[-1][0]))
            link(dve.tensor_copy(rot[:, 1, :, 1], u[-1][1]))
            m = 1
            while m < NCK - 1:
                n = min(m, NCK - 1 - m, 32)
                w = n * G5
                x = [rt[:, i, 0:w].rearrange("p (g n) -> p g n", g=G5) for i in range(4)]
                top = [rot[:, i, :, m:m + 1].to_broadcast([P, G5, n]) for i in range(2)]
                cmul(rot[:, 0, :, m + 1:m + 1 + n], rot[:, 1, :, m + 1:m + 1 + n],
                     rot[:, 0, :, 1:1 + n], rot[:, 1, :, 1:1 + n], top[0], top[1], x)
                m += n
                if m == 3 * 32:
                    lag_kernels(0)
            dve.sem_inc(rot_ready, 1)
            for q in range(1, GS):
                lag_kernels(q)


def s5_scan_readout(nc, ident, u_dram, mats, rot_dram, decay, y_dram, w_glu, b_glu, out_dram):
    NX = NCK + NCC
    SC = 8
    L0 = NCC - 1
    with Phase(nc, "scan") as ph:
        u = ph.sb("u", [P, G5, NX])
        mt = ph.sb("mt", [P, 3, 5, 2, P])
        bs = ph.sb("bs", [P, 2, SC, NCK])
        xs = ph.sb("xs", [P, 2, SC, NCK])
        tmp = ph.sb("tmp", [P, 4, SC, NCK])
        dk = ph.sb("dk", [P, SC, NCK])
        ones = ph.sb("ones", [P, NCK])
        rot = ph.sb("rot", [P, 2, 2, SC, NCK])
        rot_in = [ph.sem(f"rot_in{i}") for i in range(2)]
        st = ph.sb("st", [P, 2, SC, NCL])
        y = ph.sb("y", [P, 2, SC, NCL])
        p_b = [[ph.ps(f"p_b{i}{n}", [P, 2, NCK]) for n in range(2)] for i in range(2)]
        p_y = [ph.ps(f"p_y{n}", [P, 2, NCL]) for n in range(2)]
        u_in, m_in = ph.sem("u_in"), [ph.sem(f"m_in{i}") for i in range(3)]
        b_mm, b_out, step, st_ready, y_mm, y_out = (ph.sem(s) for s in ("b_mm", "b_out", "step", "st_ready", "y_mm", "y_out"))
        y_st = [ph.sem(f"y_st{i}") for i in range(2)]
        step_a = ph.sem("step_a")
        dk_ready = ph.sem("dk_ready")
        block = ph.block()
        NPAIR = SC // 2
        TOTAL = GS * NPAIR

        order = []
        for q in range(GS + 1):
            if q < GS:
                order += [(0, q, e) for e in range(NPAIR)]
            if q >= 1:
                order += [(1, q - 1, e) for e in range(NPAIR)]

        @block.sync
        def _(sp):
            for j in range(LCH):
                src = u_dram.rearrange("(g c) (j m) -> j c g m", c=C5, j=LCH)[j]
                sp.dma_start(u[j * C5:(j + 1) * C5, :, 0:NCK], src).then_inc(u_in, 16)
                sp.dma_start(u[j * C5:(j + 1) * C5, :, NCK:NX], src[:, :, 0:NCC]).then_inc(u_in, 16)
            for q in range(2):
                sp.dma_start(rot[:, q, :, :, :], rot_dram[:, :, SC * q:SC * (q + 1), :]).then_inc(rot_in[q], 16)
            nb, ny, users = 0, 0, []
            for n, (s, q, e) in enumerate(order):
                if n >= 3:
                    k, v = users[n - 3]
                    sp.wait_ge((b_mm, y_mm)[k], v)
                if s == 0:
                    nb += 1
                    users.append((0, nb))
                else:
                    ny += 1
                    users.append((1, ny))
                g0 = SC * q + 2 * e
                sel = slice(0, 2) if s == 0 else slice(2, 5)
                if s == 1 and e == 0 and q < GS - 2:
                    sp.wait_ge(st_ready, q + 1)
                    sp.dma_start(rot[:, q % 2, :, :, :], rot_dram[:, :, SC * (q + 2):SC * (q + 3), :]).then_inc(rot_in[q % 2], 16)
                sp.dma_start(mt[:, n % 3, sel, :, :], mats[:, sel, g0:g0 + 2, :]).then_inc(m_in[n % 3], 16)

        @block.gpsimd
        def _(pool):
            for q in range(GS):
                pool.wait_ge(y_out, NPAIR * (q + 1))
                for j in range(LCH):
                    dst = y_dram.rearrange("(g c) (j m) -> j c g m", c=C5, j=LCH)[j][:, SC * q:SC * (q + 1), :]
                    pool.dma_start(dst, y[j * C5:(j + 1) * C5, q % 2, :, :]).then_inc(y_st[q % 2], 16)
            for i in range(2):
                pool.wait_ge(y_st[i], 16 * LCH * GS // 2)

        @block.tensor
        def _(pe):
            pe.wait_ge(u_in, 16 * 2 * LCH)
            nb = ny = 0
            f, b = slice(0, 64), slice(64, P)
            for n, (s, q, e) in enumerate(order):
                pe.wait_ge(m_in[n % 3], 16 * (n // 3 + 1))
                m = mt[:, n % 3]
                if s == 0:
                    if nb >= 2:
                        pe.wait_ge(b_out, 2 * (nb - 1))
                    for i in range(2):
                        for k in range(2):
                            g = SC * q + 2 * e + k
                            pe.matmul(p_b[i][nb % 2][f, k, :], m[:, i, k, f], u[:, g, 0:NCK], start=True, stop=True)
                            mm = pe.matmul(p_b[i][nb % 2][b, k, :], m[:, i, k, b], u[:, g, NX - 1:NCC - 1:-1], start=True, stop=True)
                    nb += 1
                    mm.then_inc(b_mm, 1)
                else:
                    if ny >= 2:
                        pe.wait_ge(y_out, ny - 1)
                    pe.wait_ge(st_ready, q + 1)
                    for k in range(2):
                        g, l = SC * q + 2 * e + k, 2 * e + k
                        o = p_y[ny % 2][:, k, :]
                        pe.matmul(o, m[:, 4, k, :], u[:, g, NCC:NCK], start=True, stop=False)
                        pe.matmul(o, m[:, 2, k, :], st[:, 0, l, :], start=False, stop=False)
                        mm = pe.matmul(o, m[:, 3, k, :], st[:, 1, l, :], start=False, stop=True)
                    mm.then_inc(y_mm, 1)
                    ny += 1

        @block.scalar
        def _(act):
            nb = ny = 0
            for n, (s, q, e) in enumerate(order):
                if s == 0:
                    act.wait_ge(b_mm, nb + 1)
                    if e == 0 and q >= 1:
                        act.wait_ge(step_a, 4 * q)
                    for i in range(2):
                        act.activation(bs[:, i, 2 * e:2 * e + 2, :], p_b[i][nb % 2][:, :, :], ACT.Copy).then_inc(b_out, 1)
                    nb += 1
                else:
                    act.wait_ge(y_mm, ny + 1)
                    if e == 0 and q >= 2:
                        act.wait_ge(y_st[q % 2], 16 * LCH * (q // 2))
                    act.activation(y[:, q % 2, 2 * e:2 * e + 2, :], p_y[ny % 2][:, :, :], ACT.Copy).then_inc(y_out, 1)
                    ny += 1

        @block.vector
        def _(dve):
            link = Chain(dve, step)
            link(dve.memset(ones[:, :], 1.0))
            for q in range(GS):
                c, s = rot[:, q % 2, 0, :, :], rot[:, q % 2, 1, :, :]
                dve.wait_ge(rot_in[q % 2], 16 * (q // 2 + 1))
                for e in range(SC):
                    dve.tensor_scalar(dk[:, e, :], ones[:, :], decay[:, SC * q + e:SC * q + e + 1], None, ALU.mult).then_inc(step, 1)
                link.n += SC
                dve.wait_ge(step, link.n)
                link(dve.memset(dk[:, :, 0:1], 0.0))
                dve.wait_ge(b_out, 2 * NPAIR * (q + 1))
                dve.tensor_tensor(tmp[:, 0, :, :], bs[:, 0, :, :], c, ALU.mult).then_inc(step_a, 1)
                dve.tensor_tensor(tmp[:, 1, :, :], bs[:, 1, :, :], s, ALU.mult).then_inc(step_a, 1)
                dve.tensor_tensor(tmp[:, 2, :, :], bs[:, 1, :, :], c, ALU.mult).then_inc(step_a, 1)
                dve.tensor_tensor(tmp[:, 3, :, :], bs[:, 0, :, :], s, ALU.mult).then_inc(step_a, 1)
                dve.wait_ge(step_a, 4 * (q + 1))
                dve.tensor_tensor(tmp[:, 0, :, :], tmp[:, 0, :, :], tmp[:, 1, :, :], ALU.add).then_inc(step, 1)
                dve.tensor_tensor(tmp[:, 2, :, :], tmp[:, 2, :, :], tmp[:, 3, :, :], ALU.subtract).then_inc(step, 1)
                link.n += 2
                dve.wait_ge(step, link.n)
                flat = lambda t: t.rearrange("p g m -> p (g m)")
                for i in range(2):
                    dve.tensor_tensor_scan(flat(xs[:, i, :, :]), flat(dk[:, :, :]), flat(tmp[:, 2 * i, :, :]),
                                           0.0, ALU.mult, ALU.add).then_inc(step, 1)
                link.n += 2
                dve.wait_ge(step, link.n)
                w = slice(L0, L0 + NCL)
                x0, x1, cw, sw = xs[:, 0, :, w], xs[:, 1, :, w], c[:, :, w], s[:, :, w]
                t = [tmp[:, i, :, 0:NCL] for i in range(4)]
                for o, a, r in ((0, x0, cw), (1, x1, sw), (2, x1, cw), (3, x0, sw)):
                    dve.tensor_tensor(t[o], a, r, ALU.mult).then_inc(step, 1)
                link.n += 4
                dve.wait_ge(step, link.n)
                if q >= 1:
                    dve.wait_ge(y_mm, NPAIR * q)
                for r, back in ((slice(0, 64), 1), (slice(64, P), -1)):
                    dve.tensor_tensor(st[r, 0, :, ::back], t[0][r], t[1][r], ALU.subtract).then_inc(step, 1)
                    dve.tensor_tensor(st[r, 1, :, ::back], t[2][r], t[3][r], ALU.add).then_inc(step, 1)
                link.n += 4
                dve.wait_ge(step, link.n)
                dve.sem_inc(st_ready, 1)

    NT = W5 // P
    with Phase(nc, "glu") as ph:
        yT = ph.sb("yT", [P, NT, LCH, NCL])
        gT = ph.sb("gT", [P, NT, SEQ])
        w = ph.sb("w", [P, NT, W5])
        bias = ph.sb("bias", [P, NT])
        sg = ph.sb("sg", [P, 2, NCH])
        oT = ph.sb("oT", [P, NT, SEQ])
        stored = ph.sem("stored")
        pz = [ph.ps(f"pz{i}", [P, NCH]) for i in range(2)]
        y_in, w_in = [ph.sem(f"y_in{i}") for i in range(NT)], ph.sem("w_in")
        gelu_done, mm_done, sg_done, out_done = (ph.sem(s) for s in ("gelu_done", "mm_done", "sg_done", "out_done"))
        block = ph.block()

        @block.sync
        def _(sp):
            for i in range(NT):
                sp.dma_start(yT[:, i, :, :].rearrange("p j m -> p (j m)"), y_dram[i * P:(i + 1) * P, :]).then_inc(y_in[i], 16)
            sp.dma_start(w[:, :, :], w_glu.rearrange("(k p) n -> p k n", p=P)).then_inc(w_in, 16)
            sp.dma_start(bias[:, :], b_glu.rearrange("(k p) -> p k", p=P), allow_slow_non_contiguous=True).then_inc(w_in, 16)
            for i in range(NT):
                sp.wait_ge(out_done, 2 * i + 2)
                sp.dma_start(out_dram[i * P:(i + 1) * P, :], oT[:, i, :]).then_inc(stored, 16)
            sp.wait_ge(stored, 16 * NT)

        @block.scalar
        def _(act):
            for i in range(NT):
                act.wait_ge(y_in[i], 16)
                act.activation(gT[:, i, :].rearrange("p (m j) -> p j m", j=LCH), yT[:, i, :, :], ACT.Gelu_apprx_tanh).then_inc(gelu_done, 1)
            act.wait_ge(w_in, 32)
            for n in range(2 * NT):
                act.wait_ge(mm_done, n + 1)
                if n >= 2:
                    act.wait_ge(out_done, n - 1)
                act.activation(sg[:, n % 2, :], pz[n % 2][:, :], ACT.Sigmoid, bias=bias[:, n // 2:n // 2 + 1]).then_inc(sg_done, 1)

        @block.tensor
        def _(pe):
            pe.wait_ge(w_in, 32)
            pe.wait_ge(gelu_done, NT)
            for n in range(2 * NT):
                if n >= 2:
                    pe.wait_ge(sg_done, n - 1)
                for k in range(NT):
                    mm = pe.matmul(pz[n % 2][:, :], w[:, k, (n // 2) * P:(n // 2 + 1) * P], gT[:, k, (n % 2) * NCH:(n % 2 + 1) * NCH],
                                   start=k == 0, stop=k == NT - 1)
                mm.then_inc(mm_done, 1)

        @block.vector
        def _(dve):
            for n in range(2 * NT):
                dve.wait_ge(sg_done, n + 1)
                s = slice((n % 2) * NCH, (n % 2 + 1) * NCH)
                dve.tensor_tensor(oT[:, n // 2, s], sg[:, n % 2, :], gT[:, n // 2, s], ALU.mult).then_inc(out_done, 1)
            dve.wait_ge(out_done, 2 * NT)

NIDX = P + 3
PAD_ROWS = P
SCALE = 2.5


def residual_and_norm(nc, tag, ident, srcT, w, bias, gate, h, norm_args, x=None, src_dram=None):
    with Phase(nc, tag) as ph:
        wb = ph.sb("w", [P, KD, D])
        row = ph.sb("row", [P, D]) if bias is not None else None
        tmp = ph.sb("tmp", [P, 2, NCH])
        pz = [ph.ps(f"pz{i}", [P, NCH]) for i in range(4)]
        s_in, b_in, biased = [ph.sem(f"s_in{i}") for i in range(2)], ph.sem("b_in"), ph.sem("biased")
        w_in, x_in = [ph.sem(f"w_in{n}") for n in range(2)], ph.sem("x_in")
        mm_done, gated, added = ph.sem("mm_done"), ph.sem("gated"), ph.sem("added")
        norm = Norm(ph, ident, *norm_args, ready=added, buffers=2)
        jobs = [(t, n) for t in range(TT) for n in range(2)]
        w_v = w.rearrange("(k p) n -> p k n", p=P)
        block = ph.block()

        @block.sync
        def _(sp):
            src = lambda i: slice((0, 2 * P)[i], (2 * P, SEQ)[i])
            if src_dram is not None:
                src_v = src_dram.rearrange("(k p) n -> p k n", p=P)
                sp.dma_start(srcT[:, :, src(0)], src_v[:, :, src(0)]).then_inc(s_in[0], 16)
            sp.dma_start(wb[:, :, 0:NCH], w_v[:, :, 0:NCH]).then_inc(w_in[0], 16)
            if bias is not None:
                sp.dma_start(row[:, :], bias[None, :].to_broadcast([P, D])).then_inc(b_in, 16)
            sp.dma_start(wb[:, :, NCH:D], w_v[:, :, NCH:D]).then_inc(w_in[1], 16)
            if x is not None:
                sp.dma_start(h[:, :, :], x.rearrange("(t p) d -> p t d", p=P)).then_inc(x_in, 16)
            if src_dram is not None:
                sp.dma_start(srcT[:, :, src(1)], src_v[:, :, src(1)]).then_inc(s_in[1], 16)
            for i in range(TT):
                norm.keep(sp, i)
            norm.kept(sp)

        @block.tensor
        def _(pe):
            for j, (t, n) in enumerate(jobs):
                if src_dram is not None and n == 0 and t in (0, 2):
                    pe.wait_ge(s_in[t // 2], 16)
                pe.wait_ge(w_in[n], 16)
                if j >= 4:
                    pe.wait_ge(gated if bias is None else biased, j - 3)
                s = slice(n * NCH, (n + 1) * NCH)
                for k in range(KD):
                    mm = pe.matmul(pz[j % 4][:, :], srcT[:, k, t * P:(t + 1) * P], wb[:, k, s],
                                   start=k == 0, stop=k == KD - 1)
                mm.then_inc(mm_done, 1)
                if n == 1 and t >= 1:
                    norm.turn(pe, t - 1)
            norm.turn(pe, TT - 1)

        @block.scalar
        def _(act):
            for i in range(TT):
                norm.square(act, i)
                norm.root(act, i)
                if i >= 1:
                    norm.copy(act, i - 1)
            norm.copy(act, TT - 1)
            act.wait_ge(norm.copied, TT)

        @block.vector
        def _(dve):
            if x is not None:
                dve.wait_ge(x_in, 16)
            if bias is not None:
                dve.wait_ge(b_in, 16)
            for j, (t, n) in enumerate(jobs):
                dve.wait_ge(mm_done, j + 1)
                if j >= 2:
                    dve.wait_ge(added, j - 1)
                s = slice(n * NCH, (n + 1) * NCH)
                z = pz[j % 4][:, :]
                if bias is not None:
                    dve.tensor_tensor(tmp[:, j % 2, :], z, row[:, s], ALU.add).then_inc(biased, 1)
                    dve.wait_ge(biased, j + 1)
                    z = tmp[:, j % 2, :]
                dve.tensor_tensor(tmp[:, j % 2, :], z, gate[:, s], ALU.mult).then_inc(gated, 1)
                dve.wait_ge(gated, j + 1)
                dve.tensor_tensor(h[:, t, s], h[:, t, s], tmp[:, j % 2, :], ALU.add).then_inc(added, 1)
                if n == 1:
                    norm.variance(dve, t)
                    norm.modulate(dve, t)


def route_and_share(nc, tag, ident, fT, w_router, r_bias, w_sg, w_su, w_sd, f_dram, acc_dram, idx, wslot, bounds, slot_of,
                    w_gate, w_up, first_gu):
    with Phase(nc, tag) as ph:
        wr = ph.sb("wr", [P, KD, NE])
        rb = ph.sb("rb", [P, NE])
        wg = ph.sb("wg", [P, KD, FF])
        wu = ph.sb("wu", [P, KD, FF])
        wd = ph.sb("wd", [P, 2, D])
        zero = ph.sb("zero", [P, D])
        sil, up = ph.sb("sil", [P, 2, FF]), ph.sb("up", [P, 2, FF])
        hid, hidT = ph.sb("hid", [P, 2, FF]), ph.sb("hidT", [P, 2, 2, P])
        yo = ph.sb("yo", [P, 2, D])
        sc, sel, ms, mr, M = (ph.sb(s, [P, TT, NE]) for s in ("sc", "sel", "ms", "mr", "M"))
        t1, t2, gate, slot = (ph.sb(s, [P, TT, NE]) for s in ("t1", "t2", "gate", "slot"))
        gm = ph.sb("gm", [P, 8, TT, NG])
        low = ph.sb("low", [P, NG, NG])
        tri, ones, iota_f = ph.sb("tri", [P, P]), ph.sb("ones", [P, P]), ph.sb("iota_f", [P, P])
        iota_i = ph.sb("iota_i", [P, P], I32)
        col_i, col = ph.sb("col_i", [P, 1], I32), ph.sb("col", [P, 1])
        tok = ph.sb("tok", [P, TT])
        top = ph.sb("top", [P, TT, 8])
        s8, q8, r8, w8 = (ph.sb(s, [P, TT, TOPK]) for s in ("s8", "q8", "r8", "w8"))
        s8i, q8i, r8i = (ph.sb(s, [P, TT, TOPK], I32) for s in ("s8i", "q8i", "r8i"))
        den, rden = ph.sb("den", [P, TT]), ph.sb("rden", [P, TT])
        nbk = ph.sb("nbk", [P, 4, NE])
        thr = ph.sb("thr", [P, NE, KD])
        ebc, eb = ph.sb("ebc", [P, 2]), ph.sb("eb", [1, P], I32)
        HB = 2 * TOPK
        hot_r = ph.sb("hot_r", [P, HB, P])
        hot_q = ph.sb("hot_q", [P, HB, 2, P])
        tabf = ph.sb("tabf", [P, 2, P])
        p_l, p_pos = ph.ps("p_l", [P, TT, NE]), ph.ps("p_pos", [P, TT, NE])
        p_misc = ph.ps("p_misc", [P, NCH])
        p_g, p_u, p_h = ph.ps("p_g", [P, NCH]), ph.ps("p_u", [P, NCH]), ph.ps("p_h", [P, NCH])
        p_d = [ph.ps(f"p_d{i}", [P, NCH]) for i in range(2)]
        got_r, got_w, got_b, got_first = ph.sem("got_r"), ph.sem("got_w"), ph.sem("got_b"), ph.sem("got_first")
        zeroed, zero_out, consts, made, step = (ph.sem(s) for s in ("zeroed", "zero_out", "consts", "made", "step"))
        logits, scored, masked, counted, placed = (ph.sem(s) for s in ("logits", "scored", "masked", "counted", "placed"))
        hot_ready, hot_row, slots_ready, hot_mm, eb_ready, eb_mm, tri_ready, ones_ready = (ph.sem(s) for s in ("hot_ready", "hot_row", "slots_ready", "hot_mm", "eb_ready", "eb_mm", "tri_ready", "ones_ready"))
        gu_done, sil_done, hid_ready, h_tr, h_out, d_done, y_ready = (ph.sem(s) for s in ("gu_done", "sil_done", "hid_ready", "h_tr", "h_out", "d_done", "y_ready"))
        y_st = [ph.sem(f"y_st{i}") for i in range(2)]
        block = ph.block()

        @block.sync
        def _(sp):
            sp.dma_start(wr[:, :, :], w_router.rearrange("(p k) e -> p k e", k=KD)).then_inc(got_r, 16)
            sp.dma_start(rb[:, :], r_bias[None, :].to_broadcast([P, NE])).then_inc(got_b, 16)
            sp.dma_start(wg[:, :, :], w_sg.rearrange("(p k) f -> p k f", k=KD)).then_inc(got_w, 16)
            sp.dma_start(wu[:, :, :], w_su.rearrange("(p k) f -> p k f", k=KD)).then_inc(got_w, 16)
            sp.dma_start(wd[:, :, :], w_sd.rearrange("(j p) n -> p j n", p=P)).then_inc(got_w, 16)
            for i, w in enumerate((w_gate, w_up)):
                sp.dma_start(first_gu[:, :, i * FF:(i + 1) * FF], w[0].rearrange("(p k) f -> p k f", k=KD)).then_inc(got_first, 16)
            sp.wait_ge(zeroed, 1)
            sp.dma_start(f_dram[SEQ:SEQ + PAD_ROWS, :], zero[:, :]).then_inc(zero_out, 16)
            sp.dma_start(acc_dram[SEQ:SEQ + PAD_ROWS, :], zero[:, :]).then_inc(zero_out, 16)
            for t in range(TT):
                sp.wait_ge(y_ready, 2 * t + 2)
                sp.dma_start(acc_dram[t * P:(t + 1) * P, :], yo[:, t % 2, :]).then_inc(y_st[t % 2], 16)
            sp.wait_ge(got_first, 32)
            sp.wait_ge(zero_out, 32)
            for i in range(2):
                sp.wait_ge(y_st[i], 16 * TT // 2)

        @block.gpsimd
        def _(pool):
            pool.memset(zero[:, :], 0.0).then_inc(zeroed, 1)
            pool.memset(ones[:, :], 1.0).then_inc(ones_ready, 1)
            pool.memset(tri[:, :], 1.0).then_inc(made, 1)
            pool.memset(low[:, :, :], 1.0).then_inc(made, 1)
            pool.iota(iota_i[:, :], [[1, P]], base=0, channel_multiplier=0).then_inc(consts, 1)
            pool.iota(col_i[:, :], [[0, 1]], base=0, channel_multiplier=1).then_inc(consts, 1)
            pool.wait_ge(made, 2)
            pool.affine_select(out=tri[:, :], in_=tri[:, :], compare_op=ALU.is_gt, fill=0.0, base=0,
                               pattern=[[1, P]], channel_multiplier=-1).then_inc(tri_ready, 1)
            pool.affine_select(out=low[:, :, :], in_=low[:, :, :], compare_op=ALU.is_gt, fill=0.0, base=0,
                               pattern=[[1, NG], [-1, NG]], channel_multiplier=0).then_inc(consts, 1)
            for t in range(TT):
                pool.wait_ge(sil_done, 2 * t + 2)
                if t >= 2:
                    pool.wait_ge(h_tr, t - 1)
                pool.tensor_tensor(hid[:, t % 2, :], sil[:, t % 2, :], up[:, t % 2, :], ALU.mult).then_inc(hid_ready, 1)
                if t >= TT // 2:
                    pool.wait_ge(slots_ready, 1)
                    n = TT * TOPK // (TT // 2)
                    for j in range((t - TT // 2) * n, (t - TT // 2 + 1) * n):
                        if j >= HB:
                            pool.wait_ge(hot_mm, j - HB + 1)
                        pool.tensor_scalar(hot_r[:, j % HB, :], iota_f[:, :], r8[:, j // TOPK, j % TOPK:j % TOPK + 1], None, ALU.is_equal).then_inc(hot_row, 1)

        @block.tensor
        def _(pe):
            pe.wait_ge(got_r, 16)
            for t in range(TT):
                for k in range(KD):
                    mm = pe.matmul(p_l[:, t, :], fT[:, k, t * P:(t + 1) * P], wr[:, k, :], start=k == 0, stop=k == KD - 1)
            mm.then_inc(logits, 1)
            pe.wait_ge(got_w, 48)

            def gate_up(t):
                if t >= 1:
                    pe.wait_ge(sil_done, 2 * t)
                for k in range(KD):
                    pe.matmul(p_g[:, 0:FF], fT[:, k, t * P:(t + 1) * P], wg[:, k, :], start=k == 0, stop=k == KD - 1)
                for k in range(KD):
                    mm = pe.matmul(p_u[:, 0:FF], fT[:, k, t * P:(t + 1) * P], wu[:, k, :], start=k == 0, stop=k == KD - 1)
                mm.then_inc(gu_done, 1)

            def turn(t):
                pe.wait_ge(hid_ready, t + 1)
                if t >= 1:
                    pe.wait_ge(h_out, t)
                for j in range(2):
                    tr = pe.transpose(p_h[:, j * P:(j + 1) * P], hid[:, t % 2, j * P:(j + 1) * P], ident[:, :])
                tr.then_inc(h_tr, 1)

            def down(t):
                pe.wait_ge(h_out, t + 1)
                for n in range(2):
                    if t >= 1:
                        pe.wait_ge(y_ready, 2 * (t - 1) + n + 1)
                    for j in range(2):
                        mm = pe.matmul(p_d[n][:, :], hidT[:, t % 2, j, :], wd[:, j, n * NCH:(n + 1) * NCH], start=j == 0, stop=j == 1)
                    mm.then_inc(d_done, 1)

            def positions():
                pe.wait_ge(ones_ready, 1)
                pe.wait_ge(tri_ready, 1)
                pe.wait_ge(masked, 1)
                for t in range(TT):
                    mm = pe.matmul(p_misc[:, 0:NE], ones[:, :], M[:, t, :], start=t == 0, stop=t == TT - 1)
                mm.then_inc(counted, 1)
                for t in range(TT):
                    for s in range(t):
                        pe.matmul(p_pos[:, t, :], ones[:, :], M[:, s, :], start=s == 0, stop=False)
                    mm = pe.matmul(p_pos[:, t, :], tri[:, :], M[:, t, :], start=t == 0, stop=True)
                mm.then_inc(placed, 1)

            def tables(part):
                n = TT * TOPK // (TT // 2)
                for j in range(part * n, (part + 1) * n):
                    pe.wait_ge(hot_row, j + 1)
                    pe.wait_ge(hot_ready, 2 * (j + 1))
                    mm = pe.matmul(p_l[:, 0:4, :].rearrange("p a e -> p (a e)"), hot_r[:, j % HB, :], hot_q[:, j % HB, :, :].rearrange("p a b -> p (a b)"),
                                   start=j == 0, stop=j == TT * TOPK - 1)
                    mm.then_inc(hot_mm, 1)

            for t in range(TT):
                gate_up(t)
                if t >= 1:
                    down(t - 1)
                turn(t)
                if t == 1:
                    positions()
                if t >= TT // 2:
                    tables(t - TT // 2)
            down(TT - 1)
            pe.wait_ge(eb_ready, 1)
            pe.matmul(p_pos[0:1, 0:2, :].rearrange("p a e -> p (a e)"), ebc[:, 0:1], ident[:, :], start=True, stop=True).then_inc(eb_mm, 1)

        @block.scalar
        def _(act):
            act.wait_ge(logits, 1)
            act.activation(sc[:, :, :], p_l[:, :, :], ACT.Sigmoid).then_inc(scored, 1)
            for t in range(TT + 1):
                if t < TT:
                    act.wait_ge(gu_done, t + 1)
                    if t >= 2:
                        act.wait_ge(hid_ready, t - 1)
                    act.activation(sil[:, t % 2, :], p_g[:, 0:FF], ACT.Silu).then_inc(sil_done, 1)
                    act.activation(up[:, t % 2, :], p_u[:, 0:FF], ACT.Copy).then_inc(sil_done, 1)
                if t >= 1:
                    for n in range(2):
                        act.wait_ge(d_done, 2 * (t - 1) + n + 1)
                        if t >= 3 and n == 0:
                            act.wait_ge(y_st[(t - 1) % 2], 16 * ((t - 1) // 2))
                        act.activation(yo[:, (t - 1) % 2, n * NCH:(n + 1) * NCH], p_d[n][:, :], ACT.Copy).then_inc(y_ready, 1)
                if t < TT:
                    act.wait_ge(h_tr, t + 1)
                    act.activation(hidT[:, t % 2, :, :], p_h[:, 0:2 * P].rearrange("p (j c) -> p j c", j=2), ACT.Copy).then_inc(h_out, 1)

        @block.vector
        def _(dve):
            link = Chain(dve, step)
            dve.wait_ge(consts, 3)
            link(dve.tensor_copy(iota_f[:, :], iota_i[:, :]))
            link(dve.tensor_copy(col[:, :], col_i[:, :]))
            for t in range(TT):
                link(dve.tensor_scalar(tok[:, t:t + 1], col[:, :], float(t * P + 1), None, ALU.add))
                link(dve.memset(thr[:, :, t], float(t * P)))
            dve.wait_ge(got_b, 16)
            dve.wait_ge(scored, 1)
            link(dve.tensor_tensor(sel[:, :, :], sc[:, :, :], rb[:, None, :].to_broadcast([P, TT, NE]), ALU.add))
            g64 = lambda t: t[:, :, :].rearrange("p t (g e) -> p (t g) e", e=EG)
            col64 = lambda i: gm[:, i, :, :].rearrange("p t g -> p (t g)")
            bc64 = lambda i: col64(i)[:, :, None].to_broadcast([P, TT * NG, EG])
            link(dve.tensor_reduce(col64(0), g64(sel), AX.X, ALU.max))
            link(dve.tensor_tensor(g64(t1), g64(sel), bc64(0), ALU.is_equal))
            link(dve.tensor_reduce(col64(1), g64(t1), AX.X, ALU.add))
            link(dve.scalar_tensor_tensor(t2[:, :, :], t1[:, :, :], NEG, sel[:, :, :], ALU.mult, ALU.add))
            link(dve.tensor_reduce(col64(2), g64(t2), AX.X, ALU.max))
            link(dve.tensor_scalar(col64(3), col64(1), 1.5, -2 * NEG, ALU.is_gt, ALU.mult))
            link(dve.tensor_scalar(col64(3), col64(3), NEG, None, ALU.add))
            link(dve.tensor_tensor(col64(2), col64(2), col64(3), ALU.max))
            link(dve.tensor_tensor(col64(2), col64(2), col64(0), ALU.min))
            link(dve.tensor_tensor(col64(4), col64(0), col64(2), ALU.add))
            other = gm[:, 4, :, None, :].to_broadcast([P, TT, NG, NG])
            own = gm[:, 4, :, :, None].to_broadcast([P, TT, NG, NG])
            sq = lambda t: t[:, :, :].rearrange("p t (g e) -> p t g e", e=NG)
            link(dve.tensor_tensor(sq(t1), other, own, ALU.is_gt))
            link(dve.tensor_tensor(sq(t2), other, own, ALU.is_equal))
            link(dve.tensor_tensor(sq(t2), sq(t2), low[:, None, :, :].to_broadcast([P, TT, NG, NG]), ALU.mult))
            link(dve.tensor_tensor(t1[:, :, :], t1[:, :, :], t2[:, :, :], ALU.add))
            link(dve.tensor_reduce(col64(5), g64(t1), AX.X, ALU.add))
            link(dve.tensor_scalar(col64(6), col64(5), TOPG - 0.5, None, ALU.is_lt))
            link(dve.tensor_scalar(col64(7), col64(6), 1.0, -NEG, ALU.subtract, ALU.mult))
            link(dve.tensor_tensor(g64(ms), g64(sel), bc64(6), ALU.mult))
            link(dve.tensor_tensor(g64(ms), g64(ms), bc64(7), ALU.add))
            for t in range(TT):
                dve.max(top[:, t, :], ms[:, t, :]).then_inc(step, 1)
            link.n += TT
            dve.wait_ge(step, link.n)
            for t in range(TT):
                dve.match_replace(mr[:, t, :], top[:, t, :], ms[:, t, :], -3e38).then_inc(step, 1)
            link.n += TT
            dve.wait_ge(step, link.n)
            link(dve.tensor_tensor(M[:, :, :], mr[:, :, :], ms[:, :, :], ALU.not_equal))
            dve.sem_inc(masked, 1)
            link(dve.tensor_tensor(t1[:, :, :], M[:, :, :], sc[:, :, :], ALU.mult))
            link(dve.tensor_reduce(den[:, :], t1[:, :, :], AX.X, ALU.add))
            link(dve.reciprocal(rden[:, :], den[:, :]))
            link(dve.scalar_tensor_tensor(gate[:, :, :], t1[:, :, :], SCALE, rden[:, :, None].to_broadcast([P, TT, NE]), ALU.mult, ALU.mult))
            dve.wait_ge(counted, 1)
            link(dve.tensor_copy(nbk[:, 0, :], p_misc[:, 0:NE]))
            th = t2[:, :, :].rearrange("p t e -> p (t e)").rearrange("p (e j) -> p e j", j=KD)
            link(dve.tensor_tensor(th, nbk[:, 0, :, None].to_broadcast([P, NE, KD]), thr[:, :, :], ALU.is_gt))
            link(dve.tensor_reduce(nbk[:, 1, :], th, AX.X, ALU.add))
            link(dve.tensor_scalar(nbk[:, 1, :], nbk[:, 1, :], 1.0, None, ALU.max))
            link(dve.tensor_tensor_scan(nbk[:, 2, :], ones[:, 0:NE], nbk[:, 1, :], 0.0, ALU.mult, ALU.add))
            link(dve.tensor_tensor(nbk[:, 3, :], nbk[:, 2, :], nbk[:, 1, :], ALU.subtract))
            link(dve.tensor_scalar(nbk[:, 3, :], nbk[:, 3, :], float(P), None, ALU.mult))
            link(dve.tensor_scalar(t1[:, 0, :], nbk[:, 2, :], col[:, 0:1], None, ALU.is_lt))
            link(dve.tensor_reduce(ebc[:, 1:2], t1[:, 0, :], AX.X, ALU.add))
            link(dve.tensor_scalar(ebc[:, 0:1], ebc[:, 1:2], float(NE - 1), None, ALU.min))
            dve.sem_inc(eb_ready, 1)
            link(dve.memset(bounds[0:1, 0:1], 0))
            link(dve.tensor_copy(bounds[0:1, 1:NE + 1], nbk[0:1, 2, :]))
            dve.wait_ge(placed, 1)
            link(dve.tensor_tensor(slot[:, :, :], p_pos[:, :, :], nbk[:, 3, None, :].to_broadcast([P, TT, NE]), ALU.add))
            link(dve.scalar_tensor_tensor(slot[:, :, :], slot[:, :, :], 1.0, M[:, :, :], ALU.add, ALU.mult))
            for t in range(TT):
                dve.max(s8[:, t, :], slot[:, t, :]).then_inc(step, 1)
            link.n += TT
            dve.wait_ge(step, link.n)
            for t in range(TT):
                sh = [P, TOPK, NE]
                link(dve.tensor_tensor(t1[:, :, :], slot[:, t, None, :].to_broadcast(sh), s8[:, t, :, None].to_broadcast(sh), ALU.is_equal))
                link(dve.tensor_tensor(t1[:, :, :], t1[:, :, :], gate[:, t, None, :].to_broadcast(sh), ALU.mult))
                link(dve.tensor_reduce(w8[:, t, :], t1[:, :, :], AX.X, ALU.add))
            link(dve.tensor_scalar(s8[:, :, :], s8[:, :, :], 1.0, None, ALU.subtract))
            link(dve.tensor_copy(s8i[:, :, :], s8[:, :, :]))
            link(dve.tensor_scalar(q8i[:, :, :], s8i[:, :, :], 7, None, ALU.logical_shift_right))
            link(dve.tensor_scalar(r8i[:, :, :], s8i[:, :, :], P - 1, None, ALU.bitwise_and))
            link(dve.tensor_copy(q8[:, :, :], q8i[:, :, :]))
            link(dve.tensor_copy(r8[:, :, :], r8i[:, :, :]))
            dve.sem_inc(slots_ready, 1)
            for j in range(TT * TOPK):
                t, k = j // TOPK, j % TOPK
                if j >= HB:
                    dve.wait_ge(hot_mm, j - HB + 1)
                dve.tensor_scalar(hot_q[:, j % HB, 0, :], iota_f[:, :], q8[:, t, k:k + 1], tok[:, t:t + 1], ALU.is_equal, ALU.mult).then_inc(hot_ready, 1)
                dve.tensor_scalar(hot_q[:, j % HB, 1, :], iota_f[:, :], q8[:, t, k:k + 1], w8[:, t, k:k + 1], ALU.is_equal, ALU.mult).then_inc(hot_ready, 1)
            dve.wait_ge(hot_mm, TT * TOPK)
            tab = p_l[:, 0:4, :].rearrange("p a e -> p (a e)")
            link(dve.tensor_copy(wslot[:, 0:P], tab[:, P:2 * P]))
            link(dve.tensor_copy(tabf[:, 0, :], tab[:, 0:P]))
            link(dve.tensor_scalar(col[:, :], col[:, :], float(SEQ + 1), None, ALU.add))
            link(dve.tensor_scalar(tabf[:, 1, :], tabf[:, 0, :], 0.5, col[:, 0:1], ALU.is_lt, ALU.mult))
            link(dve.scalar_tensor_tensor(tabf[:, 0, :], tabf[:, 0, :], 1.0, tabf[:, 1, :], ALU.subtract, ALU.add))
            link(dve.tensor_copy(idx[:, 1:P + 1], tabf[:, 0, :]))
            link(dve.tensor_scalar(tabf[:, 1, 0:1], col[:, :], 1.0, None, ALU.subtract))
            for j in (0, P + 1, P + 2):
                link(dve.tensor_copy(idx[:, j:j + 1], tabf[:, 1, 0:1]))
            dve.wait_ge(eb_mm, 1)
            link(dve.tensor_copy(eb[0:1, :], p_pos[0:1, 0:2, :].rearrange("p a e -> p (a e)")))
            link(dve.tensor_scalar(slot_of[0:1, :], eb[0:1, :], 1, None, ALU.bitwise_and))


def experts(nc, tag, w_gate, w_up, w_down, f_dram, acc_dram, ident, idx, wslot, bounds, slot_of, first_gu):
    QG, QD = 4, 2
    KP = KD // QG
    with Phase(nc, tag) as ph:
        raw = ph.sb("raw", [P, KD, 2 * FF])
        raw_d = ph.sb("raw_d", [P, 2, D])
        wh, wl = ph.sb("wh", [P, 2, KD, 2 * FF], F32R), ph.sb("wl", [P, 2, KD, 2 * FF], F32R)
        dh, dl = ph.sb("dh", [P, 2, 2, D], F32R), ph.sb("dl", [P, 2, 2, D], F32R)
        xg = ph.sb("xg", [P, D])
        xh, xl = ph.sb("xh", [P, KD, P], F32R), ph.sb("xl", [P, KD, P], F32R)
        sil, hid = ph.sb("sil", [P, FF]), ph.sb("hid", [P, FF])
        hh, hl = ph.sb("hh", [P, 2, P], F32R), ph.sb("hl", [P, 2, P], F32R)
        hz = ph.sb("hz", [P, 2, P])
        yo = ph.sb("yo", [P, D])
        ig, isc = ph.sb("ig", [P, 1], U32), ph.sb("isc", [P, 1], U32)
        p_x = [ph.ps(f"p_x{i}", [P, 4, P]) for i in range(2)]
        p_gu, p_h = ph.ps("p_gu", [P, NCH]), ph.ps("p_h", [P, 2, P])
        p_d = [ph.ps(f"p_d{i}", [P, NCH]) for i in range(2)]
        gu_in, d_in = [ph.sem(f"gu_in{i}") for i in range(2)], ph.sem("d_in")
        gu_head, gu_split, d_head, d_split = (ph.sem(s) for s in ("gu_head", "gu_split", "d_head", "d_split"))
        x_in, x_tr, x_head, x_split = (ph.sem(s) for s in ("x_in", "x_tr", "x_head", "x_split"))
        gu_mm, sil_done, hid_done, h_tr, h_head, h_split = (ph.sem(s) for s in ("gu_mm", "sil_done", "hid_done", "h_tr", "h_head", "h_split"))
        zero_h, d_mm, y_act, y_dve, added = (ph.sem(s) for s in ("zero_h", "d_mm", "y_act", "y_dve", "added"))
        y_free, tick, copied = ph.sem("y_free"), ph.sem("tick"), ph.sem("copied")
        block = ph.block()

        def bound(eng, e):
            return eng.value_load(bounds[0:1, e:e + 1] if isinstance(e, int) else bounds[0:1, bass.ds(e, 1)], min_val=0, max_val=P - 1)

        def each_expert(eng, body):
            with eng.Fori(0, NE // 2 - 1) as i:
                for u in range(2):
                    body(i * 2 + u, u, True)
            body(NE - 2, 0, True)
            body(NE - 1, 1, False)

        @block.sync
        def _(sp):
            def load_d(e):
                w = w_down[e:e + 1] if isinstance(e, int) else w_down[bass.ds(e, 1), :, :]
                sp.dma_start(raw_d[:, :, :], w.rearrange("a (j p) n -> p (a j) n", p=P)).then_inc(d_in, 16)

            def load_gu(e, half):
                for i, w in enumerate((w_gate, w_up)):
                    w = w[e:e + 1] if isinstance(e, int) else w[bass.ds(e, 1), :, :]
                    ks = slice(half * KD // 2, (half + 1) * KD // 2)
                    sp.dma_start(raw[:, ks, i * FF:(i + 1) * FF],
                                 w.rearrange("a (p k) f -> p (a k) f", k=KD)[:, ks, :]).then_inc(gu_in[half], 16)

            sp.wait_ge(x_in, 16)
            load_d(0)
            for half in range(2):
                load_gu(1, half)
            sp.wait_ge(d_split, QD)
            load_d(1)

            def refill(e):
                for half in range(2):
                    sp.wait_ge(gu_split, e * QG - QG + (half + 1) * QG // 2)
                    load_gu(e, half)
                sp.wait_ge(d_split, e * QD)
                load_d(e)

            with sp.Fori(2, NE) as e:
                refill(e)

        @block.gpsimd
        def _(pool):
            blocks = bound(pool, NE)

            def gather(n, count):
                if not isinstance(n, int) or n > 0:
                    pool.wait_ge(x_tr, n)
                    pool.sem_inc(tick, 1)
                c = idx[:, n + 1:n + 2] if isinstance(n, int) else idx[:, bass.ds(n + 1, 1)]
                pool.tensor_copy(ig[:, :], c).then_inc(copied, 1)
                pool.wait_ge(copied, count)
                pool.sem_inc(tick, 1)
                pool.indirect_dma_start(xg[:, :], None, f_dram, bass.IndirectOffsetOnAxis(ap=ig[:, :], axis=0)).then_inc(x_in, 16)

            def scatter(n, count):
                if not isinstance(n, int):
                    pool.wait_ge(added, n * 16)
                pool.sem_inc(y_free, 1)
                pool.tensor_copy(isc[:, :], idx[:, n:n + 1] if isinstance(n, int) else idx[:, bass.ds(n, 1)]).then_inc(copied, 1)
                pool.wait_ge(copied, count)
                pool.sem_inc(tick, 1)
                pool.wait_ge(y_act, n + 2)
                pool.sem_inc(tick, 1)
                pool.wait_ge(y_dve, n + 2)
                pool.sem_inc(tick, 1)
                pool.indirect_dma_start(acc_dram, bass.IndirectOffsetOnAxis(ap=isc[:, :], axis=0), yo[:, :], None,
                                        compute_op=ALU.add).then_inc(added, 16)

            pool.memset(hz[:, :, :], 0.0).then_inc(zero_h, 1)
            gather(0, 1)
            gather(1, 2)
            gather(2, 3)
            scatter(0, 4)
            with pool.Fori(1, blocks) as n:
                gather(n + 2, n * 2 + 3)
                scatter(n, n * 2 + 4)
            scatter(pool.snap(blocks * 1), blocks * 2 + 3)
            pool.wait_ge(added, blocks * 16 + 16)
            pool.wait_ge(x_in, blocks * 16 + 32)
            pool.sem_inc(tick, 1)

        @block.tensor
        def _(pe):
            def turn_x(n):
                pe.wait_ge(x_in, n * 16 + 16)
                for k in range(KD):
                    tr = pe.transpose(p_x[k // 4][:, k % 4, :], xg[:, k * P:(k + 1) * P], ident[:, :])
                tr.then_inc(x_tr, 1)

            def gate_up(n, u):
                pe.wait_ge(x_head, n * 2 + 2)
                pe.wait_ge(hid_done, n + 1)
                for k in range(KD):
                    pe.matmul(p_gu[:, :], xh[:, k, :], wh[:, u, k, :], start=k == 0, stop=False)
                    pe.matmul(p_gu[:, :], xh[:, k, :], wl[:, u, k, :], start=False, stop=False)
                pe.wait_ge(x_split, n * 2 + 2)
                for k in range(KD):
                    mm = pe.matmul(p_gu[:, :], xl[:, k, :], wh[:, u, k, :], start=False, stop=k == KD - 1)
                mm.then_inc(gu_mm, 1)

            def turn_h(n):
                pe.wait_ge(hid_done, n + 2)
                for j in range(2):
                    tr = pe.transpose(p_h[:, j, :], hid[:, j * P:(j + 1) * P], ident[:, :])
                tr.then_inc(h_tr, 1)

            def down(n, u):
                pe.wait_ge(h_split, n + 1)
                pe.wait_ge(y_act, n + 1)
                pe.wait_ge(y_dve, n + 1)
                pick = lambda t, j, c: t[:, u, j, c * NCH:(c + 1) * NCH] if isinstance(u, int) else t[:, bass.ds(u, 1), j, c * NCH:(c + 1) * NCH]
                for c in range(2):
                    for j in range(2):
                        pe.matmul(p_d[c][:, :], hh[:, j, :], pick(dh, j, c), start=j == 0, stop=False)
                        pe.matmul(p_d[c][:, :], hh[:, j, :], pick(dl, j, c), start=False, stop=False)
                        mm = pe.matmul(p_d[c][:, :], hl[:, j, :], pick(dh, j, c), start=False, stop=j == 1)
                    mm.then_inc(d_mm, 1)

            def expert(e, u, more):
                first, end = bound(pe, e), bound(pe, e + 1)
                with pe.Fori(first, end) as n:
                    before = pe.value_load(slot_of[0:1, bass.ds(n, 1)], min_val=0, max_val=1)
                    pe.wait_ge(gu_split, e * QG + QG)
                    gate_up(n, u)
                    turn_x(n + 1)
                    pe.wait_ge(d_split, e * QD + QD)
                    down(n, before)
                    turn_h(n)

            turn_x(0)
            each_expert(pe, expert)
            down(bound(pe, NE), (NE - 1) % 2)

        @block.scalar
        def _(act):
            def head_gu(e, u, src):
                for q in range(QG):
                    if q % (QG // 2) == 0 and src is raw:
                        act.wait_ge(gu_in[q // (QG // 2)], e * 32)
                    act.activation(wh[:, u, q * KP:(q + 1) * KP, :], src[:, q * KP:(q + 1) * KP, :], ACT.Copy).then_inc(gu_head, 1)

            def head_d(e, u):
                act.wait_ge(d_in, e * 16 + 16)
                for q in range(QD):
                    act.activation(dh[:, u, q, :], raw_d[:, q, :], ACT.Copy).then_inc(d_head, 1)

            def head_x(n):
                act.wait_ge(x_tr, n + 1)
                for i in range(2):
                    act.activation(xh[:, 4 * i:4 * i + 4, :], p_x[i][:, :, :], ACT.Copy).then_inc(x_head, 1)

            def out(n):
                act.wait_ge(d_mm, n * 2 + 1)
                act.wait_ge(y_free, n + 1)
                act.activation(yo[:, 0:NCH], p_d[0][:, :], ACT.Copy).then_inc(y_act, 1)

            def expert(e, u, more):
                head_d(e, u)
                if more:
                    head_gu(e + 1, 1 - u, raw)
                first, end = bound(act, e), bound(act, e + 1)
                with act.Fori(first, end) as n:
                    act.wait_ge(gu_mm, n + 1)
                    act.activation(sil[:, :], p_gu[:, 0:FF], ACT.Silu).then_inc(sil_done, 1)
                    head_x(n + 1)
                    out(n)
                    act.wait_ge(h_tr, n + 1)
                    act.activation(hh[:, :, :], p_h[:, :, :], ACT.Copy).then_inc(h_head, 1)

            act.sem_inc(y_act, 1)
            act.wait_ge(zero_h, 1)
            act.activation(hh[:, :, :], hz[:, :, :], ACT.Copy).then_inc(h_head, 1)
            head_gu(0, 0, first_gu)
            head_x(0)
            each_expert(act, expert)
            out(bound(act, NE))

        @block.vector
        def _(dve):
            def rest_gu(e, u, src):
                for q in range(QG):
                    s = slice(q * KP, (q + 1) * KP)
                    dve.wait_ge(gu_head, e * QG + q + 1)
                    dve.tensor_tensor(wl[:, u, s, :], src[:, s, :], wh[:, u, s, :], ALU.subtract).then_inc(gu_split, 1)

            def rest_d(e, u):
                for q in range(QD):
                    dve.wait_ge(d_head, e * QD + q + 1)
                    dve.tensor_tensor(dl[:, u, q, :], raw_d[:, q, :], dh[:, u, q, :], ALU.subtract).then_inc(d_split, 1)

            def rest_x(n):
                for i in range(2):
                    dve.wait_ge(x_head, n * 2 + i + 1)
                    dve.tensor_tensor(xl[:, 4 * i:4 * i + 4, :], p_x[i][:, :, :], xh[:, 4 * i:4 * i + 4, :], ALU.subtract).then_inc(x_split, 1)

            def out(n):
                dve.wait_ge(d_mm, n * 2 + 2)
                dve.wait_ge(y_free, n + 1)
                dve.tensor_copy(yo[:, NCH:D], p_d[1][:, :]).then_inc(y_dve, 1)

            def expert(e, u, more):
                rest_d(e, u)
                if more:
                    rest_gu(e + 1, 1 - u, raw)
                first, end = bound(dve, e), bound(dve, e + 1)
                with dve.Fori(first, end) as n:
                    dve.wait_ge(sil_done, n + 1)
                    dve.scalar_tensor_tensor(hid[:, :], sil[:, :], wslot[:, bass.ds(n, 1)], p_gu[:, FF:2 * FF], ALU.mult, ALU.mult).then_inc(hid_done, 1)
                    rest_x(n + 1)
                    out(n)
                    dve.wait_ge(h_head, n + 2)
                    dve.tensor_tensor(hl[:, :, :], p_h[:, :, :], hh[:, :, :], ALU.subtract).then_inc(h_split, 1)

            dve.sem_inc(y_dve, 1)
            dve.sem_inc(hid_done, 1)
            dve.wait_ge(h_head, 1)
            dve.tensor_tensor(hl[:, :, :], hz[:, :, :], hh[:, :, :], ALU.subtract).then_inc(h_split, 1)
            rest_gu(0, 0, first_gu)
            rest_x(0)
            each_expert(dve, expert)
            out(bound(dve, NE))

FG = 4
FW = D // FG


def add_gated(nc, tag, acc_dram, gate, h, out):
    with Phase(nc, tag) as ph:
        a = ph.sb("a", [P, TT, D])
        a_in = [ph.sem(f"a_in{t}") for t in range(TT)]
        gated, added, stored = ph.sem("gated"), ph.sem("added"), ph.sem("stored")
        block = ph.block()

        @block.sync
        def _(sp):
            for t in range(TT):
                sp.dma_start(a[:, t, :], acc_dram[t * P:(t + 1) * P, :]).then_inc(a_in[t], 16)
            for t in range(TT):
                sp.wait_ge(added, t + 1)
                sp.dma_start(out[t * P:(t + 1) * P, :], h[:, t, :]).then_inc(stored, 16)
            sp.wait_ge(stored, 16 * TT)

        @block.vector
        def _(dve):
            for t in range(TT):
                dve.wait_ge(a_in[t], 16)
                dve.tensor_tensor(a[:, t, :], a[:, t, :], gate, ALU.mult).then_inc(gated, 1)
                dve.wait_ge(gated, t + 1)
                dve.tensor_tensor(h[:, t, :], h[:, t, :], a[:, t, :], ALU.add).then_inc(added, 1)
            dve.wait_ge(added, TT)


def add_gated_and_condition(nc, tag, acc_dram, mod, h, sums_dram, b):
    NB = ADA // NCH
    LAST = 5 * D // NCH
    with Phase(nc, tag) as ph:
        a = ph.sb("a", [P, TT, D])
        sums = ph.sb("sums", [P, ADA])
        row = ph.sb("row", [1, ADA])
        ones = ph.sb("ones", [P, P])
        bank = [ph.ps(f"p{i}", [P, NCH]) for i in range(4)]
        a_in = [ph.sem(f"a_in{t}") for t in range(TT)]
        sums_in = [ph.sem(f"sums_in{i}") for i in range(2)]
        row_in, ones_done, biased = ph.sem("row_in"), ph.sem("ones_done"), ph.sem("biased")
        gated, added, product, copied, scaled = (ph.sem(s) for s in ("gated", "added", "product", "copied", "scaled"))
        chunk = lambda i: slice(i * NCH, (i + 1) * NCH)
        half = lambda i: slice(i * ADA // 2, (i + 1) * ADA // 2)
        block = ph.block()

        @block.sync
        def _(sp):
            sp.dma_start(row[:, :], b[None, :]).then_inc(row_in, 16)
            for i in range(2):
                sp.dma_start(sums[:, half(i)], sums_dram[:, half(i)]).then_inc(sums_in[i], 16)
                for t in range(i * TT // 2, (i + 1) * TT // 2):
                    sp.dma_start(a[:, t, :], acc_dram[t * P:(t + 1) * P, :]).then_inc(a_in[t], 16)

        @block.tensor
        def _(pe):
            pe.wait_ge(ones_done, 1)
            for i in range(NB):
                pe.wait_ge(biased, i // (NB // 2) + 1)
                if i >= 4:
                    pe.wait_ge(copied, i - 3)
                pe.matmul(bank[i % 4][:, :], ones[:, :], sums[:, chunk(i)], start=True, stop=True).then_inc(product, 1)

        @block.scalar
        def _(act):
            for i in range(NB):
                act.wait_ge(product, i + 1)
                if i == LAST:
                    act.wait_ge(added, TT)
                act.activation(mod[:, chunk(i)], bank[i % 4][:, :], ACT.Copy).then_inc(copied, 1)
            act.wait_ge(copied, NB)

        @block.vector
        def _(dve):
            dve.memset(ones[:, :], 1.0).then_inc(ones_done, 1)
            dve.wait_ge(row_in, 16)
            for i in range(2):
                dve.wait_ge(sums_in[i], 16)
                dve.tensor_tensor(sums[0:1, half(i)], sums[0:1, half(i)], row[:, half(i)], ALU.add).then_inc(biased, 1)
                for t in range(i * TT // 2, (i + 1) * TT // 2):
                    dve.wait_ge(a_in[t], 16)
                    dve.tensor_tensor(a[:, t, :], a[:, t, :], mod[:, 5 * D:6 * D], ALU.mult).then_inc(gated, 1)
                    dve.wait_ge(gated, t + 1)
                    dve.tensor_tensor(h[:, t, :], h[:, t, :], a[:, t, :], ALU.add).then_inc(added, 1)
            for s in (1, 4):
                dve.wait_ge(copied, (s + 1) * D // NCH)
                dve.tensor_scalar(mod[:, s * D:(s + 1) * D], mod[:, s * D:(s + 1) * D], 1.0, None, ALU.add).then_inc(scaled, 1)
            dve.wait_ge(scaled, 2)


def fourier(nc, tag, aT, cs_feat, cos_tok, sin_tok, alt, fT):
    HT = SEQ // 2
    HK = HT // P
    with Phase(nc, tag) as ph:
        cf = ph.sb("cf", [P, 2, 2 * FW])
        odd = ph.sb("odd", [P, KD, HT])
        y = ph.sb("y", [P, HK, 2, D])
        mid = ph.sb("mid", [1, D])
        ct = ph.sb("ct", [P, HK, HT])
        st = ph.sb("st", [P, HK, HT])
        alt_row, alt_col = ph.sb("alt_row", [1, HT]), ph.sb("alt_col", [P, HK])
        one = ph.sb("one", [1, 1])
        py = [ph.ps(f"py{i}", [P, NCH]) for i in range(4)]
        pe_, po = ([ph.ps(f"{s}{i}", [P, NCH]) for i in range(2)] for s in ("even", "odd"))
        c_in, t_in = ph.sem("c_in"), ph.sem("t_in")
        odd_ready, even_ready, one_set = ph.sem("odd_ready"), ph.sem("even_ready"), ph.sem("one_set")
        y_mm, mid_mm, mid_out = ph.sem("y_mm"), ph.sem("mid_mm"), ph.sem("mid_out")
        copied = [ph.sem(f"copied{i}") for i in range(2)]
        z_mm, c_mm, even_out, sums, c_out = (ph.sem(s) for s in ("z_mm", "c_mm", "even_out", "sums", "c_out"))
        ev = ph.sb("ev", [P, 2, HT])
        jobs = [(t, g) for t in range(HK) for g in range(FG)]
        NJ = len(jobs)
        block = ph.block()

        @block.sync
        def _(sp):
            sp.dma_start(cf[:, :, :], cs_feat).then_inc(c_in, 16)
            for buf, src in ((ct, cos_tok), (st, sin_tok)):
                sp.dma_start(buf[:, :, :], src.rearrange("(k p) n -> p k n", p=P)).then_inc(t_in, 16)
            sp.dma_start(alt_row[:, :], alt[None, :]).then_inc(t_in, 16)
            sp.dma_start(alt_col[:, :], alt.rearrange("(k p) -> p k", p=P), allow_slow_non_contiguous=True).then_inc(t_in, 16)

        @block.gpsimd
        def _(pool):
            pool.memset(one[:, :], 1.0).then_inc(one_set, 1)

        @block.tensor
        def _(pe):
            pe.wait_ge(c_in, 16)
            for g in range(FG):
                for k in range(2):
                    mm = pe.matmul(py[g // 2][0:1, (g % 2) * FW:(g % 2 + 1) * FW], aT[:, 2 * g + k, HT:HT + 1], cf[:, k, 0:FW], start=k == 0, stop=k == 1)
            mm.then_inc(mid_mm, 1)
            for j, (t, g) in enumerate(jobs):
                pe.wait_ge(odd_ready, g + 1)
                pe.wait_ge(even_ready, g + 1)
                if j < 2:
                    pe.wait_ge(mid_out, 2)
                if j >= 4:
                    pe.wait_ge(copied[j % 2], (j - 4) // 2 + 1)
                for i, src in enumerate((aT, odd)):
                    for k in range(2):
                        mm = pe.matmul(py[j % 4][:, i * FW:(i + 1) * FW], src[:, 2 * g + k, t * P:(t + 1) * P], cf[:, k, i * FW:(i + 1) * FW],
                                       start=k == 0, stop=k == 1)
                mm.then_inc(y_mm, 1)
            for i in range(2):
                pe.wait_ge(copied[i], NJ // 2)
            pe.wait_ge(t_in, 64)
            pe.wait_ge(one_set, 1)
            for f in range(KD):
                fs = slice(f * P, (f + 1) * P)
                if f >= 2:
                    pe.wait_ge(even_out, f - 1)
                for k in range(HK):
                    pe.matmul(pe_[f % 2][:, :], y[:, k, 0, fs], ct[:, k, :], start=k == 0, stop=False)
                pe.matmul(pe_[f % 2][:, :], mid[:, fs], alt_row[:, :], start=False, stop=True).then_inc(z_mm, 1)
                if f >= 2:
                    pe.wait_ge(sums, 2 * (f - 1))
                for k in range(HK):
                    mm = pe.matmul(po[f % 2][:, :], y[:, k, 1, fs], st[:, k, :], start=k == 0, stop=k == HK - 1)
                mm.then_inc(z_mm, 1)
            for f in range(KD):
                fs = slice(f * P, (f + 1) * P)
                for k in range(HK):
                    pe.matmul(py[0][:, f:f + 1], y[:, k, 0, fs], alt_col[:, k:k + 1], start=k == 0, stop=False)
                mm = pe.matmul(py[0][:, f:f + 1], mid[:, fs], one[:, :], start=False, stop=True)
            mm.then_inc(c_mm, 1)

        @block.scalar
        def _(act):
            act.wait_ge(mid_mm, 1)
            for i in range(2):
                act.activation(mid[:, i * NCH:(i + 1) * NCH], py[i][0:1, :], ACT.Copy).then_inc(mid_out, 1)
            for j in range(0, NJ, 2):
                t, g = jobs[j]
                act.wait_ge(y_mm, j + 1)
                act.activation(y[:, t, :, g * FW:(g + 1) * FW], py[j % 4][:, :].rearrange("p (s f) -> p s f", s=2), ACT.Copy).then_inc(copied[0], 1)
            for f in range(KD):
                act.wait_ge(z_mm, 2 * f + 1)
                if f >= 2:
                    act.wait_ge(sums, 2 * (f - 1))
                act.activation(ev[:, f % 2, :], pe_[f % 2][:, :], ACT.Copy).then_inc(even_out, 1)
            act.wait_ge(c_mm, 1)
            act.activation(fT[:, :, HT:HT + 1].rearrange("p k o -> p (k o)"), py[0][:, 0:KD], ACT.Copy).then_inc(c_out, 1)
            act.wait_ge(c_out, 1)

        @block.vector
        def _(dve):
            for g in range(FG):
                ks = slice(2 * g, 2 * g + 2)
                near, far = aT[:, ks, 1:HT], aT[:, ks, SEQ - 1:HT:-1]
                dve.tensor_copy(odd[:, ks, 0:1], aT[:, ks, 0:1])
                dve.tensor_tensor(odd[:, ks, 1:HT], near, far, ALU.subtract).then_inc(odd_ready, 1)
                dve.wait_ge(odd_ready, g + 1)
                dve.tensor_tensor(near, near, far, ALU.add).then_inc(even_ready, 1)
            for j in range(1, NJ, 2):
                t, g = jobs[j]
                dve.wait_ge(y_mm, j + 1)
                dve.tensor_copy(y[:, t, :, g * FW:(g + 1) * FW], py[j % 4][:, :].rearrange("p (s f) -> p s f", s=2)).then_inc(copied[1], 1)
            for f in range(KD):
                dve.wait_ge(even_out, f + 1)
                dve.wait_ge(z_mm, 2 * f + 2)
                dve.tensor_tensor(fT[:, f, 0:HT], ev[:, f % 2, :], po[f % 2][:, :], ALU.add).then_inc(sums, 1)
                dve.tensor_tensor(fT[:, f, HT + 1:SEQ], ev[:, f % 2, HT - 1:0:-1], po[f % 2][:, HT - 1:0:-1], ALU.subtract).then_inc(sums, 1)
            dve.wait_ge(sums, 2 * KD)
def program(nc, x, c, ctx, c_ctx, w_ada, b_ada, w_in, s5_lam_re, s5_lam_im, s5_log_dt, s5_b_re, s5_b_im,
            s5_c_re, s5_c_im, s5_d, s5_w_glu, s5_b_glu, na_q_gain, na_k_gain, na_rpb, w_mix_out,
            w_fourier_out, b_fourier_out, w_router, router_bias, w_exp_gate, w_exp_up, w_exp_down,
            w_sh_gate, w_sh_up, w_sh_down, cs_feat, cos_tok, sin_tok, alt, out):
    def scratch(name, shape):
        return nc.dram_tensor(f"scratch_{name}", shape, F32, kind="Internal").ap()

    mats, rot, k_lags = scratch("mats", (P, 5, G5, P)), scratch("rot", (P, 2, G5, NCK)), scratch("lags", (W5, TAUS * C5))
    mix_dram, ada_sums = scratch("mix", (D, SEQ)), scratch("ada_sums", (P, ADA))
    u_dram, y_dram = scratch("u", (W5, TOK)), scratch("y", (W5, SEQ))
    pad = scratch("pad", (HEADS * RPB_R, 2 * GRID_W - 1))
    f_dram, acc_dram = scratch("f", (SEQ + PAD_ROWS, D)), scratch("acc", (SEQ + PAD_ROWS, D))
    xr = x[0]
    rows = lambda t, n: [t[i * P:(i + 1) * P, :] for i in range(n)]

    def moe(layer, mod, h, ident, last, mix):
        tag = f"moe{layer}"
        first_gu = mod[:, 0:4 * D].rearrange("p (k f) -> p k f", k=KD)
        with Phase(nc, tag) as ph:
            idx, wslot = ph.sb("idx", [P, NIDX], U32), ph.sb("wslot", [P, NIDX])
            bounds, slot_of = ph.sb("bounds", [1, NE + 1], I32), ph.sb("slot_of", [1, P], I32)
            with Phase(nc, tag + "in") as ph2:
                fT = ph2.sb("fT", [P, KD, SEQ])
                tiles = [(h[:, t, :], (mod[:, 3 * D:4 * D], mod[:, 4 * D:5 * D]), False) for t in range(TT)]
                mix((tiles, fT, True, rows(f_dram, TT)))
                route_and_share(nc, tag + "route", ident, fT, w_router[layer], router_bias[layer], w_sh_gate[layer],
                                w_sh_up[layer], w_sh_down[layer], f_dram, acc_dram, idx, wslot, bounds, slot_of,
                                w_exp_gate[layer], w_exp_up[layer], first_gu)
            experts(nc, tag + "exp", w_exp_gate[layer], w_exp_up[layer], w_exp_down[layer], f_dram, acc_dram,
                    ident, idx, wslot, bounds, slot_of, first_gu)
        if last:
            add_gated(nc, tag + "add", acc_dram, mod[:, 5 * D:6 * D], h, out[0])
        else:
            add_gated_and_condition(nc, tag + "add", acc_dram, mod, h, ada_sums, b_ada[1])

    with Phase(nc, "main") as main:
        ident = main.sb("ident", [P, P])
        decay = main.sb("decay", [P, G5])
        make_identity(nc, ident)
        s5_matrices(nc, ident, s5_lam_re[0], s5_lam_im[0], s5_log_dt[0], s5_b_re[0], s5_b_im[0], s5_c_re[0],
                    s5_c_im[0], s5_d[0], mats, k_lags, rot, decay)
        mod = main.sb("mod", [P, ADA])
        with Phase(nc, "attn") as at:
            bt = at.sb("bt", [P, HP, RPB_R, GRID_W])
            qT, kT = at.sb("qT", [P, HP, SEQ]), at.sb("kT", [P, HP, TOK])
            v_even, v_odd, v_ctx = at.sb("v_even", [P, TT, NCH]), at.sb("v_odd", [P, TT - 1, NCH]), at.sb("v_ctx", [P, CT, NCH])
            with Phase(nc, "pre") as pre:
                aT = pre.sb("aT", [P, KD, TOK])
                with Phase(nc, "cond") as cond:
                    mod_ctx = cond.sb("mod_ctx", [P, 2 * D])
                    conditioning(nc, "ada0", c.rearrange("a (p k) -> p (a k)", k=KD), w_ada[0], b_ada[0], mod,
                                 c_ctx.rearrange("(p k) -> p k", k=KD), mod_ctx)
                    tiles = [(r, (mod_ctx[:, 0:D], mod_ctx[:, D:2 * D]), True) for r in rows(ctx[0], CT)]
                    tiles += [(r, (mod[:, 0:D], mod[:, D:2 * D]), True) for r in rows(xr, TT)]
                    norm_modulate_transpose(nc, "norm", ident, tiles, aT, True)
                project(nc, ident, aT, w_in[0], na_q_gain[0], na_k_gain[0], u_dram, qT, kT, v_even, v_odd, v_ctx,
                        lambda ph: BiasTable(ph, na_rpb[0], pad, bt))
            attention(nc, ident, qT, kT, v_even, v_odd, v_ctx, bt, mix_dram[W5:, :],
                      lambda ph: RowSums(ph, c.rearrange("a (p k) -> p (a k)", k=KD), w_ada[1], ada_sums))
        s5_scan_readout(nc, ident, u_dram, mats, rot, decay, y_dram, s5_w_glu[0], s5_b_glu[0], mix_dram[0:W5, :])
        h = main.sb("h", [P, TT, D])

        def mixed(norm_args):
            with Phase(nc, "mixed") as mx:
                residual_and_norm(nc, "mix", ident, mx.sb("mixT", [P, KD, SEQ]), w_mix_out[0], None, mod[:, 2 * D:3 * D], h,
                                  norm_args, x=xr, src_dram=mix_dram)

        moe(0, mod, h, ident, False, mixed)


        def transformed(norm_args):
            with Phase(nc, "four") as fo:
                aT = fo.sb("aT", [P, KD, SEQ])
                norm_modulate_transpose(nc, "norm_f", ident, [(h[:, t, :], (mod[:, 0:D], mod[:, D:2 * D]), False) for t in range(TT)], aT, False)
                fourier(nc, "fft", aT, cs_feat, cos_tok, sin_tok, alt, aT)
                residual_and_norm(nc, "fout", ident, aT, w_fourier_out[0], b_fourier_out[0], mod[:, 2 * D:3 * D], h, norm_args)

        moe(1, mod, h, ident, True, transformed)


INPUTS = ["x", "c", "ctx", "c_ctx", "w_ada", "b_ada", "w_in", "s5_lam_re", "s5_lam_im", "s5_log_dt", "s5_b_re", "s5_b_im",
          "s5_c_re", "s5_c_im", "s5_d", "s5_w_glu", "s5_b_glu", "na_q_gain", "na_k_gain", "na_rpb", "w_mix_out",
          "w_fourier_out", "b_fourier_out", "w_router", "router_bias", "w_exp_gate", "w_exp_up", "w_exp_down",
          "w_sh_gate", "w_sh_up", "w_sh_down"]


def transform_constants():
    import numpy as np

    i = np.arange(FW)
    a = 2 * np.pi * ((i[:, None] * i[None, :]) % FW) / FW
    feat = np.concatenate([np.cos(a), np.sin(a)], axis=1) / np.sqrt(SEQ * FW)
    t = np.arange(SEQ // 2)
    b = 2 * np.pi * ((t[:, None] * t[None, :]) % SEQ) / SEQ
    return {
        "cs_feat": np.ascontiguousarray(feat.reshape(2, P, 2 * FW).transpose(1, 0, 2), dtype=np.float32),
        "cos_tok": np.cos(b).astype(np.float32),
        "sin_tok": (-np.sin(b)).astype(np.float32),
        "alt": np.where(t % 2 == 0, 1, -1).astype(np.float32),
    }


def kernel(**inputs):
    import numpy as np
    import concourse.bacc as bacc
    from concourse.bass_utils import run_bass_kernel_spmd

    nc = bacc.Bacc("TRN2", target_bir_lowering=False, num_devices=1)
    arrays, args = {}, []
    for name, a in [(n, inputs[n]) for n in INPUTS] + list(transform_constants().items()):
        a = np.ascontiguousarray(a)
        arrays[f"in_{name}"] = a
        args.append(nc.dram_tensor(f"in_{name}", a.shape, mybir.dt.from_np(a.dtype), kind="ExternalInput").ap())
    out = nc.dram_tensor("out_h", (1, SEQ, D), F32, kind="ExternalOutput").ap()
    program(nc, *args, out)
    r = run_bass_kernel_spmd(nc, [arrays], core_ids=[0])
    return r.results[0]["out_h"]
```
